# Optimizing a Trainium2 kernel written in Bass

```python
import math
import jax, jax.numpy as jnp
from jax import lax
import numpy as np

D_MODEL = 1024
BATCH = 1
SEQ = 256
DEPTH = 1
DEC_BATCH = 8
DEC_SEQ = 4
PAST_LEN = 1024
PAGE_SIZE = 128

ATT_HEAD_DIM = 64
ATT_WIDTH = D_MODEL // 2
ATT_HEADS = ATT_WIDTH // ATT_HEAD_DIM
DILATIONS = ((128, 1), (512, 4), (2048, 16))
MAX_WINDOW = 2048
ATT_BLOCK = 128
ROPE_DIM = ATT_HEAD_DIM // 4
ROPE_THETA = 500000.0
SSM_HEAD_DIM = 64
SSM_WIDTH = D_MODEL - ATT_WIDTH
SSM_HEADS = SSM_WIDTH // SSM_HEAD_DIM
SSM_GROUPS = 2
SSM_STATE = 128
CONV_WIDTH = 4
CONV_CH = SSM_WIDTH + 2 * SSM_GROUPS * SSM_STATE
SSM_CHUNK = 128
MIX_WIDTH = ATT_WIDTH + SSM_WIDTH
IN_WIDTH = 3 * ATT_WIDTH + SSM_WIDTH + SSM_HEADS + CONV_CH
N_MEM = 256
MEM_HEADS = 4
MEM_HEAD_DIM = 128
MEM_WIDTH = MEM_HEADS * MEM_HEAD_DIM
N_EXPERTS = 32
TOP_K = 4
D_FF = D_MODEL
SWIGLU_LIMIT = 7.0
SWIGLU_ALPHA = 1.702
MOE_BLOCK = 128
NORM_EPS = 1e-6

kernel_name = 'hymba_dilated_ssd_moe_decode_step'

def rmsnorm(x, gain):
    xf = x.astype(jnp.float32)
    return xf * lax.rsqrt(jnp.mean(xf * xf, axis=-1, keepdims=True) + NORM_EPS) * gain.astype(jnp.float32)

def partial_rope(x, pos):
    half = ROPE_DIM // 2
    inv_freq = jnp.power(ROPE_THETA, -jnp.arange(half, dtype=jnp.float32) / half)
    ang = pos.astype(jnp.float32)[:, None] * inv_freq[None, :]
    cos = jnp.cos(ang)[None, :, None, :]
    sin = jnp.sin(ang)[None, :, None, :]
    x1 = x[..., :half]
    x2 = x[..., half:ROPE_DIM]
    return jnp.concatenate([x1 * cos - x2 * sin, x2 * cos + x1 * sin, x[..., ROPE_DIM:]], axis=-1)

def mixer_projections(h, pos, w_in, q_gain, k_gain):
    b, l, _ = h.shape
    proj = h @ w_in
    cuts = [ATT_WIDTH, 2 * ATT_WIDTH, 3 * ATT_WIDTH, 3 * ATT_WIDTH + SSM_WIDTH,
            3 * ATT_WIDTH + SSM_WIDTH + SSM_HEADS]
    q, k, v, z, dt_raw, xbc = jnp.split(proj, cuts, axis=-1)
    q = partial_rope(rmsnorm(q.reshape(b, l, ATT_HEADS, ATT_HEAD_DIM), q_gain), pos)
    k = partial_rope(rmsnorm(k.reshape(b, l, ATT_HEADS, ATT_HEAD_DIM), k_gain), pos)
    v = v.reshape(b, l, ATT_HEADS, ATT_HEAD_DIM)
    return q, k, v, z, dt_raw, xbc

def combine_by_denominator(parts):
    m_all = parts[0][1]
    for _, m, _ in parts[1:]:
        m_all = jnp.maximum(m_all, m)
    scales = [jnp.exp(m - m_all) for _, m, _ in parts]
    num = sum(a[..., None] * o for a, (o, _, _) in zip(scales, parts))
    den = sum(a * l for a, (_, _, l) in zip(scales, parts))
    return num / den[..., None]

def dilated_band_prompt(q, k, v, window, dilation):
    b, s, h, dh = q.shape
    n = s // dilation
    n_back = window // dilation
    npad = -(-n // ATT_BLOCK) * ATT_BLOCK
    nb = npad // ATT_BLOCK

    def to_blocks(a):
        a = a.reshape(b, n, dilation, h, dh).transpose(0, 2, 1, 3, 4)
        a = jnp.pad(a, ((0, 0), (0, 0), (0, npad - n), (0, 0), (0, 0)))
        return a.reshape(b, dilation, nb, ATT_BLOCK, h, dh)

    def with_prev(a):
        prev = jnp.pad(a[:, :, :-1], ((0, 0), (0, 0), (1, 0), (0, 0), (0, 0), (0, 0)))
        return jnp.concatenate([prev, a], axis=3)

    qb = to_blocks(q)
    kk = with_prev(to_blocks(k))
    vv = with_prev(to_blocks(v))
    sc = jnp.einsum('brnqhd,brnkhd->brnhqk', qb, kk) * (dh ** -0.5)
    qi = jnp.arange(ATT_BLOCK)[:, None] + ATT_BLOCK
    ki = jnp.arange(2 * ATT_BLOCK)[None, :]
    dist = qi - ki
    band = (dist >= 0) & (dist <= n_back)
    first = (jnp.arange(nb)[:, None, None] > 0) | (ki[None] >= ATT_BLOCK)
    mask = band[None] & first
    sc = jnp.where(mask[None, None, :, None], sc, -jnp.inf)
    m = jnp.max(sc, axis=-1)
    p = jnp.exp(sc - m[..., None])
    den = jnp.sum(p, axis=-1)
    num = jnp.einsum('brnhqk,brnkhd->brnqhd', p, vv)

    def back(a):
        a = a.reshape((b, dilation, npad) + a.shape[4:])[:, :, :n]
        a = jnp.swapaxes(a, 1, 2)
        return a.reshape((b, s) + a.shape[3:])

    return back(num), back(jnp.swapaxes(m, 3, 4)), back(jnp.swapaxes(den, 3, 4))

def dilated_attention_prompt(q, k, v):
    return combine_by_denominator([dilated_band_prompt(q, k, v, w, d) for w, d in DILATIONS])

def dilated_gather_sample(q, k_all, v_all, n_buf, window, dilation):
    t = q.shape[1]
    n_back = window // dilation
    qrow = n_buf + jnp.arange(t)
    idx = qrow[:, None] - dilation * jnp.arange(n_back + 1)[None, :]
    valid = idx >= 0
    idx = jnp.maximum(idx, 0)
    kg = jnp.take(k_all, idx, axis=1)
    vg = jnp.take(v_all, idx, axis=1)
    sc = jnp.einsum('bthd,btjhd->bthj', q, kg) * (q.shape[-1] ** -0.5)
    sc = jnp.where(valid[None, :, None, :], sc, -jnp.inf)
    m = jnp.max(sc, axis=-1)
    p = jnp.exp(sc - m[..., None])
    return jnp.einsum('bthj,btjhd->bthd', p, vg), m, jnp.sum(p, axis=-1)

def dilated_attention_sample(q, k, v, k_past, v_past):
    n_buf = k_past.shape[1]
    k_all = jnp.concatenate([k_past.astype(jnp.float32), k], axis=1)
    v_all = jnp.concatenate([v_past.astype(jnp.float32), v], axis=1)
    return combine_by_denominator([dilated_gather_sample(q, k_all, v_all, n_buf, w, d) for w, d in DILATIONS])

def ssd_scan(x, dt, a, b_in, c_in, h0):
    bsz, l, nh, hp = x.shape
    rep = nh // SSM_GROUPS
    chunk = SSM_CHUNK if l % SSM_CHUNK == 0 else l
    nc = l // chunk
    bh = jnp.repeat(b_in, rep, axis=2).reshape(bsz, nc, chunk, nh, SSM_STATE)
    ch = jnp.repeat(c_in, rep, axis=2).reshape(bsz, nc, chunk, nh, SSM_STATE)
    xd = (x * dt[..., None]).reshape(bsz, nc, chunk, nh, hp)
    acum = jnp.cumsum((dt * a).reshape(bsz, nc, chunk, nh), axis=2)
    seg = acum[:, :, :, None, :] - acum[:, :, None, :, :]
    causal = jnp.tril(jnp.ones((chunk, chunk), dtype=bool))[None, None, :, :, None]
    decay = jnp.exp(jnp.where(causal, seg, -jnp.inf))
    scores = jnp.einsum('bcqhn,bckhn->bcqkh', ch, bh) * decay
    y_diag = jnp.einsum('bcqkh,bckhp->bcqhp', scores, xd)
    to_end = jnp.exp(acum[:, :, -1:, :] - acum)
    chunk_states = jnp.einsum('bckhn,bckh,bckhp->bchpn', bh, to_end, xd)
    chunk_decay = jnp.exp(acum[:, :, -1, :])

    def step(h, inp):
        dec, st = inp
        return h * dec[:, :, None, None] + st, h

    h_last, h_in = lax.scan(step, h0, (jnp.moveaxis(chunk_decay, 1, 0), jnp.moveaxis(chunk_states, 1, 0)))
    h_in = jnp.moveaxis(h_in, 0, 1)
    y_off = jnp.einsum('bcqhn,bchpn->bcqhp', ch, h_in) * jnp.exp(acum)[..., None]
    return (y_diag + y_off).reshape(bsz, l, nh, hp), h_last

def ssm_branch(xbc, dt_raw, z, conv_prev, h0, conv_w, conv_b, dt_bias, a_log, d_skip, out_gain):
    bsz, l, _ = xbc.shape
    full = jnp.concatenate([conv_prev.astype(jnp.float32), xbc], axis=1)
    conv = conv_b + full[:, 0:l] * conv_w[0]
    for i in range(1, CONV_WIDTH):
        conv = conv + full[:, i:i + l] * conv_w[i]
    conv_state = full[:, l:]
    u = jax.nn.silu(conv)
    xs, b_in, c_in = jnp.split(u, [SSM_WIDTH, SSM_WIDTH + SSM_GROUPS * SSM_STATE], axis=-1)
    xs = xs.reshape(bsz, l, SSM_HEADS, SSM_HEAD_DIM)
    b_in = b_in.reshape(bsz, l, SSM_GROUPS, SSM_STATE)
    c_in = c_in.reshape(bsz, l, SSM_GROUPS, SSM_STATE)
    dt = jax.nn.softplus(dt_raw + dt_bias)
    a = -jnp.exp(a_log.astype(jnp.float32))
    y, h_last = ssd_scan(xs, dt, a, b_in, c_in, h0.astype(jnp.float32))
    y = y + xs * d_skip[:, None]
    y = rmsnorm(y.reshape(bsz, l, SSM_WIDTH) * jax.nn.silu(z), out_gain)
    return y, conv_state, h_last

def memory_kv(mem, in_gain, w_k, w_v, k_gain):
    bsz, n, _ = mem.shape
    hm = rmsnorm(mem, in_gain)
    k = rmsnorm((hm @ w_k).reshape(bsz, n, MEM_HEADS, MEM_HEAD_DIM), k_gain)
    v = (hm @ w_v).reshape(bsz, n, MEM_HEADS, MEM_HEAD_DIM)
    return k, v

def memory_attend(h, mem_k, mem_v, w_q, q_gain, w_o):
    bsz, l, _ = h.shape
    q = rmsnorm((h @ w_q).reshape(bsz, l, MEM_HEADS, MEM_HEAD_DIM), q_gain)
    sc = jnp.einsum('blhd,bmhd->bhlm', q, mem_k.astype(jnp.float32)) * (MEM_HEAD_DIM ** -0.5)
    p = jax.nn.softmax(sc, axis=-1)
    o = jnp.einsum('bhlm,bmhd->blhd', p, mem_v.astype(jnp.float32)).reshape(bsz, l, MEM_WIDTH)
    return o @ w_o

def moe_ffn(h, w_router, b_router, w_gate_up, b_gate_up, w_down, b_down):
    b, l, d = h.shape
    n_tok = b * l
    tok = h.reshape(n_tok, d)
    logits = tok @ w_router + b_router
    top_val, top_idx = lax.top_k(logits, TOP_K)
    top_w = jax.nn.softmax(top_val, axis=-1)
    n_assign = n_tok * TOP_K
    flat_e = top_idx.reshape(-1)
    flat_t = jnp.repeat(jnp.arange(n_tok, dtype=jnp.int32), TOP_K)
    flat_w = top_w.reshape(-1)
    order = jnp.argsort(flat_e)
    se = flat_e[order]
    counts = jnp.bincount(flat_e, length=N_EXPERTS)
    padded = (counts + MOE_BLOCK - 1) // MOE_BLOCK * MOE_BLOCK
    pend = jnp.cumsum(padded)
    pstart = pend - padded
    start = jnp.cumsum(counts) - counts
    dest = pstart[se] + jnp.arange(n_assign) - start[se]
    n_blocks = -(-(n_assign + N_EXPERTS * (MOE_BLOCK - 1)) // MOE_BLOCK)
    n_rows = n_blocks * MOE_BLOCK
    row_tok = jnp.zeros((n_rows,), jnp.int32).at[dest].set(flat_t[order])
    row_w = jnp.zeros((n_rows,), jnp.float32).at[dest].set(flat_w[order])
    block_e = jnp.minimum(jnp.searchsorted(pend, jnp.arange(n_blocks) * MOE_BLOCK, side='right'), N_EXPERTS - 1)
    xb = tok[row_tok].reshape(n_blocks, MOE_BLOCK, d)

    def expert_block(args):
        xe, e = args
        gu = xe @ w_gate_up[e] + b_gate_up[e]
        g = jnp.minimum(gu[:, 0::2], SWIGLU_LIMIT)
        u = jnp.clip(gu[:, 1::2], -SWIGLU_LIMIT, SWIGLU_LIMIT)
        act = (u + 1.0) * (g * jax.nn.sigmoid(SWIGLU_ALPHA * g))
        return act @ w_down[e] + b_down[e]

    yb = lax.map(expert_block, (xb, block_e))
    out = jnp.zeros((n_tok, d), jnp.float32).at[row_tok].add(yb.reshape(n_rows, d) * row_w[:, None])
    return out.reshape(b, l, d)

def decoder_layer(x, pos, mem_k, mem_v, win_k_past, win_v_past, conv_prev, ssm_prev,
                  norm_mix, w_in, q_gain, k_gain, conv_w, conv_b, dt_bias, a_log, d_skip, ssm_out_gain, w_out,
                  norm_mem, w_mem_q, mem_q_gain, w_mem_o,
                  norm_ffn, w_router, b_router, w_gate_up, b_gate_up, w_down, b_down):
    b, l, _ = x.shape
    h = rmsnorm(x, norm_mix)
    q, k, v, z, dt_raw, xbc = mixer_projections(h, pos, w_in, q_gain, k_gain)
    if win_k_past is None:
        att = dilated_attention_prompt(q, k, v)
    else:
        att = dilated_attention_sample(q, k, v, win_k_past, win_v_past)
    y_ssm, conv_state, ssm_state = ssm_branch(xbc, dt_raw, z, conv_prev, ssm_prev, conv_w, conv_b,
                                              dt_bias, a_log, d_skip, ssm_out_gain)
    mixed = jnp.concatenate([att.reshape(b, l, ATT_WIDTH), y_ssm], axis=-1)
    x = x + mixed @ w_out
    x = x + memory_attend(rmsnorm(x, norm_mem), mem_k, mem_v, w_mem_q, mem_q_gain, w_mem_o)
    x = x + moe_ffn(rmsnorm(x, norm_ffn), w_router, b_router, w_gate_up, b_gate_up, w_down, b_down)
    return x, k, v, conv_state, ssm_state

def setup_inputs(seed: int = 0) -> dict:
    key = jax.random.key(seed)
    it = iter(jax.random.split(key, 48))

    def normal(shape, scale):
        return jax.random.normal(next(it), shape, jnp.float32) * scale

    def gain(shape):
        return 1.0 + normal(shape, 0.02)

    win_buf = min(MAX_WINDOW, PAST_LEN)
    dt_init = jnp.exp(jax.random.uniform(next(it), (DEPTH, SSM_HEADS), jnp.float32,
                                         math.log(1e-3), math.log(1e-1)))
    a_init = jax.random.uniform(next(it), (DEPTH, SSM_HEADS), jnp.float32, 1.0, 16.0)
    return {
        'x_prompt': normal((BATCH, SEQ, D_MODEL), 1.0),
        'x_sample': normal((DEC_BATCH, DEC_SEQ, D_MODEL), 1.0),
        'cache_win_k': normal((DEPTH, DEC_BATCH, win_buf, ATT_HEADS, ATT_HEAD_DIM), 1.0),
        'cache_win_v': normal((DEPTH, DEC_BATCH, win_buf, ATT_HEADS, ATT_HEAD_DIM), 1.0),
        'state_conv': normal((DEPTH, DEC_BATCH, CONV_WIDTH - 1, CONV_CH), 1.0),
        'state_ssm': normal((DEPTH, DEC_BATCH, SSM_HEADS, SSM_HEAD_DIM, SSM_STATE), 0.1),
        'cache_mem_k': normal((DEPTH, DEC_BATCH, N_MEM, MEM_HEADS, MEM_HEAD_DIM), 1.0),
        'cache_mem_v': normal((DEPTH, DEC_BATCH, N_MEM, MEM_HEADS, MEM_HEAD_DIM), 1.0),
        'mem_prompt': normal((BATCH, N_MEM, D_MODEL), 1.0),
        'norm_mix': gain((DEPTH, D_MODEL)),
        'w_in': normal((DEPTH, D_MODEL, IN_WIDTH), D_MODEL ** -0.5),
        'q_gain': gain((DEPTH, ATT_HEAD_DIM)),
        'k_gain': gain((DEPTH, ATT_HEAD_DIM)),
        'conv_w': normal((DEPTH, CONV_WIDTH, CONV_CH), CONV_WIDTH ** -0.5),
        'conv_b': normal((DEPTH, CONV_CH), 0.02),
        'dt_bias': dt_init + jnp.log(-jnp.expm1(-dt_init)),
        'a_log': jnp.log(a_init),
        'd_skip': gain((DEPTH, SSM_HEADS)),
        'ssm_out_gain': gain((DEPTH, SSM_WIDTH)),
        'w_out': normal((DEPTH, MIX_WIDTH, D_MODEL), MIX_WIDTH ** -0.5),
        'norm_mem': gain((DEPTH, D_MODEL)),
        'mem_in_gain': gain((DEPTH, D_MODEL)),
        'w_mem_q': normal((DEPTH, D_MODEL, MEM_WIDTH), D_MODEL ** -0.5),
        'w_mem_k': normal((DEPTH, D_MODEL, MEM_WIDTH), D_MODEL ** -0.5),
        'w_mem_v': normal((DEPTH, D_MODEL, MEM_WIDTH), D_MODEL ** -0.5),
        'mem_q_gain': gain((DEPTH, MEM_HEAD_DIM)),
        'mem_k_gain': gain((DEPTH, MEM_HEAD_DIM)),
        'w_mem_o': normal((DEPTH, MEM_WIDTH, D_MODEL), MEM_WIDTH ** -0.5),
        'norm_ffn': gain((DEPTH, D_MODEL)),
        'w_router': normal((DEPTH, D_MODEL, N_EXPERTS), D_MODEL ** -0.5),
        'b_router': normal((DEPTH, N_EXPERTS), 0.01),
        'w_gate_up': normal((DEPTH, N_EXPERTS, D_MODEL, 2 * D_FF), D_MODEL ** -0.5),
        'b_gate_up': normal((DEPTH, N_EXPERTS, 2 * D_FF), 0.01),
        'w_down': normal((DEPTH, N_EXPERTS, D_FF, D_MODEL), D_FF ** -0.5),
        'b_down': normal((DEPTH, N_EXPERTS, D_MODEL), 0.01),
    }

def reference(x_prompt, x_sample, cache_win_k, cache_win_v, state_conv, state_ssm, cache_mem_k, cache_mem_v,
              mem_prompt, norm_mix, w_in, q_gain, k_gain, conv_w, conv_b, dt_bias, a_log, d_skip, ssm_out_gain,
              w_out, norm_mem, mem_in_gain, w_mem_q, w_mem_k, w_mem_v, mem_q_gain, mem_k_gain, w_mem_o,
              norm_ffn, w_router, b_router, w_gate_up, b_gate_up, w_down, b_down):
    f32 = jnp.float32
    xp = x_prompt.astype(f32)
    xs = x_sample.astype(f32)
    bp, lp = xp.shape[0], xp.shape[1]
    ls = xs.shape[1]
    pos_p = jnp.arange(lp, dtype=jnp.int32)
    pos_s = PAST_LEN + jnp.arange(ls, dtype=jnp.int32)
    keep = min(MAX_WINDOW, lp)
    wk_p, wv_p, wk_s, wv_s, cv_p, cv_s, st_p, st_s, mk_l, mv_l = ([] for _ in range(10))
    for i in range(DEPTH):
        lw = (norm_mix[i], w_in[i], q_gain[i], k_gain[i], conv_w[i], conv_b[i], dt_bias[i], a_log[i],
              d_skip[i], ssm_out_gain[i], w_out[i], norm_mem[i], w_mem_q[i], mem_q_gain[i], w_mem_o[i],
              norm_ffn[i], w_router[i], b_router[i], w_gate_up[i], b_gate_up[i], w_down[i], b_down[i])
        mk_p, mv_p = memory_kv(mem_prompt, mem_in_gain[i], w_mem_k[i], w_mem_v[i], mem_k_gain[i])
        xp, kp, vp, cp, sp = decoder_layer(
            xp, pos_p, mk_p, mv_p, None, None,
            jnp.zeros((bp, CONV_WIDTH - 1, CONV_CH), f32),
            jnp.zeros((bp, SSM_HEADS, SSM_HEAD_DIM, SSM_STATE), f32), *lw)
        xs, k_new, v_new, c_new, s_new = decoder_layer(
            xs, pos_s, cache_mem_k[i], cache_mem_v[i], cache_win_k[i], cache_win_v[i],
            state_conv[i], state_ssm[i], *lw)
        wk_p.append(kp[:, lp - keep:])
        wv_p.append(vp[:, lp - keep:])
        wk_s.append(k_new)
        wv_s.append(v_new)
        cv_p.append(cp)
        cv_s.append(c_new)
        st_p.append(sp)
        st_s.append(s_new)
        mk_l.append(mk_p)
        mv_l.append(mv_p)
    return (xp.astype(x_prompt.dtype), xs.astype(x_sample.dtype),
            jnp.stack(wk_p), jnp.stack(wv_p), jnp.stack(wk_s), jnp.stack(wv_s),
            jnp.stack(cv_p), jnp.stack(cv_s), jnp.stack(st_p), jnp.stack(st_s),
            jnp.stack(mk_l), jnp.stack(mv_l))


_drawn_inputs = setup_inputs


def setup_inputs(seed=0):
    import zlib

    import numpy as np

    out = dict(_drawn_inputs(seed))
    spreads = {}
    factors = {'q_gain': 5.934,
     'k_gain': 2.874,
     'd_skip': 4.903,
     'norm_mem': 4.041,
     'mem_in_gain': 2.738,
     'mem_q_gain': 5.569,
     'mem_k_gain': 3.054,
     'b_gate_up': 8.0,
     'b_down': 8.0}
    for name, (base, spread) in spreads.items():
        noise = np.random.default_rng([zlib.crc32(name.encode()), seed]).standard_normal(out[name].shape)
        drawn = base * np.exp(spread * noise) if base else spread * noise
        out[name] = __import__('jax').numpy.asarray(drawn.astype(out[name].dtype))
    for name, factor in factors.items():
        out[name] = (out[name] * factor).astype(out[name].dtype)
    return out
```

```python
from contextlib import ExitStack

import concourse.bass as bass
import concourse.mybir as mybir
import numpy as np

F32 = mybir.dt.float32
I32 = mybir.dt.int32
U32 = mybir.dt.uint32
ALU = mybir.AluOpType
ACT = mybir.ActivationFunctionType
AX = mybir.AxisListType

P = 128
D = 1024
KT = D // P
SEQ = 256
NB = 8
NS = 4
NTS = NB * NS
PAST = 1024
NTOK = SEQ + NTS
ROWS = [P, P, NTS]
COL0 = [0, P, 2 * P]
AH, DH = 8, 64
SH, NST = 8, 128
MH, MD, NM = 4, 128, 256
NE, FF = 32, 1024
TOPK = 4
EPS = 1e-6
SLOTS = 64
NPASS_MAX = -(-NTOK // SLOTS)
INW = 3080
NEG = -1.0e30
ROPE_HALF = 8
UNIT = 4096
RING = 6

UNITS = (["q", "k", "v", "z", "xbc0", "xbc1", "h0", "scratch"]
         + [f"{c}{b}" for g in range(2) for c in "KV" for b in range(4 * g, 4 * g + 4)]
         + ["wout0", "wout1", "wmk", "wmv", "wmq"] + [f"mem{i}" for i in range(4)] + ["wmo", "pad", "pad"])
assert len(UNITS) % RING == 0
U = {n: i for i, n in enumerate(UNITS)}


def slot_loads(upto, slot):
    return sum({"s": 0, "p": 0, "K": 2, "V": 2, "m": 2}.get(UNITS[i][0], 1) for i in range(slot, upto, RING))


def constants():
    f = np.float32
    k, q = np.arange(P)[:, None], np.arange(P)[None, :]
    c = {}
    c["ident"] = (k == q).astype(f)
    c["tri"] = (k <= q).astype(f)
    c["strict"] = (k < q).astype(f)
    c["ones"] = np.ones((P, P), f)
    c["eps"] = np.full((P, 1), EPS, f)
    s, t = np.arange(NTS)[:, None], np.arange(NTS)[None, :]
    same = (s // NS) == (t // NS)
    c["tri_s"] = ((s <= t) & same).astype(f)
    c["same_s"] = same.astype(f)
    c["bsel"] = (s // NS == np.arange(NB)[None, :]).astype(f)
    c["iota64"] = np.broadcast_to(np.arange(SLOTS, dtype=f), (P, SLOTS))
    c["iota32"] = np.broadcast_to(np.arange(NE, dtype=f), (P, NE))
    c["thr"] = np.broadcast_to(SLOTS * np.arange(1, NPASS_MAX, dtype=f), (P, NPASS_MAX - 1))
    inv = np.power(f(500000.0), -np.arange(ROPE_HALF, dtype=f) / f(ROPE_HALF))
    ang = np.arange(SEQ, dtype=f)[:, None] * inv[None, :]
    ang_s = (PAST + np.tile(np.arange(NS), 2 * NB)).astype(f)[:, None] * inv[None, :]
    for n, fn in (("cos", np.cos), ("sin", np.sin)):
        c[n] = fn(ang).astype(f).reshape(2, P, ROPE_HALF).transpose(1, 0, 2).reshape(P, -1)
        c[n + "_s"] = fn(ang_s).astype(f)

    def count(dist):
        return sum(((dist >= 0) & (dist % d == 0) & (dist <= w)).astype(f)
                   for w, d in ((128, 1), (512, 4), (2048, 16)))

    def log_count(n, scale):
        return np.where(n > 0, np.log(np.maximum(n, 1)) / scale, NEG).astype(f)

    scale = DH ** -0.5
    for i in range(2):
        n = count((i * P + np.arange(P))[:, None] - np.arange((i + 1) * P)[None, :])
        c[f"bias{i}"] = log_count(n, scale)
    row = np.arange(P)
    step = row % NS
    old = (16 * np.arange(32)[:, None] + np.arange(4)[None, :]).reshape(-1)
    dense = PAST - 512 + (4 * np.arange(P)[None, :] + np.arange(4)[:, None]).reshape(-1)
    c["bias_past"] = log_count(count((PAST + step)[:, None] - np.concatenate([old, dense])[None, :]), scale)
    for g in range(2):
        nk = np.arange(NTS)
        n = count(step[:, None] - (nk % NS)[None, :]) * ((nk // NS)[None, :] == (4 * g + row // 32)[:, None])
        c[f"bias_new{g}"] = log_count(n, scale)
    return c


def packed_constants():
    at, cols, parts = {}, 0, []
    for n, a in constants().items():
        r, w = a.shape
        at[n] = (r, cols, w)
        full = np.zeros((P, w), np.float32)
        full[:r] = a
        parts.append(full)
        cols += w
    return at, np.concatenate(parts, 1)


ROWP = [("q_gain", DH), ("k_gain", DH), ("dt_bias", SH), ("a_log", SH), ("d_skip", SH), ("mem_q_gain", MD),
        ("mem_k_gain", MD), ("b_router", NE), ("norm_ffn", D)]
COLP = [("norm_mix", 8), ("norm_mem", 8), ("mem_in_gain", 8), ("norm_ffn_c", 8), ("ssm_out_gain", 4),
        ("conv_b", 8), ("conv_w", 32), ("qk_gain_s", DH)]


def offsets(pairs):
    at, c = {}, 0
    for n, w in pairs:
        at[n] = (c, w)
        c += w
    return at, c


def build(nc, a, o, until=99):
    const_at, const_np = packed_constants()
    NC = const_np.shape[1]
    row_at, NR = offsets(ROWP)
    col_at, NCP = offsets(COLP)
    with ExitStack() as ctx:
        def sb(name, shape, dt=F32):
            return ctx.enter_context(nc.sbuf_tensor(name, shape, dt))

        sems = {}

        def sem(name):
            if name not in sems:
                sems[name] = ctx.enter_context(nc.semaphore(name))
            return sems[name]

        ring = sb("ring", [P, RING, UNIT])
        X = sb("X", [P, 3, D])
        CN = sb("CN", [P, NC])
        RP = sb("RP", [P, NR])
        CP = sb("CP", [P, NCP])
        mixT = sb("mixT", [P, 8, NTOK])
        WDT = sb("WDT", [P, KT, SH])
        WR = sb("WR", [P, KT, NE])
        small = sb("small", [P, 512])
        top_i = sb("top_i", [P, 3, 8], U32)
        npass_i = sb("npass_i", [P, 1], I32)
        AR = 18800
        arena = sb("arena", [P, AR])
        PS = ctx.enter_context(nc.psum_tensor("PS", [P, 8, 512], F32))

        def cst(n):
            r, c, w = const_at[n]
            return CN[0:r, c:c + w]

        def rowp(n, rows=P):
            c, w = row_at[n]
            return RP[0:rows, c:c + w]

        def colp(n):
            c, w = col_at[n]
            return CP[:, c:c + w]

        def ar(at, *dims):
            n = int(np.prod(dims))
            assert at + n <= AR, (at, dims)
            v = arena[:, at:at + n]
            if len(dims) == 1:
                return v
            names = "abcde"[:len(dims)]
            return v.rearrange("p (" + " ".join(names) + ") -> p " + " ".join(names),
                               **{names[i]: dims[i] for i in range(len(dims))})

        def sm(at, *dims):
            n = int(np.prod(dims))
            assert at + n <= 512
            v = small[:, at:at + n]
            if len(dims) == 1:
                return v
            names = "abcde"[:len(dims)]
            return v.rearrange("p (" + " ".join(names) + ") -> p " + " ".join(names),
                               **{names[i]: dims[i] for i in range(len(dims))})

        def slot(name, *dims):
            v = ring[:, (U[name] if isinstance(name, str) else name) % RING, 0:int(np.prod(dims))]
            if len(dims) == 1:
                return v
            names = "abcde"[:len(dims)]
            return v.rearrange("p (" + " ".join(names) + ") -> p " + " ".join(names),
                               **{names[i]: dims[i] for i in range(len(dims))})

        ident = cst("ident")

        XN = ar(0, 3, D)
        hT = ar(3072, KT, NTOK)
        QK = ar(5376, 2, 2, AH, DH)
        QKS = ar(7424, AH, DH)
        V = ar(7936, 3, AH * DH)
        Z = ar(9472, 3, 512)
        XP = ar(11008, 8, 3 + SEQ)
        XS = ar(13080, 8, NB, 3 + NS)
        QSC = ar(13528, 2 * AH, DH)
        CVS = ar(14552, 8, NTS)
        TAIL = ar(14808, 8, 27)
        CONVO = ar(15024, D)
        UT = ar(16496, 8, NTOK)
        SC = ar(17000, D)
        QB = ar(0, 4, NB, NTS)
        kTs = ar(1024, 4, NTS)
        qT = ar(1152, 4, SEQ)
        kT = ar(2176, 4, SEQ)
        SCO = [ar(5376, 8, P), ar(3200, 8, SEQ)]
        PT = ar(13528, 2, 8, P)
        XB = ar(11008, 3, 768)
        XD = ar(1152, 3, 512)
        XDE = ar(2688, 3, 512)
        HT0 = ar(4224, 512)
        CM = ar(4736, 2, NB, NTS)
        SEG = ar(5376, SH, P)
        DTRI = ar(6400, SH, P)
        DREP = ar(6912, SH, DH)
        STM = ar(7424, 2, P)
        Y = ar(13528, 3, 512)
        HOUT = ar(15064, 4, NST)
        YSQ = ar(15576, 512)
        BNM = ar(16496, 2, NB, P)
        KTB = ar(1152, 2, 4, 5 * P)
        SS = ar(6272, 5 * P + NTS)
        PTS = ar(6944, 6, P)
        HMT = ar(5376, KT, NM)
        MK = ar(7424, 2, MH, MD)
        MV = ar(8448, 2, MH * MD)
        MKT = ar(9472, MH, NM)
        MQ = ar(10496, 3, MH, MD)
        QMT = ar(12032, MH, NTOK)
        QMB = ar(13184, MH, NB, 32)
        SMM = ar(14208, MH, NM)
        PTM = ar(15232, 2, MH, P)
        KTM = ar(16256, 2, MH, NM)
        MP = ar(16256, 2, D)
        SS2 = ar(10496, NM)
        OT = mixT[:, 0:MH, :]
        BGU = ar(5376, 2 * FF)
        BD = ar(7424, D)
        XT = ar(8448, KT, SLOTS)
        AT = ar(8960, 4, P)
        YB = ar(9472, 512)
        SW = ar(14040, 3 * P)
        SEL = ar(10272, 3, SLOTS)
        SELW = ar(10464, 3, 2, SLOTS)
        G1 = ar(10848, 2, SLOTS * 4)
        SG = ar(11360, 2, SLOTS * 4)
        U1 = ar(11872, 2, SLOTS * 4)
        AC = ar(12384, 512)
        EROW = ar(12896, SLOTS)
        POSM = ar(12960, NE + 1, 3)
        GW = ar(13060, NE + 1, 3)
        MSK = ar(13160, 3, NE)
        LG = ar(13256, 3, NE)
        OH4 = ar(13352, 3, TOPK, NE)
        GWT = ar(13736, NTOK)
        SSQ = sm(0, 3)
        RS = sm(3, 3)
        SSH = sm(8, 48)
        DTR = sm(56, 3, SH)
        DTA = sm(80, 3, SH)
        DTV = sm(104, 3, SH)
        ACU = sm(128, 3, SH)
        EAC = sm(152, 3, SH)
        TOE = sm(176, 3, SH)
        DT1 = sm(200, 3, SH)
        AEX = sm(224, SH)
        DEC1 = sm(232, SH)
        DECS = sm(240, 4, NB)
        MX = sm(272, 3, 8)
        NMX = sm(296, 3, 8)
        DEN = sm(320, 3, 8)
        RDEN = sm(344, 3, 8)
        TOPV = sm(368, 3, 8)
        TOPF = sm(392, 3, 8)
        TOPW = sm(416, 3, TOPK)
        CNT = sm(428, 4)
        NPF = sm(432, 1)
        TS = sm(436, 8)

        block = ctx.enter_context(nc.Block())

        @block.tensor
        def _(pe):
            mm = nc.tensor.matmul

            def transpose_rows(src, tiles, n0, free=None):
                for t in tiles:
                    pe.wait_ge(sem("rows_normed"), n0 + t + 1)
                    n = ROWS[t]
                    for k in range(KT):
                        bank, col = (2 * t + k // 4, k % 4 * P) if t < 2 else (4, k * n)
                        last = nc.tensor.transpose(PS[:, bank, col:col + n], src[0:n, t, k * P:(k + 1) * P],
                                                   ident[0:n, 0:n])
                    last.then_inc(sem("rows_turned"), 1)

            def loaded(name):
                u = U[name]
                pe.wait_ge(sem(f"slot{u % RING}_loaded"), 16 * slot_loads(u + 1, u % RING))

            pe.wait_ge(sem("consts_loaded"), 16)
            transpose_rows(XN, (0, 1, 2), 0)
            pe.wait_ge(sem("state_conv_loaded"), 16)
            for m in range(8):
                last = nc.tensor.transpose(PS[:, 5, m * 24:(m + 1) * 24], SC[0:24, m * P:(m + 1) * P],
                                           ident[0:24, 0:24])
            last.then_inc(sem("conv_state_turned"), 1)

            pe.wait_ge(sem("cols_ready"), 3)
            for g, name in enumerate("qkvz"):
                loaded(name)
                w = slot(name, KT, 512)
                for t in range(2):
                    if 2 * g + t == 5:
                        pe.wait_ge(sem("conv_state_kept"), 1)
                    for k in range(KT):
                        last = mm(PS[:, 2 * g + t, :], hT[:, k, t * P:(t + 1) * P], w[:, k, :],
                                  start=k == 0, stop=k == KT - 1)
                    last.then_inc(sem("proj_ready"), 1)
            pe.wait_ge(sem("proj_kept"), 1)
            for k in range(KT):
                for g, name in enumerate("qkvz"):
                    last = mm(PS[32 * g:32 * g + 32, 0, :], hT[:, k, SEQ:NTOK], slot(name, KT, 512)[:, k, :],
                              start=k == 0, stop=k == KT - 1, tile_position=(0, 32 * g))
            last.then_inc(sem("proj_ready"), 1)
            pe.wait_ge(sem("proj_kept"), 2)
            pe.wait_ge(sem("dt_weights_loaded"), 16)
            for t in range(3):
                for k in range(KT):
                    last = mm(PS[0:ROWS[t], 1, t * 8:t * 8 + 8], hT[:, k, COL0[t]:COL0[t] + ROWS[t]], WDT[:, k, :],
                              start=k == 0, stop=k == KT - 1)
            last.then_inc(sem("dt_raw_ready"), 1)
            for m in range(8):
                loaded(f"xbc{m // 4}")
                bank = (2 + m) % 8
                pe.wait_ge(sem("proj_kept"), (bank + 1) if m < 6 else 11)
                if m == 7:
                    pe.wait_ge(sem("dt_raw_kept"), 1)
                w = slot(f"xbc{m // 4}", KT, 512)
                for k in range(KT):
                    last = mm(PS[:, bank, 0:NTOK], w[:, k, m % 4 * P:(m % 4 + 1) * P], hT[:, k, :],
                              start=k == 0, stop=k == KT - 1)
                last.then_inc(sem("xbc_ready"), 1)

            pe.wait_ge(sem("tails_ready"), 1)
            for m in range(8):
                last = nc.tensor.transpose(PS[0:27, 6 + m // 4, m % 4 * P:(m % 4 + 1) * P], TAIL[:, m, :], ident)
            last.then_inc(sem("tail_rows_ready"), 1)

            for t in range(2):
                pe.wait_ge(sem("qk_normed"), t + 1)
                pe.wait_ge(sem("xbc_kept"), 16)
                for j in range(2):
                    for p in range(4):
                        last = nc.tensor.transpose(PS[:, 2 * t + j, p * P:(p + 1) * P],
                                                   QK[:, t, j, 2 * p:2 * p + 2, :].rearrange("p h d -> p (h d)"),
                                                   ident)
                    last.then_inc(sem("qk_turned"), 1)
            pe.wait_ge(sem("qk_normed"), 3)
            for j in range(2):
                r = slice(32 * j, 32 * j + 32)
                for p in range(4):
                    last = nc.tensor.transpose(PS[:, 4 + j, p * NTS:(p + 1) * NTS],
                                               QKS[r, 2 * p:2 * p + 2, :].rearrange("p h d -> p (h d)"),
                                               ident[r, r])
            last.then_inc(sem("qk_turned"), 1)

            pe.wait_ge(sem("tail_rows_kept"), 2)
            pe.wait_ge(sem("qk_kept"), 7)
            for i in range(2):
                for b in range(4):
                    for c in range(2):
                        p, e = 2 * (b // 2) + c, b % 2
                        nk = (i + 1) * P
                        last = mm(PS[:, 4 * (1 - i) + b, c * 256:c * 256 + nk],
                                  qT[64 * e:64 * e + 64, p, i * P:(i + 1) * P], kT[64 * e:64 * e + 64, p, 0:nk],
                                  start=True, stop=True)
                last.then_inc(sem("scores_ready"), 1)

            pe.wait_ge(sem("conv_silu_ready"), 8)
            for t in range(3):
                pe.wait_ge(sem("scores_kept"), 1 if t < 2 else 2)
                n = ROWS[t]
                for m in range(6):
                    last = nc.tensor.transpose(PS[0:n, (4, 6, 0)[t] + m // 4, m % 4 * P:(m % 4 + 1) * P],
                                               UT[:, m, COL0[t]:COL0[t] + n], ident)
                last.then_inc(sem("xb_turned"), 1)

            def turn_probs(i, banks):
                pe.wait_ge(sem("probs_ready"), i + 1)
                for j in range(i + 1):
                    for s in range(8):
                        last = nc.tensor.transpose(PS[:, banks[2 * j + s // 4], s % 4 * P:(s % 4 + 1) * P],
                                                   SCO[i][:, s, j * P:(j + 1) * P], ident)
                last.then_inc(sem("probs_turned"), 1)

            def weigh_values(i, bank):
                pe.wait_ge(sem("probs_kept"), i + 1)
                for s in range(8):
                    b, c = s // 2, s % 2
                    p, e = 2 * (b // 2) + c, b % 2
                    h = 2 * p + e
                    for j in range(i + 1):
                        last = mm(PS[64 * e:64 * e + 64, bank, p * P:(p + 1) * P], V[:, j, h * DH:(h + 1) * DH],
                                  PT[:, j, s, :], start=j == 0, stop=j == i)
                last.then_inc(sem("att_ready"), 1)

            turn_probs(0, (2, 3))
            pe.wait_ge(sem("xb_kept"), 2)
            weigh_values(0, 4)
            turn_probs(1, (2, 3, 5, 6))
            weigh_values(1, 7)

            pe.wait_ge(sem("dta_ready"), 1)
            pe.wait_ge(sem("xb_kept"), 3)
            for t in range(3):
                n = ROWS[t]
                tri = cst("tri") if t < 2 else cst("tri_s")
                tot = cst("ones") if t < 2 else cst("same_s")
                mm(PS[0:n, 0, t * 8:t * 8 + 8], tri, DTA[0:n, t, :], start=True, stop=True)
                last = mm(PS[0:n, 0, 32 + t * 8:40 + t * 8], tot, DTA[0:n, t, :], start=True, stop=True)
            pe.wait_ge(sem("drep_ready"), 1)
            for p in range(4):
                last = mm(PS[:, 0, 64 + 8 * p:72 + 8 * p],
                          DREP[0:NTS, 2 * p:2 * p + 2, :].rearrange("p h d -> p (h d)"), cst("bsel"),
                          start=True, stop=True)
            last.then_inc(sem("cumulated"), 1)

            loaded("h0")
            pe.wait_ge(sem("probs_kept"), 2)
            H0 = slot("h0", NB, 4, NST)
            for b in range(NB):
                if b >= 2:
                    pe.wait_ge(sem("h0t_kept"), b - 1)
                for p in range(4):
                    last = nc.tensor.transpose(PS[:, 1 + b % 2, p * P:(p + 1) * P], H0[:, b, p, :], ident)
                last.then_inc(sem("h0_turned"), 1)
            H0T = slot("scratch", NB, 512)

            for t in range(3):
                n = ROWS[t]
                if t:
                    pe.wait_ge(sem("st_kept"), t)
                else:
                    pe.wait_ge(sem("att_kept"), 2)
                    pe.wait_ge(sem("probs_kept"), 2)
                for g in range(2):
                    last = mm(PS[0:n, 3, g * P:g * P + n], UT[:, 4 + g, COL0[t]:COL0[t] + n],
                              UT[:, 6 + g, COL0[t]:COL0[t] + n], start=True, stop=True)
                last.then_inc(sem("st_ready"), 1)
                pe.wait_ge(sem("dtri_ready"), t + 1)
                pe.wait_ge(sem("seg_kept"), t)
                for half in range(2):
                    last = mm(PS[0:n, 4 + half, 0:4 * n], cst("ones")[0:n, 0:n],
                              DTRI[0:n, 4 * half:4 * half + 4, 0:n], start=True, stop=True)
                last.then_inc(sem("arow_ready"), 1)
                pe.wait_ge(sem("decay_ready"), t + 1)
                pe.wait_ge(sem("y_kept"), t)
                for h in range(SH):
                    last = mm(PS[0:n, 6, h * DH:(h + 1) * DH], SEG[0:n, h, 0:n], XD[0:n, t, h * DH:(h + 1) * DH],
                              start=True, stop=True)
                last.then_inc(sem("y_within_ready"), 1)
                if t == 1:
                    pe.wait_ge(sem("state_ready"), 1)
                    for g in range(2):
                        last = mm(PS[:, 7, g * 256:(g + 1) * 256], UT[:, 6 + g, P:2 * P],
                                  HT0[:, g * 256:(g + 1) * 256], start=True, stop=True)
                    last.then_inc(sem("y_carried_ready"), 1)
                if t == 2:
                    pe.wait_ge(sem("h0t_kept"), NB)
                    pe.wait_ge(sem("cm_ready"), 1)
                    for g in range(2):
                        for b in range(NB):
                            last = mm(PS[0:NTS, 7, g * 256:(g + 1) * 256], CM[:, g, b, :],
                                      H0T[:, b, g * 256:(g + 1) * 256], start=b == 0, stop=b == NB - 1)
                    last.then_inc(sem("y_carried_ready"), 1)
                if t < 2:
                    pe.wait_ge(sem("xde_ready"), 1)
                    pe.wait_ge(sem("h0t_kept"), NB)
                    pe.wait_ge(sem("state_ready"), t)
                    for g in range(2):
                        last = mm(PS[:, 1, g * 256:(g + 1) * 256], XB[:, t, 512 + g * P:512 + (g + 1) * P],
                                  XDE[:, t, g * 256:(g + 1) * 256], start=True, stop=True)
                    last.then_inc(sem("chunk_state_ready"), 1)
            pe.wait_ge(sem("state_ready"), 2)
            for p in range(4):
                last = nc.tensor.transpose(PS[:, 2, p * P:(p + 1) * P], HT0[:, p * P:(p + 1) * P], ident)
            last.then_inc(sem("state_rows_ready"), 1)
            pe.wait_ge(sem("bnm_ready"), 1)
            pe.wait_ge(sem("seg_kept"), 3)
            for n in range(8):
                p, half = n // 2, n % 2
                if n >= 2:
                    pe.wait_ge(sem("h_updated"), n - 1)
                last = mm(PS[:, 4 + n % 2, :], XDE[0:NTS, 2, p * P:(p + 1) * P],
                          BNM[0:NTS, p // 2, 4 * half:4 * half + 4, :].rearrange("p b n -> p (b n)"),
                          start=True, stop=True)
                last.then_inc(sem("h_added"), 1)

            for t in range(3):
                n = ROWS[t]
                pe.wait_ge(sem("y_normed"), t + 1)
                if t == 0:
                    pe.wait_ge(sem("ssd_exps_ready"), 1)
                if t == 2:
                    pe.wait_ge(sem("state_rows_kept"), 1)
                for k in range(4):
                    last = nc.tensor.transpose(PS[:, t, k * n:(k + 1) * n], Y[0:n, t, k * P:(k + 1) * P],
                                               ident[0:n, 0:n])
                last.then_inc(sem("y_turned"), 1)

            for g in range(2):
                for bb in range(2):
                    for b in range(2):
                        name = f"K{4 * g + 2 * bb + b}"
                        loaded(name)
                        K = slot(name, 5, 512)
                        for j in range(5):
                            n = 20 * g + 10 * bb + 5 * b + j
                            pe.wait_ge(sem("kt_kept"), max(n - 2, 0))
                            if n == 0:
                                pe.wait_ge(sem("h_updated"), 8)
                                pe.wait_ge(sem("st_kept"), 3)
                            for p in range(4):
                                last = nc.tensor.transpose(PS[:, 3 + n % 3, p * P:(p + 1) * P],
                                                           K[:, j, p * P:(p + 1) * P], ident)
                            last.then_inc(sem("kt_turned"), 1)
                    pe.wait_ge(sem("kt_kept"), 20 * g + 10 * (bb + 1))
                    if g == 0 and bb == 0:
                        pe.wait_ge(sem("y_kept"), 3)
                    if bb == 0:
                        pe.wait_ge(sem("scores_s_kept"), g)
                    for part in range(3):
                        for p in range(4):
                            for b in range(2):
                                r = 64 * bb + 32 * b
                                batch = 4 * g + 2 * bb + b
                                lhs = QB[:, p, batch, :]
                                if part == 0:
                                    dst, rhs = PS[r:r + 32, 6, :], KTB[:, b, p, 0:512]
                                elif part == 1:
                                    dst, rhs = PS[r:r + 32, 7, 0:P], KTB[:, b, p, 512:640]
                                else:
                                    dst, rhs = PS[r:r + 32, 7, P:P + NTS], kTs[:, p, :]
                                last = mm(dst, lhs, rhs, start=p == 0, stop=p == 3, tile_position=(0, r),
                                          skip_group_check=True)
                    last.then_inc(sem("scores_s_ready"), 1)
                pe.wait_ge(sem("probs_ready"), 3 + g)
                for j in range(6):
                    w = P if j < 5 else NTS
                    last = nc.tensor.transpose(PS[0:w, 3 + j // 4, j % 4 * P:(j % 4 + 1) * P],
                                               SS[:, j * P:j * P + w], ident)
                last.then_inc(sem("probs_turned"), 1)
                pe.wait_ge(sem("probs_s_kept"), 2 * (g + 1))
                if g == 0:
                    pe.wait_ge(sem("y_turned_kept"), 1)
                for b in range(4):
                    name = f"V{4 * g + b}"
                    loaded(name)
                    Vc = slot(name, 5, 512)
                    for p in range(4):
                        dst = PS[:, 0, ((4 * g + b) * 4 + p) * 8:((4 * g + b) * 4 + p) * 8 + 8]
                        cols = slice(32 * b + 8 * p, 32 * b + 8 * p + 8)
                        for j in range(5):
                            mm(dst, Vc[:, j, p * P:(p + 1) * P], PTS[:, j, cols], start=j == 0, stop=False)
                        last = mm(dst, V[0:NTS, 2, p * P:(p + 1) * P], PTS[0:NTS, 5, cols], start=False, stop=True)
                    last.then_inc(sem("att_s_ready"), 1)

            def project_rows(lhs, nk, w_of, sem_out):
                for t in range(2):
                    for half in range(2):
                        w = w_of(half)
                        for k in range(nk):
                            last = mm(PS[:, 2 * t + half, :], lhs[:, k, t * P:(t + 1) * P], w(k),
                                      start=k == 0, stop=k == nk - 1)
                        last.then_inc(sem(sem_out), 1)
                for k in range(nk):
                    for half in range(2):
                        last = mm(PS[32 * half:32 * half + 32, 4, :], lhs[:, k, SEQ:NTOK], w_of(half)(k),
                                  start=k == 0, stop=k == nk - 1, tile_position=(0, 32 * half))
                last.then_inc(sem(sem_out), 1)

            def wout(half):
                loaded(f"wout{half}")
                w = slot(f"wout{half}", KT, 512)
                return lambda k: w[:, k, :]

            pe.wait_ge(sem("mix_ready"), 1)
            pe.wait_ge(sem("y_turned_kept"), 3)
            project_rows(mixT, 8, wout, "mixed_ready")

            for t in range(2):
                pe.wait_ge(sem("rows_normed"), 3 + t + 1)
                if t == 1:
                    pe.wait_ge(sem("hm_kept"), 1)
                else:
                    pe.wait_ge(sem("probs_s_kept"), 4)
                    pe.wait_ge(sem("scores_s_kept"), 2)
                for k in range(KT):
                    last = nc.tensor.transpose(PS[:, 5 + k // 4, k % 4 * P:(k % 4 + 1) * P],
                                               XN[:, t, k * P:(k + 1) * P], ident)
                last.then_inc(sem("hm_turned"), 1)
            pe.wait_ge(sem("hm_kept"), 2)
            for n in range(4):
                kv, t = n // 2, n % 2
                name = ("wmk", "wmv")[kv]
                loaded(name)
                w = slot(name, KT, 512)
                if n == 2:
                    pe.wait_ge(sem("mkv_kept"), 1)
                if n == 3:
                    pe.wait_ge(sem("mkv_kept"), 2)
                for k in range(KT):
                    last = mm(PS[:, (5, 6, 7, 5)[n], :] if n != 2 else PS[:, 7, :], HMT[:, k, t * P:(t + 1) * P],
                              w[:, k, :], start=k == 0, stop=k == KT - 1)
                last.then_inc(sem("mkv_ready"), 1)
            pe.wait_ge(sem("mk_normed"), 1)
            pe.wait_ge(sem("mkv_kept"), 4)
            for t in range(2):
                for h in range(MH):
                    last = nc.tensor.transpose(PS[:, 6 + t, h * P:(h + 1) * P], MK[:, t, h, :], ident)
                last.then_inc(sem("mk_turned"), 1)

            pe.wait_ge(sem("residual_ready"), 1)
            transpose_rows(XN, (0, 1, 2), 5)
            pe.wait_ge(sem("cols_ready"), 6)
            loaded("wmq")
            w = slot("wmq", KT, 512)
            for t in range(3):
                for k in range(KT):
                    last = mm(PS[0:ROWS[t], t, :], hT[:, k, COL0[t]:COL0[t] + ROWS[t]], w[:, k, :],
                              start=k == 0, stop=k == KT - 1)
                last.then_inc(sem("mq_ready"), 1)
            for t in range(3):
                n = ROWS[t]
                pe.wait_ge(sem("mq_normed"), t + 1)
                for h in range(MH):
                    last = nc.tensor.transpose(PS[:, 3 + t, h * n:(h + 1) * n], MQ[0:n, t, h, :], ident[0:n, 0:n])
                last.then_inc(sem("mq_turned"), 1)
            pe.wait_ge(sem("mk_turned_kept"), 2)
            pe.wait_ge(sem("mq_turned_kept"), 4)
            for i in range(2):
                for h in range(MH):
                    last = mm(PS[:, (6, 0)[i] + h // 2, h % 2 * 256:(h % 2 + 1) * 256], QMT[:, h, i * P:(i + 1) * P],
                              MKT[:, h, :], start=True, stop=True)
                last.then_inc(sem("mscores_ready"), 1)
            for i in range(2):
                pe.wait_ge(sem("probs_ready"), 5 + i)
                for j in range(2):
                    for h in range(MH):
                        last = nc.tensor.transpose(PS[:, 2 + 2 * i + j, h * P:(h + 1) * P],
                                                   SMM[:, h, j * P:(j + 1) * P], ident)
                last.then_inc(sem("probs_turned"), 1)
                pe.wait_ge(sem("mprobs_kept"), 2 * (i + 1))
                if i == 1:
                    pe.wait_ge(sem("mo_kept"), 1)
                for h in range(MH):
                    for j in range(2):
                        last = mm(PS[:, 2 + 2 * i, h * P:(h + 1) * P], MV[:, j, h * P:(h + 1) * P],
                                  PTM[:, j, h, :], start=j == 0, stop=j == 1)
                last.then_inc(sem("mo_ready"), 1)
            for g in range(2):
                for u in range(2):
                    name = f"mem{2 * g + u}"
                    loaded(name)
                    M = slot(name, 2, 2, 2, MH * MD)
                    for b in range(2):
                        for j in range(2):
                            n = 8 * g + 4 * u + 2 * b + j
                            pe.wait_ge(sem("ktm_kept"), max(n - 1, 0))
                            for h in range(MH):
                                last = nc.tensor.transpose(PS[:, (3, 5)[n % 2], h * P:(h + 1) * P],
                                                           M[:, 0, b, j, h * P:(h + 1) * P], ident)
                            last.then_inc(sem("ktm_turned"), 1)
                    pe.wait_ge(sem("ktm_kept"), 8 * g + 4 * (u + 1))
                    if u == 0:
                        pe.wait_ge(sem("exp_ready"), 6 + g)
                    for h in range(MH):
                        for b in range(2):
                            r = 64 * u + 32 * b
                            last = mm(PS[r:r + 32, 6, 0:NM], QMB[:, h, 4 * g + 2 * u + b, :], KTM[:, b, h, :],
                                      start=h == 0, stop=h == MH - 1, tile_position=(0, r))
                    last.then_inc(sem("mscores_s_ready"), 1)
                pe.wait_ge(sem("probs_ready"), 7 + g)
                for j in range(2):
                    last = nc.tensor.transpose(PS[:, 7, j * P:(j + 1) * P], SS2[:, j * P:(j + 1) * P], ident)
                last.then_inc(sem("probs_turned"), 1)
                pe.wait_ge(sem("mprobs_kept"), 4 + g + 1)
                if g == 0:
                    pe.wait_ge(sem("mo_kept"), 2)
                for b in range(4):
                    M = slot(f"mem{2 * g + b // 2}", 2, 2, 2, MH * MD)
                    for h in range(MH):
                        for j in range(2):
                            last = mm(PS[:, 4, (h * NB + 4 * g + b) * NS:(h * NB + 4 * g + b + 1) * NS],
                                      M[:, 1, b % 2, j, h * P:(h + 1) * P],
                                      PTM[:, 0, j, 32 * b + 4 * h:32 * b + 4 * h + 4], start=j == 0, stop=j == 1)
                last.then_inc(sem("mo_ready"), 1)

            def wmo(half):
                loaded("wmo")
                w = slot("wmo", MH, D)
                return lambda k: w[:, k, half * 512:(half + 1) * 512]

            pe.wait_ge(sem("mo_kept"), 3)
            project_rows(OT, MH, wmo, "mixed_ready")

            pe.wait_ge(sem("residual_ready"), 2)
            transpose_rows(XN, (0, 1, 2), 8)
            pe.wait_ge(sem("cols_ready"), 9)
            pe.wait_ge(sem("router_loaded"), 16)
            for t in range(3):
                for k in range(KT):
                    last = mm(PS[0:ROWS[t], 5, t * NE:(t + 1) * NE], hT[:, k, COL0[t]:COL0[t] + ROWS[t]], WR[:, k, :],
                              start=k == 0, stop=k == KT - 1)
            last.then_inc(sem("logits_ready"), 1)
            pe.wait_ge(sem("routed"), 1)
            for t in range(3):
                n = ROWS[t]
                for s in range(t + 1):
                    m = ROWS[s]
                    lhs = (cst("strict") if s == t else cst("ones"))[0:m, 0:n]
                    mm(PS[0:n, 6, t * NE:(t + 1) * NE], lhs, MSK[0:m, s, :], start=s == 0, stop=s == t)
            for s in range(3):
                m = ROWS[s]
                last = mm(PS[:, 6, 96:128], cst("ones")[0:m, :], MSK[0:m, s, :], start=s == 0, stop=s == 2)
            last.then_inc(sem("ranks_ready"), 1)
            pe.wait_ge(sem("gw_ready"), 1)
            for t in range(3):
                n = ROWS[t]
                last = nc.tensor.transpose(PS[0:NE, 7, COL0[t]:COL0[t] + n], GW[0:n, 0:NE, t], ident[0:n, 0:n])
            last.then_inc(sem("sw_turned"), 1)
            pe.wait_ge(sem("gwt_kept"), 1)
            pe.wait_ge(sem("expert_biases_loaded"), 32)
            for t in range(3):
                for half in range(2):
                    bank = 2 * t + half
                    last = mm(PS[0:ROWS[t], bank, :], GWT[0:NE, COL0[t]:COL0[t] + ROWS[t]],
                              BD[0:NE, half * 512:(half + 1) * 512], start=True, stop=True)
            last.then_inc(sem("gathered"), 1)
            pe.wait_ge(sem("scatter_added"), 1)

            front = len(UNITS)

            def gather(n):
                pe.wait_ge(sem("sel_ready"), n + 1)
                for k in range(KT):
                    for t in range(3):
                        m = ROWS[t]
                        last = mm(PS[:, 2, k * SLOTS:(k + 1) * SLOTS], XN[0:m, t, k * P:(k + 1) * P],
                                  SEL[0:m, t, :], start=t == 0, stop=t == 2)
                last.then_inc(sem("gathered"), 1)

            def scatter(n, t):
                pe.wait_ge(sem("scatter_added"), n + 1)
                for half in range(2):
                    r = slice(64 * half, 64 * half + 64)
                    last = mm(PS[:, 6 + half, :], SW[r, t * P:(t + 1) * P], YB[r, :],
                              start=True, stop=True)
                last.then_inc(sem("scattered"), 1)

            npass = pe.value_load(npass_i[0:1, 0:1], min_val=1, max_val=NPASS_MAX)
            with pe.Fori(0, npass) as r:
                pe.wait_ge(sem("sw_cleared"), r + 1)
                gather(r * (NE + 1))
                with pe.Fori(0, NE) as e:
                    it = r * NE + e
                    q = r * (NE + 1) + e
                    pe.wait_ge(sem("xt_ready"), q + 1)
                    pe.wait_ge(sem("erow_ready"), q + 1)
                    pe.wait_ge(sem("act_ready"), it + 1)
                    halves = [(nb, half) for nb in range(2) for half in range(2)]
                    for nb, half in halves:
                        c = half * 1024 + nb * 512
                        mm(PS[64 * half:64 * half + 64, nb, :], EROW[0:NE, :], BGU[0:NE, c:c + 512],
                           start=True, stop=False, tile_position=(0, 64 * half))
                    for k in range(KT):
                        j = k // 2
                        if k % 2 == 0:
                            pe.wait_ge(sem(f"slot{j}_loaded"), 16 * slot_loads(front, j) + 16 + it * 16)
                        w = slot(j, 2, 2 * FF)
                        for nb, half in halves:
                            c = half * 1024 + nb * 512
                            last = mm(PS[64 * half:64 * half + 64, nb, :], XT[:, k, :], w[:, k % 2, c:c + 512],
                                      start=False, stop=k == KT - 1, tile_position=(0, 64 * half))
                        if k % 2 == 1 and k < KT - 1:
                            last.then_inc(sem("expert_units_used"), 1)
                    last.then_inc(sem("gate_up_ready"), 1)
                    pe.wait_ge(sem("y_rows_ready"), it + 1)
                    pe.wait_ge(sem("sw_ready"), it + 1)
                    scatter(3 * q, 0)
                    gather(q + 1)
                    pe.wait_ge(sem("act_ready"), it + 2)
                    for c in range(4):
                        last = nc.tensor.transpose(PS[:, 4, c * P:(c + 1) * P], AC[:, c * P:(c + 1) * P], ident)
                    last.then_inc(sem("act_turned"), 1)
                    scatter(3 * q + 1, 1)
                    pe.wait_ge(sem("at_ready"), it + 1)
                    for k in range(KT):
                        j = 4 + k // 4
                        if k % 4 == 0:
                            pe.wait_ge(sem(f"slot{j}_loaded"), 16 * slot_loads(front, j) + 16 + it * 16)
                        if k == 4:
                            scatter(3 * q + 2, 2)
                        w = slot(j, 4, D)
                        for half in range(2):
                            last = mm(PS[64 * half:64 * half + 64, 5, :], AT[:, k % 4, 64 * (k // 4):64 * (k // 4) + 64],
                                      w[:, k % 4, half * 512:(half + 1) * 512],
                                      start=k == 0, stop=k == KT - 1, tile_position=(0, 64 * half))
                        if k == 3:
                            last.then_inc(sem("expert_units_used"), 1)
                    last.then_inc(sem("down_ready"), 1)
                    pe.wait_ge(sem("selw_ready"), it + 1)
                    for t in range(3):
                        n = ROWS[t]
                        last = nc.tensor.transpose(PS[:, 3, COL0[t]:COL0[t] + n],
                                                   SELW[0:n, t].rearrange("p a s -> p (a s)"), ident[0:n, 0:n])
                    last.then_inc(sem("sw_turned"), 1)
                pe.wait_ge(sem("y_rows_ready"), r * NE + NE + 1)
                pe.wait_ge(sem("sw_ready"), r * NE + NE + 1)
                for t in range(3):
                    scatter(3 * (r * (NE + 1) + NE) + t, t)

        @block.vector
        def _(dve):
            v = nc.vector
            own, roots = [0], [0]

            def step(ins):
                own[0] += 1
                ins.then_inc(sem("dve_steps"), 1)

            def settle():
                dve.wait_ge(sem("dve_steps"), own[0])

            def bc(ap, axis, n):
                ap = ap.unsqueeze(axis)
                shape = list(ap.shape)
                shape[axis] = n
                return ap.to_broadcast(shape)

            def inverse_root(dst):
                roots[0] += 1
                dve.wait_ge(sem("roots_ready"), roots[0])
                step(v.reciprocal(dst, dst))
                settle()

            def norm_rows(src, tiles, gain=None):
                inverse_root(RS[:, 0:len(tiles)])
                for t in tiles:
                    n = ROWS[t]
                    if gain is None:
                        ins = v.tensor_scalar(XN[0:n, t, :], src[0:n, t, :], RS[0:n, t:t + 1], None, ALU.mult)
                    else:
                        ins = v.scalar_tensor_tensor(XN[0:n, t, :], src[0:n, t, :], RS[0:n, t:t + 1], gain[0:n],
                                                     ALU.mult, ALU.mult)
                    ins.then_inc(sem("rows_normed"), 1)

            def keep_columns(n0, gain=None):
                for t in range(3):
                    n = ROWS[t]
                    dve.wait_ge(sem("rows_turned"), n0 + t + 1)
                    for b in range(2):
                        src = (PS[:, 2 * t + b, :] if t < 2 else PS[:, 4, 4 * b * n:4 * (b + 1) * n])
                        src = src.rearrange("p (k n) -> p k n", k=4)
                        dst = hT[:, 4 * b:4 * b + 4, COL0[t]:COL0[t] + n]
                        if gain is None:
                            ins = v.tensor_copy(dst, src)
                        else:
                            ins = v.tensor_tensor(dst, src, bc(colp(gain)[:, 4 * b:4 * b + 4], 2, n), ALU.mult)
                        if b:
                            ins.then_inc(sem("cols_ready"), 1)

            def head_norm(x, n, heads, width, gain, scratch):
                sq = scratch[0:n, 0:heads, :]
                step(v.tensor_tensor(sq, x, x, ALU.mult))
                settle()
                ss = SSH[0:n, 0:heads]
                v.tensor_reduce(ss, sq, AX.X, ALU.add).then_inc(sem("head_squares_ready"), 1)
                inverse_root(ss)
                step(v.tensor_tensor(x, x, bc(ss, 2, width), ALU.mult))
                settle()

            def rope(x, n, heads, cos, sin, scratch):
                r = ROPE_HALF
                x1, x2 = x[:, :, 0:r], x[:, :, r:2 * r]
                c, s = bc(cos, 1, heads), bc(sin, 1, heads)
                t = [scratch[0:n, 0:heads, i * r:(i + 1) * r] for i in range(4)]
                step(v.tensor_tensor(t[0], x1, c, ALU.mult))
                step(v.tensor_tensor(t[1], x2, s, ALU.mult))
                step(v.tensor_tensor(t[2], x2, c, ALU.mult))
                step(v.tensor_tensor(t[3], x1, s, ALU.mult))
                settle()
                step(v.tensor_tensor(x1, t[0], t[1], ALU.subtract))
                return v.tensor_tensor(x2, t[2], t[3], ALU.add)

            step(v.memset(SSQ, 1.0))
            dve.wait_ge(sem("dve_steps"), 1)
            v.memset(small[:, 8:512], 0.0).then_inc(sem("small_cleared"), 1)
            dve.wait_ge(sem("consts_loaded"), 16)
            dve.wait_ge(sem("params_loaded"), 32)
            norm_rows(X, (0, 1, 2))
            keep_columns(0, "norm_mix")

            dve.wait_ge(sem("small_cleared"), 1)
            for t in range(2):
                dve.wait_ge(sem("proj_kept"), 3 + t)
                x = QK[:, t].rearrange("p j h d -> p (j h) d")
                head_norm(x, P, 2 * AH, DH, None, QSC)
                g = RP[:, 0:2 * DH].rearrange("p (j d) -> p j d", j=2)
                step(v.tensor_tensor(QK[:, t], QK[:, t], bc(g, 2, AH), ALU.mult))
                settle()
                rope(x, P, 2 * AH, cst("cos")[:, 8 * t:8 * t + 8], cst("sin")[:, 8 * t:8 * t + 8],
                     QSC).then_inc(sem("qk_normed"), 1)
                dve.wait_ge(sem("qk_normed"), t + 1)
            dve.wait_ge(sem("dt_raw_ready"), 1)
            step(v.tensor_tensor(DTR[:, 0:2, :], PS[:, 1, 0:16].rearrange("p (t h) -> p t h", t=2),
                                 bc(rowp("dt_bias"), 1, 2), ALU.add))
            v.tensor_tensor(DTR[0:NTS, 2, :], PS[0:NTS, 1, 16:24], rowp("dt_bias", NTS),
                            ALU.add).then_inc(sem("dt_raw_kept"), 1)
            dve.wait_ge(sem("proj_kept"), 9)
            x = QKS[0:64]
            head_norm(x, 64, AH, DH, None, QSC)
            step(v.tensor_tensor(x, x, bc(colp("qk_gain_s")[0:64], 1, AH), ALU.mult))
            settle()
            rope(x, 64, AH, cst("cos_s"), cst("sin_s"), QSC).then_inc(sem("qk_normed"), 1)
            dve.wait_ge(sem("dt_raw_kept"), 1)
            settle()
            v.scalar_tensor_tensor(DT1, DTR, -1.0, DTR, ALU.mult, ALU.max).then_inc(sem("dt_abs_ready"), 1)

            w = colp("conv_w")
            for m in range(8):
                dve.wait_ge(sem("xbc_kept"), 2 * m + 2)
                if m == 0:
                    dve.wait_ge(sem("pool_cleared"), 1)
                    dve.wait_ge(sem("conv_state_turned"), 1)
                for i in range(4):
                    if i == 0:
                        step(v.tensor_scalar(UT[:, m, 0:SEQ], XP[:, m, 0:SEQ], w[:, m:m + 1], None, ALU.mult))
                    else:
                        step(v.scalar_tensor_tensor(UT[:, m, 0:SEQ], XP[:, m, i:i + SEQ], w[:, 8 * i + m:8 * i + m + 1],
                                                    UT[:, m, 0:SEQ], ALU.mult, ALU.add))
                    settle()
            us = UT[:, :, SEQ:NTOK].rearrange("p m (b t) -> p m b t", b=NB)
            cv = CVS.rearrange("p m (b t) -> p m b t", b=NB)
            dve.wait_ge(sem("conv_state_kept"), 1)
            for i in range(4):
                wi = bc(bc(w[:, 8 * i:8 * i + 8], 2, NB), 3, NS)
                step(v.tensor_tensor(cv if i else us, XS[:, :, :, i:i + NS], wi, ALU.mult))
                settle()
                if i:
                    ins = v.tensor_tensor(us, us, cv, ALU.add)
                    if i < 3:
                        step(ins)
                        settle()
            ins.then_inc(sem("conv_ready"), 1)

            dve.wait_ge(sem("dt_log_ready"), 1)
            step(v.tensor_scalar(DTR[:, :, :], DTR[:, :, :], 0.0, None, ALU.max))
            settle()
            step(v.tensor_tensor(DTV[:, :, :], DTR[:, :, :], DT1[:, :, :], ALU.add))
            settle()
            v.scalar_tensor_tensor(DTA[:, :, :], DTV[:, :, :], -1.0, bc(AEX, 1, 3), ALU.mult,
                                   ALU.mult).then_inc(sem("dta_ready"), 1)

            dve.wait_ge(sem("window_stored"), 64)
            dve.wait_ge(sem("qk_turned"), 5)
            for i in range(2):
                nk = (i + 1) * P
                dve.wait_ge(sem("scores_ready"), i + 1)
                src = PS[:, 4 * (1 - i):4 * (1 - i) + 4, :].rearrange("p b (c k) -> p b c k", c=2)[:, :, :, 0:nk]
                dst = SCO[i].rearrange("p (b c) k -> p b c k", c=2)
                v.tensor_tensor(dst, src, bc(bc(cst(f"bias{i}"), 1, 2), 1, 4), ALU.add).then_inc(sem("scores_kept"), 1)
                dve.wait_ge(sem("scores_kept"), i + 1)
                step(v.tensor_reduce(MX[:, i, :], SCO[i], AX.X, ALU.max))
                settle()
                v.tensor_scalar(NMX[:, i, :], MX[:, i, :], -DH ** -0.5, None, ALU.mult).then_inc(sem("max_ready"), 1)
            for i in range(2):
                dve.wait_ge(sem("exp_ready"), i + 1)
                step(v.reciprocal(RDEN[:, i, :], DEN[:, i, :]))
                settle()
                v.tensor_tensor(SCO[i], SCO[i], bc(RDEN[:, i, :], 2, (i + 1) * P),
                                ALU.mult).then_inc(sem("probs_ready"), 1)

            dve.wait_ge(sem("dta_ready"), 1)
            for t in range(3):
                n = ROWS[t]
                dve.wait_ge(sem("xb_kept"), t + 1)
                if t == 0:
                    dve.wait_ge(sem("scores_ready"), 2)
                step(v.tensor_tensor(XD[0:n, t, :].rearrange("p (h d) -> p h d", h=SH),
                                     XB[0:n, t, 0:512].rearrange("p (h d) -> p h d", h=SH),
                                     bc(DTV[0:n, t, :], 2, DH), ALU.mult))
            dve.wait_ge(sem("cumulated"), 1)
            for t in range(3):
                n = ROWS[t]
                step(v.tensor_copy(ACU[0:n, t, :], PS[0:n, 0, 8 * t:8 * t + 8]))
            settle()
            for t in range(3):
                n = ROWS[t]
                ins = v.tensor_tensor(DT1[0:n, t, :], PS[0:n, 0, 32 + 8 * t:40 + 8 * t], ACU[0:n, t, :], ALU.subtract)
            ins.then_inc(sem("acum_ready"), 1)
            dve.wait_ge(sem("ssd_exps_ready"), 1)
            dve.wait_ge(sem("probs_turned"), 2)
            settle()
            for t in range(3):
                n = ROWS[t]
                ins = v.tensor_tensor(XDE[0:n, t, :].rearrange("p (h d) -> p h d", h=SH),
                                      XD[0:n, t, :].rearrange("p (h d) -> p h d", h=SH),
                                      bc(TOE[0:n, t, :], 2, DH), ALU.mult)
            ins.then_inc(sem("xde_ready"), 1)
            for t in range(3):
                n = ROWS[t]
                tri = cst("tri") if t < 2 else cst("tri_s")
                dve.wait_ge(sem("st_ready"), t + 1)
                v.tensor_tensor(STM[0:n, :, 0:n], PS[0:n, 3, 0:256].rearrange("p (g q) -> p g q", g=2)[:, :, 0:n],
                                bc(tri, 1, 2), ALU.mult).then_inc(sem("st_kept"), 1)
                dve.wait_ge(sem("arow_ready"), t + 1)
                dve.wait_ge(sem("y_within_ready"), t)
                seg = SEG[0:n, :, 0:n].rearrange("p (a h) q -> p a h q", a=2)
                src = PS[0:n, 4:6, 0:4 * n].rearrange("p a (h q) -> p a h q", h=4)
                acu = bc(ACU[0:n, t, :].rearrange("p (a h) -> p a h", a=2), 3, n)
                v.tensor_tensor(seg, src, acu, ALU.subtract).then_inc(sem("seg_kept"), 1)
                dve.wait_ge(sem("seg_kept"), t + 1)
                v.tensor_scalar(SEG[0:n, :, 0:n], SEG[0:n, :, 0:n], 0.0, None, ALU.min).then_inc(sem("seg_ready"), 1)
                dve.wait_ge(sem("seg_exp_ready"), t + 1)
                dve.wait_ge(sem("st_kept"), t + 1)
                seg = SEG[0:n, :, 0:n].rearrange("p (g h) q -> p g h q", g=2)
                v.tensor_tensor(seg, seg, bc(STM[0:n, :, 0:n], 2, 4), ALU.mult).then_inc(sem("decay_ready"), 1)
                y = Y[0:n, t, :]
                yh = y.rearrange("p (h d) -> p h d", h=SH)
                if t == 0:
                    dve.wait_ge(sem("att_ready"), 2)
                step(v.tensor_tensor(yh, XB[0:n, t, 0:512].rearrange("p (h d) -> p h d", h=SH),
                                     bc(rowp("d_skip", n), 2, DH), ALU.mult))
                if t:
                    dve.wait_ge(sem("y_carried_ready"), t)
                    step(v.tensor_tensor(YSQ[0:n].rearrange("p (h d) -> p h d", h=SH),
                                         PS[0:n, 7, :].rearrange("p (h d) -> p h d", h=SH),
                                         bc(EAC[0:n, t, :], 2, DH), ALU.mult))
                    settle()
                    step(v.tensor_tensor(y, y, YSQ[0:n], ALU.add))
                settle()
                dve.wait_ge(sem("y_within_ready"), t + 1)
                v.tensor_tensor(y, y, PS[0:n, 6, :], ALU.add).then_inc(sem("y_kept"), 1)
                dve.wait_ge(sem("y_kept"), t + 1)
                dve.wait_ge(sem("z_silu_ready"), t + 1)
                v.tensor_tensor(y, y, Z[0:n, t, :], ALU.mult).then_inc(sem("y_gated"), 1)
                if t < 2:
                    dve.wait_ge(sem("chunk_state_ready"), t + 1)
                    if t == 1:
                        h3 = HT0.rearrange("p (h d) -> p h d", h=SH)
                        step(v.tensor_tensor(h3, h3, bc(DEC1, 2, DH), ALU.mult))
                        settle()
                        v.tensor_tensor(HT0, HT0, PS[:, 1, :], ALU.add).then_inc(sem("state_ready"), 1)
                    else:
                        v.tensor_copy(HT0, PS[:, 1, :]).then_inc(sem("state_ready"), 1)
                        dve.wait_ge(sem("state_ready"), 1)
            dve.wait_ge(sem("h0_scaled"), 4)
            H0 = slot("h0", NB, 4, NST)
            for n in range(8):
                p, half = n // 2, n % 2
                dve.wait_ge(sem("h_added"), n + 1)
                dst = H0[:, 4 * half:4 * half + 4, p, :]
                v.tensor_tensor(dst, dst, PS[:, 4 + n % 2, :].rearrange("p (b n) -> p b n", b=4),
                                ALU.add).then_inc(sem("h_updated"), 1)
            dve.wait_ge(sem("y_gated"), 3)
            inverse_root(RS)
            for t in range(3):
                n = ROWS[t]
                v.tensor_scalar(Y[0:n, t, :], Y[0:n, t, :], RS[0:n, t:t + 1], None,
                                ALU.mult).then_inc(sem("y_normed"), 1)
            for t in range(3):
                n = ROWS[t]
                dve.wait_ge(sem("y_turned"), t + 1)
                v.tensor_tensor(mixT[:, 4:8, COL0[t]:COL0[t] + n],
                                PS[:, t, 0:4 * n].rearrange("p (k n) -> p k n", k=4),
                                bc(colp("ssm_out_gain"), 2, n), ALU.mult).then_inc(sem("y_turned_kept"), 1)

            for g in range(2):
                dve.wait_ge(sem("scores_s_ready"), 2 * g + 2)
                if g:
                    dve.wait_ge(sem("probs_turned"), 3)
                step(v.tensor_tensor(SS[:, 0:512], PS[:, 6, :], cst("bias_past")[:, 0:512], ALU.add))
                step(v.tensor_tensor(SS[:, 512:640], PS[:, 7, 0:P], cst("bias_past")[:, 512:640], ALU.add))
                v.tensor_tensor(SS[:, 640:672], PS[:, 7, P:P + NTS], cst(f"bias_new{g}"),
                                ALU.add).then_inc(sem("scores_s_kept"), 1)
                settle()
                dve.wait_ge(sem("scores_s_kept"), g + 1)
                step(v.tensor_reduce(MX[:, 2, g:g + 1], SS, AX.X, ALU.max))
                settle()
                v.tensor_scalar(NMX[:, 2, g:g + 1], MX[:, 2, g:g + 1], -DH ** -0.5, None,
                                ALU.mult).then_inc(sem("max_ready"), 1)
                dve.wait_ge(sem("exp_ready"), 3 + g)
                step(v.reciprocal(RDEN[:, 2, g:g + 1], DEN[:, 2, g:g + 1]))
                settle()
                v.tensor_scalar(SS, SS, RDEN[:, 2, g:g + 1], None, ALU.mult).then_inc(sem("probs_ready"), 1)

            def add_rows(n0, count):
                for t in range(2):
                    for half in range(2):
                        dve.wait_ge(sem("mixed_ready"), n0 + 2 * t + half + 1)
                        x = X[:, t, half * 512:(half + 1) * 512]
                        step(v.tensor_tensor(x, x, PS[:, 2 * t + half, :], ALU.add))
                dve.wait_ge(sem("mixed_ready"), n0 + 5)
                for half in range(2):
                    x = X[0:NTS, 2, half * 512:(half + 1) * 512]
                    ins = v.tensor_tensor(x, PS[32 * half:32 * half + 32, 4, :], x, ALU.add)
                    if not half:
                        step(ins)
                ins.then_inc(sem("residual_ready"), 1)
                dve.wait_ge(sem("residual_ready"), count)
                settle()

            add_rows(0, 1)

            dve.wait_ge(sem("att_s_ready"), 8)
            dve.wait_ge(sem("mem_loaded"), 16)
            norm_rows(MP, (0, 1))
            for t in range(2):
                dve.wait_ge(sem("hm_turned"), t + 1)
                for b in range(2):
                    ins = v.tensor_tensor(HMT[:, 4 * b:4 * b + 4, t * P:(t + 1) * P],
                                          PS[:, 5 + b, :].rearrange("p (k n) -> p k n", k=4),
                                          bc(colp("mem_in_gain")[:, 4 * b:4 * b + 4], 2, P), ALU.mult)
                ins.then_inc(sem("hm_kept"), 1)
            dve.wait_ge(sem("mkv_kept"), 2)
            x = MK.rearrange("p t h d -> p (t h) d")
            head_norm(x, P, 8, MD, None, SMM.rearrange("p h (a d) -> p (h a) d", a=2))
            v.tensor_tensor(x, x, bc(rowp("mem_k_gain"), 1, 8), ALU.mult).then_inc(sem("mk_normed"), 1)

            norm_rows(X, (0, 1, 2))
            keep_columns(3, "norm_mem")
            for t in range(3):
                n = ROWS[t]
                dve.wait_ge(sem("mq_kept"), t + 1)
                head_norm(MQ[0:n, t], n, MH, MD, None, SMM[:, :, 0:MD])
                v.tensor_tensor(MQ[0:n, t], MQ[0:n, t], bc(rowp("mem_q_gain", n), 1, MH),
                                ALU.mult).then_inc(sem("mq_normed"), 1)

            def memory_max(i, src, cols):
                step(v.tensor_reduce(MX[:, 0, cols], src, AX.X, ALU.max))
                settle()
                v.tensor_scalar(NMX[:, 0, cols], MX[:, 0, cols], -MD ** -0.5, None,
                                ALU.mult).then_inc(sem("max_ready"), 1)

            for i in range(2):
                dve.wait_ge(sem("mscores_ready"), i + 1)
                if i:
                    dve.wait_ge(sem("exp_ready"), 5)
                b0 = (6, 0)[i]
                memory_max(i, PS[:, b0:b0 + 2, :].rearrange("p b (c k) -> p (b c) k", c=2), slice(0, 4))
                dve.wait_ge(sem("exp_ready"), 5 + i)
                step(v.reciprocal(RDEN[:, 0, 0:4], DEN[:, 0, 0:4]))
                settle()
                v.tensor_tensor(SMM, SMM, bc(RDEN[:, 0, 0:4], 2, NM), ALU.mult).then_inc(sem("probs_ready"), 1)
            for g in range(2):
                dve.wait_ge(sem("mscores_s_ready"), 2 * g + 2)
                c = slice(4 + g, 5 + g)
                memory_max(2 + g, PS[:, 6, 0:NM], c)
                dve.wait_ge(sem("exp_ready"), 7 + g)
                step(v.reciprocal(RDEN[:, 0, c], DEN[:, 0, c]))
                settle()
                v.tensor_scalar(SS2, SS2, RDEN[:, 0, c], None, ALU.mult).then_inc(sem("probs_ready"), 1)
            add_rows(5, 2)

            norm_rows(X, (0, 1, 2), rowp("norm_ffn"))
            keep_columns(6)
            step(v.memset(LG, 0.0))
            step(v.memset(POSM, -1.0))
            step(v.memset(GW, 0.0))
            dve.wait_ge(sem("logits_ready"), 1)
            settle()
            br = rowp("b_router")
            step(v.tensor_tensor(LG[:, 0:2, :], PS[:, 5, 0:64].rearrange("p (t e) -> p t e", t=2), bc(br, 1, 2),
                                 ALU.add))
            step(v.tensor_tensor(LG[0:NTS, 2, :], PS[0:NTS, 5, 64:96], br[0:NTS], ALU.add))
            settle()
            for t in range(3):
                step(v.max(TOPV[:, t, :], LG[:, t, :]))
            settle()
            for t in range(3):
                step(v.max_index(top_i[:, t, :], TOPV[:, t, :], LG[:, t, :]))
            step(v.tensor_tensor(TOPW, TOPV[:, :, 0:TOPK], bc(TOPV[:, :, 0], 2, TOPK), ALU.subtract))
            settle()
            v.tensor_copy(TOPF[:, :, :], top_i[:, :, :]).then_inc(sem("top_ready"), 1)
            dve.wait_ge(sem("top_exp_ready"), 1)
            dve.wait_ge(sem("top_ready"), 1)
            step(v.tensor_reduce(TS[:, 0:3], TOPW, AX.X, ALU.add))
            settle()
            step(v.reciprocal(TS[:, 3:6], TS[:, 0:3]))
            settle()
            step(v.tensor_tensor(TOPW, TOPW, bc(TS[:, 3:6], 2, TOPK), ALU.mult))
            iota = bc(bc(cst("iota32"), 1, TOPK), 1, 3)
            step(v.tensor_tensor(OH4, iota, bc(TOPF[:, :, 0:TOPK], 3, NE), ALU.is_equal))
            settle()
            v.tensor_reduce(MSK, OH4.rearrange("p t j e -> p t e j"), AX.X, ALU.add).then_inc(sem("routed"), 1)
            dve.wait_ge(sem("routed"), 1)
            step(v.tensor_tensor(OH4, OH4, bc(TOPW, 3, NE), ALU.mult))
            settle()
            v.tensor_reduce(GW[:, 0:NE, :].rearrange("p e t -> p t e"), OH4.rearrange("p t j e -> p t e j"), AX.X,
                            ALU.add).then_inc(sem("gw_ready"), 1)
            dve.wait_ge(sem("ranks_ready"), 1)
            pos = POSM[:, 0:NE, :].rearrange("p e t -> p t e")
            step(v.scalar_tensor_tensor(pos[:, 0:2], MSK[:, 0:2], -1024.0,
                                        PS[:, 6, 0:64].rearrange("p (t e) -> p t e", t=2), ALU.mult, ALU.add))
            step(v.scalar_tensor_tensor(pos[0:NTS, 2], MSK[0:NTS, 2], -1024.0, PS[0:NTS, 6, 64:96], ALU.mult, ALU.add))
            step(v.tensor_reduce(CNT[:, 0:1], PS[:, 6, 96:128], AX.X, ALU.max))
            settle()
            step(v.tensor_scalar(POSM[:, 0:NE, :], POSM[:, 0:NE, :], 1024.0, None, ALU.add))
            step(v.tensor_scalar(TS[:, 0:NPASS_MAX - 1], cst("thr"), CNT[:, 0:1], None, ALU.is_lt))
            settle()
            step(v.tensor_reduce(NPF, TS[:, 0:NPASS_MAX - 1], AX.X, ALU.add))
            settle()
            v.tensor_scalar(npass_i[:, 0:1], NPF, 1.0, None, ALU.add).then_inc(sem("npass_ready"), 1)
            v.memset(YB, 0.0).then_inc(sem("y_rows_ready"), 1)
            v.memset(SW, 0.0).then_inc(sem("sw_ready"), 1)
            v.memset(AC, 0.0).then_inc(sem("act_ready"), 1)
            dve.wait_ge(sem("gathered"), 1)
            for t in range(3):
                for half in range(2):
                    n = ROWS[t]
                    x = X[0:n, t, half * 512:(half + 1) * 512]
                    ins = v.tensor_tensor(x, x, PS[0:n, 2 * t + half, :], ALU.add)
                    if 2 * t + half < 5:
                        step(ins)
            ins.then_inc(sem("scatter_added"), 1)
            settle()
            dve.wait_ge(sem("scatter_added"), 1)
            dve.wait_ge(sem("gw_ready"), 1)

            def select(n, e):
                dve.wait_ge(sem("gathered"), n + 1)
                v.tensor_tensor(SEL, bc(cst("iota64"), 1, 3), bc(POSM[:, bass.ds(e, 1), :].rearrange("p a t -> p (a t)"), 2, SLOTS),
                                ALU.is_equal).then_inc(sem("sel_ready"), 1)

            def expert_row(e):
                v.tensor_scalar(EROW[0:NE, :], cst("ones")[0:NE, 0:SLOTS], erow_of[0:NE, bass.ds(e, 1)], None,
                                ALU.mult).then_inc(sem("erow_ready"), 1)

            erow_of = CN[:, const_at["ident"][1]:const_at["ident"][1] + P]
            dve.wait_ge(sem("npass_ready"), 1)
            npass = dve.value_load(npass_i[0:1, 0:1], min_val=1, max_val=NPASS_MAX)
            with dve.Fori(0, npass) as r:
                dve.wait_ge(sem("sw_ready"), r * NE + 1)
                v.memset(SW, 0.0).then_inc(sem("sw_cleared"), 1)
                select(r * (NE + 1), 0)
                expert_row(0)
                with dve.Fori(0, NE) as e:
                    it = r * NE + e
                    q = r * (NE + 1) + e
                    select(q + 1, e + 1)
                    dve.wait_ge(sem("sw_turned"), it + 1)
                    posb = bc(bc(POSM[:, bass.ds(e, 1), :].rearrange("p a t -> p (a t)"), 2, 2), 3, SLOTS)
                    gwb = bc(bc(GW[:, bass.ds(e, 1), :].rearrange("p a t -> p (a t)"), 2, 2), 3, SLOTS)
                    v.tensor_tensor(SELW, bc(bc(cst("iota64"), 1, 2), 1, 3), posb,
                                    ALU.is_equal).then_inc(sem("selw_compared"), 1)
                    dve.wait_ge(sem("selw_compared"), it + 1)
                    v.tensor_tensor(SELW, SELW, gwb, ALU.mult).then_inc(sem("selw_ready"), 1)
                    dve.wait_ge(sem("gate_up_ready"), it + 1)
                    gu = PS[:, 0:2, :].rearrange("p b (c two) -> p b c two", two=2)
                    v.tensor_scalar(G1, gu[:, :, :, 0], 7.0, None, ALU.min).then_inc(sem("gate_ready"), 1)
                    v.tensor_scalar(U1, gu[:, :, :, 1], 7.0, -7.0, ALU.min, ALU.max).then_inc(sem("up_ready"), 1)
                    dve.wait_ge(sem("sigmoid_ready"), it + 1)
                    v.tensor_tensor(SG, SG, G1, ALU.mult).then_inc(sem("gated"), 1)
                    dve.wait_ge(sem("gated"), it + 1)
                    dve.wait_ge(sem("up_ready"), it + 1)
                    v.scalar_tensor_tensor(AC, U1.rearrange("p b c -> p (b c)"), 1.0, SG.rearrange("p b c -> p (b c)"),
                                           ALU.add, ALU.mult).then_inc(sem("act_ready"), 1)
                    expert_row(e + 1)
                    for t in range(3):
                        n = ROWS[t]
                        dve.wait_ge(sem("scattered"), 3 * q + t + 1)
                        x = X[0:n, t, :].rearrange("p (b c) -> p b c", b=2)
                        v.tensor_tensor(x, x, PS[0:n, 6:8, :], ALU.add).then_inc(sem("scatter_added"), 1)
                last = 3 * (r * (NE + 1) + NE)
                for t in range(3):
                    n = ROWS[t]
                    dve.wait_ge(sem("scattered"), last + t + 1)
                    x = X[0:n, t, :].rearrange("p (b c) -> p b c", b=2)
                    v.tensor_tensor(x, x, PS[0:n, 6:8, :], ALU.add).then_inc(sem("scatter_added"), 1)
                dve.wait_ge(sem("gathered"), (r + 1) * (NE + 1) + 1)
                v.tensor_scalar(POSM, POSM, float(SLOTS), None, ALU.subtract).then_inc(sem("slots_moved"), 1)
                dve.wait_ge(sem("slots_moved"), r + 1)
                dve.wait_ge(sem("scatter_added"), last + 4)
            v.memset(OH4[:, 0, 0, 0:1], 0.0).then_inc(sem("x_final"), 1)

        @block.scalar
        def _(act):
            s = nc.scalar

            heads_rooted = [0]

            def root(dst, sums, width):
                s.activation(dst, sums, ACT.Sqrt, scale=1.0 / width, bias=cst("eps")[0:dst.shape[0], :]
                             ).then_inc(sem("roots_ready"), 1)

            def root_heads(rows, heads, width):
                heads_rooted[0] += 1
                act.wait_ge(sem("head_squares_ready"), heads_rooted[0])
                root(SSH[0:rows, 0:heads], SSH[0:rows, 0:heads], width)

            def square_rows(src, tiles, scratch, n0):
                for t in tiles:
                    n = ROWS[t]
                    s.activation(scratch[0:n, t, :], src[0:n, t, :], ACT.Square,
                                 accum_out=SSQ[0:n, t:t + 1]).then_inc(sem("rows_squared"), 1)
                act.wait_ge(sem("rows_squared"), n0 + len(tiles))
                root(RS[:, 0:len(tiles)], SSQ[:, 0:len(tiles)], D)

            def square_y(t):
                n = ROWS[t]
                s.activation(Z[0:n, t, :], Y[0:n, t, :], ACT.Square,
                             accum_out=SSQ[0:n, t:t + 1]).then_inc(sem("y_squared"), 1)

            act.wait_ge(sem("dve_steps"), 1)
            act.wait_ge(sem("x_loaded"), 32)
            act.wait_ge(sem("consts_loaded"), 16)
            square_rows(X, (0, 1, 2), XN, 0)
            act.wait_ge(sem("conv_state_turned"), 1)
            s.copy(XS[:, :, :, 0:3], PS[:, 5, 0:192].rearrange("p (m b i) -> p m b i", m=8,
                                                               b=NB)).then_inc(sem("conv_state_kept"), 1)
            act.wait_ge(sem("params_loaded"), 32)
            act.wait_ge(sem("small_cleared"), 1)
            s.activation(AEX, rowp("a_log"), ACT.Exp)
            for i in range(8):
                g, t = i // 2, i % 2
                act.wait_ge(sem("proj_ready"), i + 1)
                dst = (QK[:, t, 0].rearrange("p h d -> p (h d)"), QK[:, t, 1].rearrange("p h d -> p (h d)"),
                       V[:, t, :], Z[:, t, :])[g]
                s.copy(dst, PS[:, i, :]).then_inc(sem("proj_kept"), 1)
                if i in (5, 7):
                    root_heads(P, 2 * AH, DH)
            act.wait_ge(sem("proj_ready"), 9)
            s.copy(QKS[0:64].rearrange("p h d -> p (h d)"), PS[0:64, 0, :]).then_inc(sem("proj_kept"), 1)
            s.copy(V[0:NTS, 2, :], PS[64:96, 0, :]).then_inc(sem("proj_kept"), 1)
            s.copy(Z[0:NTS, 2, :], PS[96:128, 0, :]).then_inc(sem("proj_kept"), 1)
            for m in range(8):
                bank = (2 + m) % 8
                act.wait_ge(sem("xbc_ready"), m + 1)
                s.copy(XP[:, m, 3:3 + SEQ], PS[:, bank, 0:SEQ]).then_inc(sem("xbc_kept"), 1)
                s.copy(XS[:, m, :, 3:3 + NS], PS[:, bank, SEQ:NTOK].rearrange("p (b t) -> p b t", b=NB)
                       ).then_inc(sem("xbc_kept"), 1)
                if m == 1:
                    root_heads(64, AH, DH)
            act.wait_ge(sem("dt_abs_ready"), 1)
            s.activation(DT1[:, :, :], DT1[:, :, :], ACT.Exp, scale=-1.0).then_inc(sem("dt_exp_ready"), 1)
            act.wait_ge(sem("dt_exp_ready"), 1)
            s.activation(DT1[:, :, :], DT1[:, :, :], ACT.Ln, bias=cst("ones")[:, 0:1]).then_inc(sem("dt_log_ready"), 1)
            act.wait_ge(sem("tail_rows_ready"), 1)
            for j in range(2):
                s.copy(CONVO[0:27, 512 * j:512 * j + 512], PS[0:27, 6 + j, :]).then_inc(sem("tail_rows_kept"), 1)
            for n in range(4):
                t, j = n // 2, n % 2
                act.wait_ge(sem("qk_turned"), n + 1)
                s.copy((qT, kT)[j][:, :, t * P:(t + 1) * P],
                       PS[:, n, :].rearrange("p (c n) -> p c n", c=4)).then_inc(sem("qk_kept"), 1)
            act.wait_ge(sem("qk_turned"), 5)
            act.wait_ge(sem("pool_cleared"), 2)
            s.copy(kTs, PS[:, 5, 0:P].rearrange("p (c n) -> p c n", c=4)).then_inc(sem("qk_kept"), 1)
            for e in range(2):
                r = slice(64 * e, 64 * e + 64)
                dst = arena[r, 4 * e:4 * e + 1056].rearrange("p (c x) -> p c x", c=4)[:, :, 0:256]
                dst = dst.rearrange("p c (b u) -> p c b u", b=NB)[:, :, :, 0:NS]
                s.copy(dst, PS[r, 4, 0:P].rearrange("p (c b t) -> p c b t", c=4, b=NB)).then_inc(sem("qk_kept"), 1)
            act.wait_ge(sem("conv_ready"), 1)
            for m in range(8):
                s.activation(UT[:, m, :], UT[:, m, :], ACT.Silu,
                             bias=colp("conv_b")[:, m:m + 1]).then_inc(sem("conv_silu_ready"), 1)
            for t in range(3):
                n = ROWS[t]
                act.wait_ge(sem("proj_kept"), 11)
                s.activation(Z[0:n, t, :], Z[0:n, t, :], ACT.Silu).then_inc(sem("z_silu_ready"), 1)
            for i in range(2):
                nk = (i + 1) * P
                act.wait_ge(sem("max_ready"), i + 1)
                for h in range(8):
                    ins = s.activation(SCO[i][:, h, :], SCO[i][:, h, :], ACT.Exp, bias=NMX[:, i, h:h + 1],
                                       scale=DH ** -0.5, accum_out=DEN[:, i, h:h + 1])
                ins.then_inc(sem("exp_ready"), 1)
            act.wait_ge(sem("tails_ready"), 1)
            for t in range(3):
                n = ROWS[t]
                b = (4, 6, 0)[t]
                act.wait_ge(sem("xb_turned"), t + 1)
                s.copy(XB[0:n, t, 0:512], PS[0:n, b, :])
                s.copy(XB[0:n, t, 512:768], PS[0:n, b + 1, 0:256]).then_inc(sem("xb_kept"), 1)
            act.wait_ge(sem("conv_stored"), 32)
            for i in range(2):
                act.wait_ge(sem("probs_turned"), i + 1)
                banks = (2, 3, 5, 6)
                for j in range(i + 1):
                    for c in range(2):
                        ins = s.copy(PT[:, j, 4 * c:4 * c + 4, :],
                                     PS[:, banks[2 * j + c], :].rearrange("p (h q) -> p h q", h=4))
                ins.then_inc(sem("probs_kept"), 1)
                act.wait_ge(sem("att_ready"), i + 1)
                s.copy(mixT[:, 0:4, i * P:(i + 1) * P],
                       PS[:, (4, 7)[i], :].rearrange("p (c q) -> p c q", c=4)).then_inc(sem("att_kept"), 1)
            act.wait_ge(sem("acum_ready"), 1)
            s.activation(TOE, DT1, ACT.Exp)
            s.activation(EAC, ACU, ACT.Exp)
            s.activation(DEC1, PS[:, 0, 40:48], ACT.Exp)
            s.activation(DECS, PS[:, 0, 64:96].rearrange("p (c b) -> p c b", c=4),
                         ACT.Exp).then_inc(sem("ssd_exps_ready"), 1)
            H0T = slot("scratch", NB, 512)
            act.wait_ge(sem("proj_ready"), 9)
            for b in range(NB):
                act.wait_ge(sem("h0_turned"), b + 1)
                s.copy(H0T[:, b, :], PS[:, 1 + b % 2, :]).then_inc(sem("h0t_kept"), 1)
            for t in range(3):
                n = ROWS[t]
                act.wait_ge(sem("seg_ready"), t + 1)
                s.activation(SEG[0:n, :, 0:n], SEG[0:n, :, 0:n], ACT.Exp).then_inc(sem("seg_exp_ready"), 1)
                if t:
                    act.wait_ge(sem("y_gated"), t)
                    square_y(t - 1)
            act.wait_ge(sem("y_gated"), 3)
            square_y(2)
            act.wait_ge(sem("y_squared"), 3)
            root(RS, SSQ, 512)
            act.wait_ge(sem("state_rows_ready"), 1)
            s.copy(HOUT, PS[:, 2, :].rearrange("p (c n) -> p c n", c=4)).then_inc(sem("state_rows_kept"), 1)
            act.wait_ge(sem("h_added"), 8)
            for g in range(2):
                for n in range(20 * g, 20 * g + 20):
                    b, j = n // 5 % 2, n % 5
                    act.wait_ge(sem("kt_turned"), n + 1)
                    s.copy(KTB[:, b, :, j * P:(j + 1) * P],
                           PS[:, 3 + n % 3, :].rearrange("p (c k) -> p c k", c=4)).then_inc(sem("kt_kept"), 1)
                act.wait_ge(sem("max_ready"), 3 + g)
                s.activation(SS, SS, ACT.Exp, bias=NMX[:, 2, g:g + 1], scale=DH ** -0.5,
                             accum_out=DEN[:, 2, g:g + 1]).then_inc(sem("exp_ready"), 1)
                act.wait_ge(sem("probs_turned"), 3 + g)
                s.copy(PTS[:, 0:4, :], PS[:, 3, :].rearrange("p (j r) -> p j r", j=4))
                s.copy(PTS[:, 4, :], PS[:, 4, 0:P]).then_inc(sem("probs_s_kept"), 1)
                s.copy(PTS[0:NTS, 5, :], PS[0:NTS, 4, P:2 * P]).then_inc(sem("probs_s_kept"), 1)
            act.wait_ge(sem("att_s_ready"), 8)
            for e in range(2):
                r = slice(64 * e, 64 * e + 64)
                src = PS[r, 0, 0:256].rearrange("p (b c u) -> p c b u", b=NB, c=4)[:, :, :, 4 * e:4 * e + 4]
                ins = s.copy(mixT[r, 0:4, SEQ:NTOK].rearrange("p c (b t) -> p c b t", b=NB), src)
            ins.then_inc(sem("mix_ready"), 1)
            act.wait_ge(sem("mem_loaded"), 16)
            square_rows(MP, (0, 1), XN, 3)
            for n in range(4):
                act.wait_ge(sem("mkv_ready"), n + 1)
                dst = MK[:, n % 2].rearrange("p h d -> p (h d)") if n < 2 else MV[:, n % 2, :]
                s.copy(dst, PS[:, (5, 6, 7, 5)[n], :]).then_inc(sem("mkv_kept"), 1)
            root_heads(P, 8, MD)
            act.wait_ge(sem("residual_ready"), 1)
            act.wait_ge(sem("hm_turned"), 2)
            square_rows(X, (0, 1, 2), XN, 5)
            for t in range(2):
                act.wait_ge(sem("mk_turned"), t + 1)
                s.copy(MKT[:, :, t * P:(t + 1) * P],
                       PS[:, 6 + t, :].rearrange("p (h n) -> p h n", h=MH)).then_inc(sem("mk_turned_kept"), 1)
            for t in range(3):
                n = ROWS[t]
                act.wait_ge(sem("mq_ready"), t + 1)
                s.copy(MQ[0:n, t].rearrange("p h d -> p (h d)"), PS[0:n, t, :]).then_inc(sem("mq_kept"), 1)
            for t in range(3):
                root_heads(ROWS[t], MH, MD)
            for t in range(2):
                act.wait_ge(sem("mq_turned"), t + 1)
                s.copy(QMT[:, :, t * P:(t + 1) * P],
                       PS[:, 3 + t, :].rearrange("p (h n) -> p h n", h=MH)).then_inc(sem("mq_turned_kept"), 1)
            act.wait_ge(sem("mq_turned"), 3)
            act.wait_ge(sem("pool_cleared"), 4)
            for h in range(MH):
                s.copy(QMB[:, h, :, 4 * h:4 * h + 4],
                       PS[:, 5, h * NTS:(h + 1) * NTS].rearrange("p (b t) -> p b t", b=NB)
                       ).then_inc(sem("mq_turned_kept"), 1)
            for i in range(2):
                act.wait_ge(sem("max_ready"), 5 + i)
                if i:
                    act.wait_ge(sem("probs_turned"), 5)
                for h in range(MH):
                    ins = s.activation(SMM[:, h, :], PS[:, (6, 0)[i] + h // 2, h % 2 * 256:(h % 2 + 1) * 256], ACT.Exp,
                                       bias=NMX[:, 0, h:h + 1], scale=MD ** -0.5, accum_out=DEN[:, 0, h:h + 1])
                ins.then_inc(sem("exp_ready"), 1)
                act.wait_ge(sem("probs_turned"), 5 + i)
                for j in range(2):
                    s.copy(PTM[:, j], PS[:, 2 + 2 * i + j, :].rearrange("p (h q) -> p h q", h=MH)
                           ).then_inc(sem("mprobs_kept"), 1)
                act.wait_ge(sem("mo_ready"), i + 1)
                s.copy(OT[:, :, i * P:(i + 1) * P],
                       PS[:, 2 + 2 * i, :].rearrange("p (h q) -> p h q", h=MH)).then_inc(sem("mo_kept"), 1)
            for g in range(2):
                for n in range(8 * g, 8 * g + 8):
                    b, j = n // 2 % 2, n % 2
                    act.wait_ge(sem("ktm_turned"), n + 1)
                    s.copy(KTM[:, b, :, j * P:(j + 1) * P],
                           PS[:, (3, 5)[n % 2], :].rearrange("p (h k) -> p h k", h=MH)).then_inc(sem("ktm_kept"), 1)
                act.wait_ge(sem("max_ready"), 7 + g)
                s.activation(SS2, PS[:, 6, 0:NM], ACT.Exp, bias=NMX[:, 0, 4 + g:5 + g], scale=MD ** -0.5,
                             accum_out=DEN[:, 0, 4 + g:5 + g]).then_inc(sem("exp_ready"), 1)
                act.wait_ge(sem("probs_turned"), 7 + g)
                s.copy(PTM[:, 0, 0:2, :], PS[:, 7, 0:256].rearrange("p (j r) -> p j r", j=2)
                       ).then_inc(sem("mprobs_kept"), 1)
            act.wait_ge(sem("mo_ready"), 4)
            s.copy(OT[:, :, SEQ:NTOK], PS[:, 4, 0:P].rearrange("p (h n) -> p h n", h=MH)).then_inc(sem("mo_kept"), 1)
            act.wait_ge(sem("residual_ready"), 2)
            act.wait_ge(sem("rows_turned"), 6)
            square_rows(X, (0, 1, 2), XN, 8)
            act.wait_ge(sem("top_ready"), 1)
            s.activation(TOPW, TOPW, ACT.Exp).then_inc(sem("top_exp_ready"), 1)
            act.wait_ge(sem("sw_turned"), 1)
            s.copy(GWT[0:NE, :], PS[0:NE, 7, 0:NTOK]).then_inc(sem("gwt_kept"), 1)

            def keep_gathered(n):
                act.wait_ge(sem("gathered"), n + 2)
                s.copy(XT, PS[:, 2, :].rearrange("p (k s) -> p k s", k=KT)).then_inc(sem("xt_ready"), 1)

            act.wait_ge(sem("npass_ready"), 1)
            npass = act.value_load(npass_i[0:1, 0:1], min_val=1, max_val=NPASS_MAX)
            with act.Fori(0, npass) as r:
                keep_gathered(r * (NE + 1))
                with act.Fori(0, NE) as e:
                    it = r * NE + e
                    q = r * (NE + 1) + e
                    act.wait_ge(sem("gate_ready"), it + 1)
                    s.activation(SG, G1, ACT.Sigmoid, scale=1.702).then_inc(sem("sigmoid_ready"), 1)
                    keep_gathered(q + 1)
                    act.wait_ge(sem("act_turned"), it + 1)
                    s.copy(AT, PS[:, 4, :].rearrange("p (c n) -> p c n", c=4)).then_inc(sem("at_ready"), 1)
                    act.wait_ge(sem("down_ready"), it + 1)
                    s.copy(YB, PS[:, 5, :]).then_inc(sem("y_rows_ready"), 1)
                    act.wait_ge(sem("sw_turned"), it + 2)
                    s.copy(SW[:, 0:NTOK], PS[:, 3, 0:NTOK]).then_inc(sem("sw_ready"), 1)

        @block.gpsimd
        def _(pool):
            g_ = nc.gpsimd

            def bc(ap, axis, n):
                ap = ap.unsqueeze(axis)
                shape = list(ap.shape)
                shape[axis] = n
                return ap.to_broadcast(shape)

            g_.memset(XP[:, :, 0:3], 0.0).then_inc(sem("pool_cleared"), 1)
            pool.wait_ge(sem("xbc_ready"), 8)
            g_.memset(arena[:, 0:1024], 0.0).then_inc(sem("pool_cleared"), 1)
            pool.wait_ge(sem("qk_normed"), 3)
            pool.dma_start(o["win_k_prompt"][0, 0].rearrange("(t p) h d -> p t (h d)", p=P),
                           QK[:, :, 1].rearrange("p t h d -> p t (h d)")).then_inc(sem("window_stored"), 16)
            pool.dma_start(o["win_v_prompt"][0, 0].rearrange("(t p) h d -> p t (h d)", p=P),
                           V[:, 0:2, :]).then_inc(sem("window_stored"), 16)
            pool.dma_start(o["win_k_sample"].rearrange("l b t h d -> (l b t) (h d)"),
                           QKS[32:64].rearrange("p h d -> p (h d)")).then_inc(sem("window_stored"), 16)
            pool.dma_start(o["win_v_sample"].rearrange("l b t h d -> (l b t) (h d)"),
                           V[0:NTS, 2, :]).then_inc(sem("window_stored"), 16)
            pool.wait_ge(sem("xbc_kept"), 16)
            for m in range(8):
                g_.tensor_copy(TAIL[:, m, 0:24].rearrange("p (b i) -> p b i", b=NB), XS[:, m, :, NS:NS + 3])
            g_.tensor_copy(TAIL[:, :, 24:27], XP[:, :, SEQ:SEQ + 3]).then_inc(sem("tails_ready"), 1)
            pool.wait_ge(sem("tail_rows_kept"), 2)
            pool.dma_start(o["conv_sample"].rearrange("l b i c -> (l b i) c"), CONVO[0:24]
                           ).then_inc(sem("conv_stored"), 16)
            pool.dma_start(o["conv_prompt"].rearrange("l b i c -> (l b i) c"), CONVO[24:27]
                           ).then_inc(sem("conv_stored"), 16)
            pool.wait_ge(sem("window_stored"), 64)
            pool.wait_ge(sem("qk_turned"), 5)
            pool.wait_ge(sem("dta_ready"), 1)
            g_.tensor_copy(DREP[0:NTS], bc(DTA[0:NTS, 2, :], 2, DH)).then_inc(sem("drep_ready"), 1)
            pool.wait_ge(sem("probs_turned"), 2)
            g_.memset(arena[:, 4736:5248], 0.0).then_inc(sem("pool_cleared"), 1)
            pool.wait_ge(sem("pool_cleared"), 3)
            pool.wait_ge(sem("conv_silu_ready"), 8)
            for g in range(2):
                dst = arena[:, 4736 + 256 * g:4736 + 256 * g + 288].rearrange("p (b x) -> p b x", x=36)[:, :, 0:NS]
                ins = g_.tensor_copy(dst, UT[:, 6 + g, SEQ:NTOK].rearrange("p (b t) -> p b t", b=NB))
            ins.then_inc(sem("cm_ready"), 1)
            pool.wait_ge(sem("cumulated"), 1)
            for t in range(3):
                n = ROWS[t]
                pool.wait_ge(sem("arow_ready"), t)
                tri = cst("tri") if t < 2 else cst("tri_s")
                g_.tensor_tensor(DTRI[0:n, :, 0:n], bc(DTA[0:n, t, :], 2, n), bc(tri, 1, SH),
                                 ALU.mult).then_inc(sem("dtri_ready"), 1)
                if t == 1:
                    pool.wait_ge(sem("h0_turned"), NB)
                    pool.wait_ge(sem("ssd_exps_ready"), 1)
                    H0 = slot("h0", NB, 4, NST)
                    for p in range(4):
                        g_.tensor_tensor(H0[:, :, p, :], H0[:, :, p, :], bc(DECS[:, p, :], 2, NST),
                                         ALU.mult).then_inc(sem("h0_scaled"), 1)
            pool.wait_ge(sem("st_ready"), 3)
            pool.wait_ge(sem("y_carried_ready"), 1)
            pool.wait_ge(sem("xb_kept"), 3)
            for g in range(2):
                ins = g_.tensor_tensor(BNM[0:NTS, g], bc(XB[0:NTS, 2, 512 + g * P:512 + (g + 1) * P], 1, NB),
                                       bc(cst("bsel"), 2, P), ALU.mult)
            ins.then_inc(sem("bnm_ready"), 1)
            pool.wait_ge(sem("state_rows_kept"), 1)
            pool.dma_start(o["ssm_prompt"][0, 0].rearrange("(c h) d n -> (h d) c n", h=2), HOUT
                           ).then_inc(sem("prompt_state_stored"), 16)
            pool.wait_ge(sem("h_updated"), 8)
            H0 = slot("h0", NB * 4, NST)
            pool.dma_start(o["ssm_sample"][0].rearrange("b (c h) d n -> (h d) (b c) n", h=2), H0
                           ).then_inc(sem("states_stored"), 16)
            pool.dma_start(MP, a["mem_prompt"][0].rearrange("(t p) d -> p t d", p=P)).then_inc(sem("mem_loaded"), 16)
            pool.wait_ge(sem("att_s_ready"), 8)
            g_.memset(QMB, 0.0).then_inc(sem("pool_cleared"), 1)
            pool.wait_ge(sem("mkv_kept"), 4)
            pool.dma_start(o["mem_v_prompt"][0, 0].rearrange("(t p) h d -> p t (h d)", p=P), MV
                           ).then_inc(sem("mem_stored"), 16)
            pool.wait_ge(sem("mk_normed"), 1)
            pool.dma_start(o["mem_k_prompt"][0, 0].rearrange("(t p) h d -> p t (h d)", p=P),
                           MK.rearrange("p t h d -> p t (h d)")).then_inc(sem("mem_stored"), 16)
            pool.wait_ge(sem("mk_turned"), 2)
            pool.wait_ge(sem("mem_stored"), 32)
            pool.dma_start(BGU[0:NE], a["b_gate_up"].rearrange("l e f -> (l e) f")
                           ).then_inc(sem("expert_biases_loaded"), 16)
            pool.dma_start(BD[0:NE], a["b_down"].rearrange("l e f -> (l e) f")
                           ).then_inc(sem("expert_biases_loaded"), 16)
            pool.wait_ge(sem("prompt_state_stored"), 16)

        @block.sync
        def _(sp):
            sp.dma_start(X[:, 0:2, :], a["x_prompt"][0].rearrange("(t p) d -> p t d", p=P)).then_inc(sem("x_loaded"), 16)
            sp.dma_start(X[0:NTS, 2, :], a["x_sample"].rearrange("b t d -> (b t) d")).then_inc(sem("x_loaded"), 16)
            sp.dma_start(CN[:, :], a["consts"]).then_inc(sem("consts_loaded"), 16)
            sp.dma_start(RP[:, :], a["row_params"].to_broadcast([P, NR])).then_inc(sem("params_loaded"), 16)
            sp.dma_start(CP[:, :], a["col_params"]).then_inc(sem("params_loaded"), 16)
            sp.dma_start(SC[0:24], a["state_conv"].rearrange("l b i c -> (l b i) c")).then_inc(sem("state_conv_loaded"), 16)
            w_in = a["w_in"][0].rearrange("(k p) n -> p k n", p=P)
            in_col = dict(q=0, k=512, v=1024, z=1536, xbc0=2056, xbc1=2568)

            def load(name):
                u = U[name]
                if name in in_col:
                    dst, src = slot(name, KT, 512), w_in[:, :, in_col[name]:in_col[name] + 512]
                elif name == "h0":
                    dst, src = slot(name, NB * 4, NST), a["state_ssm"][0].rearrange("b (c h) d n -> (h d) (b c) n", h=2)
                elif name[0] in "KV":
                    cache = a["cache_win_k" if name[0] == "K" else "cache_win_v"]
                    c = cache[0, int(name[1:])].rearrange("s h d -> s (h d)")
                    old = c[0:512].rearrange("(i r) d -> i r d", r=16)
                    s_old = slot(name, 5, 512)[:, 0, :]
                    sp.dma_start(s_old, old[:, 0:4, :]).then_inc(sem(f"slot{u % RING}_loaded"), 16)
                    dst = slot(name, 5 * 512)[:, 512:2560]
                    src = c[PAST - 512:PAST].rearrange("(p j) d -> p (j d)", j=4)
                    sp.dma_start(dst, src).then_inc(sem(f"slot{u % RING}_loaded"), 16)
                    return
                elif name.startswith("wout"):
                    half = int(name[4])
                    dst = slot(name, KT, 512)
                    src = a["w_out"][0].rearrange("(k p) n -> p k n", p=P)[:, :, half * 512:(half + 1) * 512]
                elif name in ("wmk", "wmv", "wmq"):
                    dst = slot(name, KT, 512)
                    src = a["w_mem_" + name[2]][0].rearrange("(k p) n -> p k n", p=P)
                elif name == "wmo":
                    dst, src = slot(name, MH, D), a["w_mem_o"][0].rearrange("(k p) n -> p k n", p=P)
                sp.dma_start(dst, src).then_inc(sem(f"slot{u % RING}_loaded"), 16)

            freed = dict(q=("proj_ready", 9), k=("proj_ready", 9), v=("proj_ready", 9), z=("proj_ready", 9),
                         xbc0=("xbc_ready", 4), xbc1=("xbc_ready", 8), h0=("states_stored", 16),
                         scratch=("y_carried_ready", 2), wout0=("mixed_ready", 5), wout1=("mixed_ready", 5),
                         wmk=("mkv_ready", 2), wmv=("mkv_ready", 4), wmq=("mq_ready", 3), mem0=("mo_ready", 3),
                         mem1=("mo_ready", 3), mem2=("mo_ready", 4), mem3=("mo_ready", 4), wmo=("mixed_ready", 10))
            for b in range(NB):
                freed[f"K{b}"] = ("kt_turned", 5 * b + 5)
                freed[f"V{b}"] = ("att_s_ready", b + 1)

            def wait_freed(u):
                name = UNITS[u - RING]
                sp.wait_ge(sem(freed[name][0]), freed[name][1])

            for u, name in enumerate(UNITS):
                if name in ("scratch", "pad"):
                    continue
                if u >= RING:
                    wait_freed(u)
                if name.startswith("mem"):
                    i = int(name[3:])
                    M = slot(name, 2, 4, MH * MD)
                    for j, kv in enumerate("kv"):
                        src = a["cache_mem_" + kv][0, 2 * i:2 * i + 2].rearrange("b (t p) h d -> p (b t) (h d)", p=P)
                        sp.dma_start(M[:, j], src
                                     ).then_inc(sem(f"slot{u % RING}_loaded"), 16)
                else:
                    load(name)
                if u == 3:
                    sp.dma_start(WDT[:, :, :], w_in[:, :, 2048:2056]).then_inc(sem("dt_weights_loaded"), 16)
                if u == 12:
                    sp.dma_start(WR[:, :, :], a["w_router"][0].rearrange("(k p) n -> p k n", p=P)
                                 ).then_inc(sem("router_loaded"), 16)
            gu = a["w_gate_up"][0].rearrange("e (j t p) n -> e j p t n", p=P, t=2)
            dn = a["w_down"][0].rearrange("e (j t p) n -> e j p t n", p=P, t=4)

            def load_expert(j, e):
                src = gu[e, j] if j < 4 else dn[e, j - 4]
                dst = slot(j, 2, 2 * FF) if j < 4 else slot(j, 4, D)
                if not isinstance(e, int):
                    src = (gu[bass.ds(e, 1), j] if j < 4 else dn[bass.ds(e, 1), j - 4]).rearrange("a p t n -> (a p) t n")
                sp.dma_start(dst, src).then_inc(sem(f"slot{j}_loaded"), 16)

            base = len(UNITS) - RING
            for j in range(RING):
                name = UNITS[base + j]
                if name == "pad":
                    name = UNITS[base + j - RING]
                sp.wait_ge(sem(freed[name][0]), freed[name][1])
                load_expert(j, 0)

            def next_expert(used, e):
                for j in range(RING):
                    if j == 3:
                        sp.wait_ge(sem("gate_up_ready"), used + 1)
                    elif j == 5:
                        sp.wait_ge(sem("down_ready"), used + 1)
                    else:
                        sp.wait_ge(sem("expert_units_used"), 4 * used + (j + 1 if j < 3 else 4))
                    load_expert(j, e)

            with sp.Fori(1, NE) as e:
                next_expert(e - 1, e)
            npass = sp.value_load(npass_i[0:1, 0:1], min_val=1, max_val=NPASS_MAX)
            with sp.If(npass > 1):
                with sp.Fori(1, npass) as r:
                    with sp.Fori(0, NE) as e:
                        next_expert(r * NE + e - 1, e)
            sp.wait_ge(sem("x_final"), 1)
            sp.dma_start(o["y_prompt"][0].rearrange("(t p) d -> p t d", p=P), X[:, 0:2, :]).then_inc(sem("rows_stored"), 16)
            sp.dma_start(o["y_sample"].rearrange("b t d -> (b t) d"), X[0:NTS, 2, :]).then_inc(sem("rows_stored"), 16)
            sp.wait_ge(sem("rows_stored"), 32)
            sp.wait_ge(sem("prompt_state_stored"), 16)
            sp.wait_ge(sem("window_stored"), 64)
            sp.wait_ge(sem("conv_stored"), 32)
            sp.wait_ge(sem("states_stored"), 16)
            sp.wait_ge(sem("mem_stored"), 32)


OUTS = [("y_prompt", (1, SEQ, D)), ("y_sample", (NB, NS, D)),
        ("win_k_prompt", (1, 1, SEQ, AH, DH)), ("win_v_prompt", (1, 1, SEQ, AH, DH)),
        ("win_k_sample", (1, NB, NS, AH, DH)), ("win_v_sample", (1, NB, NS, AH, DH)),
        ("conv_prompt", (1, 1, 3, D)), ("conv_sample", (1, NB, 3, D)),
        ("ssm_prompt", (1, 1, SH, DH, NST)), ("ssm_sample", (1, NB, SH, DH, NST)),
        ("mem_k_prompt", (1, 1, NM, MH, MD)), ("mem_v_prompt", (1, 1, NM, MH, MD))]
WHOLE = ["x_prompt", "x_sample", "cache_win_k", "cache_win_v", "state_conv", "state_ssm", "cache_mem_k",
         "cache_mem_v", "mem_prompt", "w_in", "w_out", "w_mem_q", "w_mem_k", "w_mem_v", "w_mem_o", "w_router",
         "w_gate_up", "b_gate_up", "w_down", "b_down"]


def lay_out(inputs):
    arrays = {n: np.ascontiguousarray(inputs[n]) for n in WHOLE}
    arrays["consts"] = packed_constants()[1]
    row = [np.asarray(inputs[n]).reshape(1, -1) for n, _ in ROWP]
    arrays["row_params"] = np.ascontiguousarray(np.concatenate(row, 1))

    def columns(x):
        return np.asarray(x).reshape(-1, P).T

    gains = np.concatenate([np.tile(np.asarray(inputs["q_gain"]).reshape(1, -1), (32, 1)),
                            np.tile(np.asarray(inputs["k_gain"]).reshape(1, -1), (96, 1))], 0)
    col = [columns(inputs[n]) for n in ("norm_mix", "norm_mem", "mem_in_gain", "norm_ffn", "ssm_out_gain", "conv_b")]
    arrays["col_params"] = np.ascontiguousarray(np.concatenate(col + [columns(inputs["conv_w"]), gains], 1))
    return arrays


def kernel(**inputs):
    import concourse.bacc as bacc
    from concourse.bass_utils import run_bass_kernel_spmd

    nc = bacc.Bacc("TRN2", target_bir_lowering=False, num_devices=1)
    arrays, a, o = {}, {}, {}
    for n, x in lay_out(inputs).items():
        arrays[f"in_{n}"] = x
        a[n] = nc.dram_tensor(f"in_{n}", x.shape, mybir.dt.from_np(x.dtype), kind="ExternalInput").ap()
    for n, shape in OUTS:
        o[n] = nc.dram_tensor(f"out_{n}", shape, F32, kind="ExternalOutput").ap()
    build(nc, a, o)
    r = run_bass_kernel_spmd(nc, [arrays], core_ids=[0])
    return tuple(r.results[0][f"out_{n}"] for n, _ in OUTS)
```

```python
from contextlib import ExitStack

import concourse.bass as bass
import concourse.mybir as mybir
import numpy as np

F32 = mybir.dt.float32
I32 = mybir.dt.int32
U32 = mybir.dt.uint32
ALU = mybir.AluOpType
ACT = mybir.ActivationFunctionType
AX = mybir.AxisListType

P = 128
D = 1024
KT = D // P
SEQ = 256
NB = 8
NS = 4
NTS = NB * NS
PAST = 1024
NTOK = SEQ + NTS
ROWS = [P, P, NTS]
COL0 = [0, P, 2 * P]
AH, DH = 8, 64
SH, NST = 8, 128
MH, MD, NM = 4, 128, 256
NE, FF = 32, 1024
TOPK = 4
EPS = 1e-6
SLOTS = 64
NPASS_MAX = -(-NTOK // SLOTS)
INW = 3080
NEG = -1.0e30
ROPE_HALF = 8
UNIT = 4096
RING = 6

UNITS = (["q", "k", "v", "z", "xbc0", "xbc1", "h0", "scratch"]
         + [f"{c}{b}" for g in range(2) for c in "KV" for b in range(4 * g, 4 * g + 4)]
         + ["wout0", "wout1", "wmk", "wmv", "wmq"] + [f"mem{i}" for i in range(4)] + ["wmo", "pad", "pad"])
assert len(UNITS) % RING == 0
U = {n: i for i, n in enumerate(UNITS)}


def slot_loads(upto, slot):
    return sum({"s": 0, "p": 0, "K": 2, "V": 2, "m": 2}.get(UNITS[i][0], 1) for i in range(slot, upto, RING))


def constants():
    f = np.float32
    k, q = np.arange(P)[:, None], np.arange(P)[None, :]
    c = {}
    c["ident"] = (k == q).astype(f)
    c["eps"] = np.full((P, 1), EPS, f)
    c["tri"] = (k <= q).astype(f)
    c["strict"] = (k < q).astype(f)
    c["ones"] = np.ones((P, P), f)
    s, t = np.arange(NTS)[:, None], np.arange(NTS)[None, :]
    same = (s // NS) == (t // NS)
    c["tri_s"] = ((s <= t) & same).astype(f)
    c["same_s"] = same.astype(f)
    c["bsel"] = (s // NS == np.arange(NB)[None, :]).astype(f)
    c["iota64"] = np.broadcast_to(np.arange(SLOTS, dtype=f), (P, SLOTS))
    c["iota32"] = np.broadcast_to(np.arange(NE, dtype=f), (P, NE))
    c["thr"] = np.broadcast_to(SLOTS * np.arange(1, NPASS_MAX, dtype=f), (P, NPASS_MAX - 1))
    inv = np.power(f(500000.0), -np.arange(ROPE_HALF, dtype=f) / f(ROPE_HALF))
    ang = np.arange(SEQ, dtype=f)[:, None] * inv[None, :]
    ang_s = (PAST + np.tile(np.arange(NS), 2 * NB)).astype(f)[:, None] * inv[None, :]
    for n, fn in (("cos", np.cos), ("sin", np.sin)):
        c[n] = fn(ang).astype(f).reshape(2, P, ROPE_HALF).transpose(1, 0, 2).reshape(P, -1)
        c[n + "_s"] = fn(ang_s).astype(f)

    def count(dist):
        return sum(((dist >= 0) & (dist % d == 0) & (dist <= w)).astype(f)
                   for w, d in ((128, 1), (512, 4), (2048, 16)))

    def log_count(n, scale):
        return np.where(n > 0, np.log(np.maximum(n, 1)) / scale, NEG).astype(f)

    scale = DH ** -0.5
    for i in range(2):
        n = count((i * P + np.arange(P))[:, None] - np.arange((i + 1) * P)[None, :])
        c[f"bias{i}"] = log_count(n, scale)
    row = np.arange(P)
    step = row % NS
    old = (16 * np.arange(32)[:, None] + np.arange(4)[None, :]).reshape(-1)
    dense = PAST - 512 + (4 * np.arange(P)[None, :] + np.arange(4)[:, None]).reshape(-1)
    c["bias_past"] = log_count(count((PAST + step)[:, None] - np.concatenate([old, dense])[None, :]), scale)
    for g in range(2):
        nk = np.arange(NTS)
        n = count(step[:, None] - (nk % NS)[None, :]) * ((nk // NS)[None, :] == (4 * g + row // 32)[:, None])
        c[f"bias_new{g}"] = log_count(n, scale)
    c["head8"] = (row[:, None] % 32 // NS == np.arange(AH)[None, :]).astype(f)
    c["head4"] = (row[:, None] % 32 // NS == np.arange(MH)[None, :]).astype(f)
    c["token16"] = (row[:, None] // 32 * NS + step[:, None] == np.arange(4 * NS)[None, :]).astype(f)
    c["expert"] = (row[:, None] % NE == np.arange(NE + 1)[None, :] % NE).astype(f)
    return c


def packed_constants():
    at, cols, parts = {}, 0, []
    for n, a in constants().items():
        r, w = a.shape
        at[n] = (r, cols, w)
        full = np.zeros((P, w), np.float32)
        full[:r] = a
        parts.append(full)
        cols += w
    return at, np.concatenate(parts, 1)


ROWP = [("q_gain", DH), ("k_gain", DH), ("dt_bias", SH), ("a_log", SH), ("d_skip", SH), ("mem_q_gain", MD),
        ("mem_k_gain", MD), ("b_router", NE), ("norm_ffn", D)]
COLP = [("norm_mix", 8), ("norm_mem", 8), ("mem_in_gain", 8), ("ssm_out_gain", 4),
        ("conv_b", 8), ("conv_w", 32), ("qk_gain_s", DH)]


def offsets(pairs):
    at, c = {}, 0
    for n, w in pairs:
        at[n] = (c, w)
        c += w
    return at, c


def build(nc, a, o):
    const_at, const_np = packed_constants()
    NC = const_np.shape[1]
    row_at, NR = offsets(ROWP)
    col_at, NCP = offsets(COLP)
    with ExitStack() as ctx:
        def sb(name, shape, dt=F32):
            return ctx.enter_context(nc.sbuf_tensor(name, shape, dt))

        sems = {}

        def sem(name):
            if name not in sems:
                sems[name] = ctx.enter_context(nc.semaphore(name))
            return sems[name]

        ring = sb("ring", [P, RING, UNIT])
        X = sb("X", [P, 3, D])
        CN = sb("CN", [P, NC])
        RP = sb("RP", [P, NR])
        CP = sb("CP", [P, NCP])
        mixT = sb("mixT", [P, 8, NTOK])
        WDT = sb("WDT", [P, KT, SH])
        WR = sb("WR", [P, KT, NE])
        small = sb("small", [P, 512])
        top_i = sb("top_i", [P, 3, 8], U32)
        npass_i = sb("npass_i", [P, 1], I32)
        AR = 18800
        arena = sb("arena", [P, AR])
        PS = ctx.enter_context(nc.psum_tensor("PS", [P, 8, 512], F32))

        def cst(n):
            r, c, w = const_at[n]
            return CN[0:r, c:c + w]

        def rowp(n, rows=P):
            c, w = row_at[n]
            return RP[0:rows, c:c + w]

        def colp(n):
            c, w = col_at[n]
            return CP[:, c:c + w]

        def ar(at, *dims):
            n = int(np.prod(dims))
            assert at + n <= AR, (at, dims)
            v = arena[:, at:at + n]
            if len(dims) == 1:
                return v
            names = "abcde"[:len(dims)]
            return v.rearrange("p (" + " ".join(names) + ") -> p " + " ".join(names),
                               **{names[i]: dims[i] for i in range(len(dims))})

        def sm(at, *dims):
            n = int(np.prod(dims))
            assert at + n <= 512
            v = small[:, at:at + n]
            if len(dims) == 1:
                return v
            names = "abcde"[:len(dims)]
            return v.rearrange("p (" + " ".join(names) + ") -> p " + " ".join(names),
                               **{names[i]: dims[i] for i in range(len(dims))})

        def slot(name, *dims):
            v = ring[:, (U[name] if isinstance(name, str) else name) % RING, 0:int(np.prod(dims))]
            if len(dims) == 1:
                return v
            names = "abcde"[:len(dims)]
            return v.rearrange("p (" + " ".join(names) + ") -> p " + " ".join(names),
                               **{names[i]: dims[i] for i in range(len(dims))})

        ident = cst("ident")

        XN = ar(0, 3, D)
        hT = ar(3072, KT, NTOK)
        QK = ar(5376, 2, 2, AH, DH)
        QKS = ar(7424, AH, DH)
        V = ar(7936, 3, AH * DH)
        Z = ar(9472, 3, 512)
        XP = ar(11008, 8, 3 + SEQ)
        XS = ar(13080, 8, NB, 3 + NS)
        QSC = ar(13528, 2 * AH, DH)
        CVS = ar(14552, 8, NTS)
        TAIL = ar(14808, 8, 27)
        CONVO = ar(15024, D)
        UT = ar(16496, 8, NTOK)
        SC = ar(17000, D)
        QB = ar(0, 4, NB, NTS)
        kTs = ar(1024, 4, NTS)
        qT = ar(1152, 4, SEQ)
        kT = ar(2176, 4, SEQ)
        SCO = [ar(5376, 8, P), ar(3200, 8, SEQ)]
        PT = ar(13528, 2, 8, P)
        XB = ar(11008, 3, 768)
        XD = ar(1152, 3, 512)
        XDE = ar(2688, 3, 512)
        HT0 = ar(4224, 512)
        CM = ar(4736, 2, NB, NTS)
        SEG = ar(5376, SH, P)
        DTRI = ar(6400, SH, P)
        DREP = ar(6912, SH, DH)
        STM = ar(7424, 2, P)
        Y = ar(13528, 3, 512)
        HOUT = ar(15064, 4, NST)
        YSQ = ar(15576, 512)
        BNM = ar(16496, 2, NB, P)
        KTB = ar(1152, 2, 4, 5 * P)
        SS = ar(6272, 5 * P + NTS)
        PTS = ar(6944, 6, P)
        HMT = ar(5376, KT, NM)
        MK = ar(7424, 2, MH, MD)
        MV = ar(8448, 2, MH * MD)
        MKT = ar(9472, MH, NM)
        MQ = ar(10496, 3, MH, MD)
        QMT = ar(12032, MH, NTOK)
        QMB = ar(13184, MH, NB, 32)
        SMM = [ar(14208, MH, NM), ar(10496, MH, NM)]
        MOM = ar(14208, MH * MD)
        PTM = ar(15232, 2, MH, P)
        KTM = ar(16256, 2, MH, NM)
        MP = ar(16256, 2, D)
        SS2 = ar(10496, NM)
        OT = mixT[:, 0:MH, :]
        MKV_BANKS = (5, 6, 7, 5)
        BGU = ar(5376, 2 * FF)
        BD = ar(7424, D)
        XG = ar(13736, 512)
        XT = ar(8448, KT, SLOTS)
        AT = ar(8960, 4, P)
        YB = ar(9472, 512)
        LP = ar(10848, NTOK)
        LAST_BANKS = ((6, 7), (2, 3), (4, 5))
        SW = ar(14248, 3 * P)
        SEL = ar(10272, 3, SLOTS)
        SELW = ar(10464, 3, 2, SLOTS)
        G1 = ar(10848, 2, SLOTS * 4)
        SG = ar(11360, 2, SLOTS * 4)
        U1 = ar(11872, 2, SLOTS * 4)
        AC = ar(12384, 512)
        SPARE = ar(14640, 2, 2 * FF)
        EROW = ar(12896, SLOTS)
        POSM = ar(12960, NE + 1, 3)
        GW = ar(13060, NE + 1, 3)
        MSK = ar(13160, 3, NE)
        LG = ar(13256, 3, NE)
        OH4 = ar(13352, 3, TOPK, NE)
        CUM = 256
        SSQ = sm(0, 3)
        RS = sm(3, 3)
        SSH = sm(8, 48)
        DTR = sm(56, 3, SH)
        DTA = sm(80, 3, SH)
        DTV = sm(104, 3, SH)
        ACU = sm(128, 3, SH)
        EAC = sm(152, 3, SH)
        TOE = sm(176, 3, SH)
        DT1 = sm(200, 3, SH)
        AEX = sm(224, SH)
        DEC1 = sm(232, SH)
        DECS = sm(240, 4, NB)
        MX = sm(272, 3, 8)
        NMX = sm(296, 3, 8)
        DEN = sm(320, 3, 8)
        RDEN = sm(344, 3, 8)
        TOPV = sm(368, 3, 8)
        TOPF = sm(392, 3, 8)
        TOPW = sm(416, 3, TOPK)
        CNT = sm(428, 4)
        NPF = sm(432, 1)
        TS = sm(436, 8)
        HD = sm(444, 8)

        block = ctx.enter_context(nc.Block())

        @block.tensor
        def _(pe):
            mm = nc.tensor.matmul

            def transpose_rows(src, tiles, n0):
                for t in tiles:
                    pe.wait_ge(sem("rows_normed"), n0 + t + 1)
                    n = ROWS[t]
                    for k in range(KT):
                        bank, col = (2 * t + k // 4, k % 4 * P) if t < 2 else (4, k * n)
                        last = nc.tensor.transpose(PS[:, bank, col:col + n], src[0:n, t, k * P:(k + 1) * P],
                                                   ident[0:n, 0:n])
                    last.then_inc(sem("rows_turned"), 1)

            def loaded(name):
                u = U[name]
                pe.wait_ge(sem(f"slot{u % RING}_loaded"), 16 * slot_loads(u + 1, u % RING))

            pe.wait_ge(sem("consts_loaded"), 32)
            transpose_rows(XN, (0, 1, 2), 0)
            pe.wait_ge(sem("state_conv_loaded"), 16)
            for m in range(8):
                last = nc.tensor.transpose(PS[:, 5, m * 24:(m + 1) * 24], SC[0:24, m * P:(m + 1) * P],
                                           ident[0:24, 0:24])
            last.then_inc(sem("conv_state_turned"), 1)

            pe.wait_ge(sem("cols_ready"), 3)
            for g, name in enumerate("qkvz"):
                loaded(name)
                w = slot(name, KT, 512)
                for t in range(2):
                    if 2 * g + t == 5:
                        pe.wait_ge(sem("conv_state_kept"), 1)
                    for k in range(KT):
                        last = mm(PS[:, 2 * g + t, :], hT[:, k, t * P:(t + 1) * P], w[:, k, :],
                                  start=k == 0, stop=k == KT - 1)
                    last.then_inc(sem("proj_ready"), 1)
            pe.wait_ge(sem("proj_kept"), 1)
            for k in range(KT):
                for g, name in enumerate("qkvz"):
                    last = mm(PS[32 * g:32 * g + 32, 0, :], hT[:, k, SEQ:NTOK], slot(name, KT, 512)[:, k, :],
                              start=k == 0, stop=k == KT - 1, tile_position=(0, 32 * g))
            last.then_inc(sem("proj_ready"), 1)
            pe.wait_ge(sem("proj_kept"), 2)
            pe.wait_ge(sem("dt_weights_loaded"), 16)
            for t in range(3):
                for k in range(KT):
                    last = mm(PS[0:ROWS[t], 1, t * 8:t * 8 + 8], hT[:, k, COL0[t]:COL0[t] + ROWS[t]], WDT[:, k, :],
                              start=k == 0, stop=k == KT - 1)
            last.then_inc(sem("dt_raw_ready"), 1)
            for m in range(8):
                loaded(f"xbc{m // 4}")
                bank = (2 + m) % 8
                pe.wait_ge(sem("proj_kept"), (bank + 1) if m < 6 else 11)
                if m == 7:
                    pe.wait_ge(sem("dt_raw_kept"), 1)
                w = slot(f"xbc{m // 4}", KT, 512)
                for k in range(KT):
                    last = mm(PS[:, bank, 0:NTOK], w[:, k, m % 4 * P:(m % 4 + 1) * P], hT[:, k, :],
                              start=k == 0, stop=k == KT - 1)
                last.then_inc(sem("xbc_ready"), 1)

            for t in range(2):
                pe.wait_ge(sem("qk_normed"), t + 1)
                pe.wait_ge(sem("xbc_kept"), 16)
                for j in range(2):
                    for p in range(4):
                        last = nc.tensor.transpose(PS[:, 2 * t + j, p * P:(p + 1) * P],
                                                   QK[:, t, j, 2 * p:2 * p + 2, :].rearrange("p h d -> p (h d)"),
                                                   ident)
                    last.then_inc(sem("qk_turned"), 1)
            pe.wait_ge(sem("qk_normed"), 3)
            for j in range(2):
                r = slice(32 * j, 32 * j + 32)
                for p in range(4):
                    last = nc.tensor.transpose(PS[:, 4 + j, p * NTS:(p + 1) * NTS],
                                               QKS[r, 2 * p:2 * p + 2, :].rearrange("p h d -> p (h d)"),
                                               ident[r, r])
            last.then_inc(sem("qk_turned"), 1)

            pe.wait_ge(sem("tails_ready"), 1)
            for m in range(8):
                last = nc.tensor.transpose(PS[0:27, 6 + m // 4, m % 4 * P:(m % 4 + 1) * P], TAIL[:, m, :], ident)
            last.then_inc(sem("tail_rows_ready"), 1)

            pe.wait_ge(sem("tail_rows_kept"), 2)
            pe.wait_ge(sem("qk_kept"), 7)
            for i in range(2):
                for b in range(4):
                    for c in range(2):
                        p, e = 2 * (b // 2) + c, b % 2
                        nk = (i + 1) * P
                        last = mm(PS[:, 4 * (1 - i) + b, c * 256:c * 256 + nk],
                                  qT[64 * e:64 * e + 64, p, i * P:(i + 1) * P], kT[64 * e:64 * e + 64, p, 0:nk],
                                  start=True, stop=True)
                last.then_inc(sem("scores_ready"), 1)

            for t in range(3):
                pe.wait_ge(sem("conv_silu_ready"), 8 if t < 2 else 16)
                pe.wait_ge(sem("scores_kept"), 1 if t < 2 else 2)
                if t == 2:
                    pe.wait_ge(sem("dta_ready"), 1)
                    pe.wait_ge(sem("scores_kept"), 2)
                    for c in range(3):
                        n = ROWS[c]
                        tri = cst("tri") if c < 2 else cst("tri_s")
                        tot = cst("ones") if c < 2 else cst("same_s")
                        mm(PS[0:n, 1, CUM + c * 8:CUM + c * 8 + 8], tri, DTA[0:n, c, :], start=True, stop=True)
                        last = mm(PS[0:n, 1, CUM + 32 + c * 8:CUM + 40 + c * 8], tot, DTA[0:n, c, :], start=True, stop=True)
                    pe.wait_ge(sem("drep_ready"), 1)
                    for p in range(4):
                        last = mm(PS[:, 1, CUM + 64 + 8 * p:CUM + 72 + 8 * p],
                                  DREP[0:NTS, 2 * p:2 * p + 2, :].rearrange("p h d -> p (h d)"), cst("bsel"),
                                  start=True, stop=True)
                    last.then_inc(sem("cumulated"), 1)
                n = ROWS[t]
                for m in range(6):
                    last = nc.tensor.transpose(PS[0:n, (4, 6, 0)[t] + m // 4, m % 4 * P:(m % 4 + 1) * P],
                                               UT[:, m, COL0[t]:COL0[t] + n], ident)
                last.then_inc(sem("xb_turned"), 1)

            def turn_probs(i, banks):
                pe.wait_ge(sem("probs_ready"), i + 1)
                for j in range(i + 1):
                    for s in range(8):
                        last = nc.tensor.transpose(PS[:, banks[2 * j + s // 4], s % 4 * P:(s % 4 + 1) * P],
                                                   SCO[i][:, s, j * P:(j + 1) * P], ident)
                last.then_inc(sem("probs_turned"), 1)

            def weigh_values(i, bank):
                pe.wait_ge(sem("probs_kept"), i + 1)
                for s in range(8):
                    b, c = s // 2, s % 2
                    p, e = 2 * (b // 2) + c, b % 2
                    h = 2 * p + e
                    for j in range(i + 1):
                        last = mm(PS[64 * e:64 * e + 64, bank, p * P:(p + 1) * P], V[:, j, h * DH:(h + 1) * DH],
                                  PT[:, j, s, :], start=j == 0, stop=j == i)
                last.then_inc(sem("att_ready"), 1)

            turn_probs(0, (2, 3))
            pe.wait_ge(sem("xb_kept"), 2)
            weigh_values(0, 4)
            turn_probs(1, (2, 3, 5, 6))
            weigh_values(1, 7)

            loaded("h0")
            pe.wait_ge(sem("ssd_exps_ready"), 1)
            pe.wait_ge(sem("xb_kept"), 3)
            pe.wait_ge(sem("probs_kept"), 2)
            H0 = slot("h0", NB, 4, NST)

            def turn_states(b0, b1):
                for b in range(b0, b1):
                    if b >= 2:
                        pe.wait_ge(sem("h0t_kept"), b - 1)
                    for p in range(4):
                        last = nc.tensor.transpose(PS[:, 1 + b % 2, p * P:(p + 1) * P], H0[:, b, p, :], ident)
                    last.then_inc(sem("h0_turned"), 1)

            H0T = slot("scratch", NB, 512)

            for t in range(3):
                n = ROWS[t]
                if t:
                    pe.wait_ge(sem("st_kept"), t)
                else:
                    pe.wait_ge(sem("att_kept"), 2)
                    pe.wait_ge(sem("probs_kept"), 2)
                for g in range(2):
                    last = mm(PS[0:n, 3, g * P:g * P + n], UT[:, 4 + g, COL0[t]:COL0[t] + n],
                              UT[:, 6 + g, COL0[t]:COL0[t] + n], start=True, stop=True)
                last.then_inc(sem("st_ready"), 1)
                pe.wait_ge(sem("dtri_ready"), t + 1)
                pe.wait_ge(sem("seg_kept"), t)
                for half in range(2):
                    last = mm(PS[0:n, 4 + half, 0:4 * n], cst("ones")[0:n, 0:n],
                              DTRI[0:n, 4 * half:4 * half + 4, 0:n], start=True, stop=True)
                last.then_inc(sem("arow_ready"), 1)
                if t < 2:
                    turn_states(4 * t, 4 * t + 4)
                if t:
                    pe.wait_ge(sem("y_kept"), t)
                if t == 1:
                    pe.wait_ge(sem("state_ready"), 1)
                    for g in range(2):
                        last = mm(PS[:, 7, g * 256:(g + 1) * 256], UT[:, 6 + g, P:2 * P],
                                  HT0[:, g * 256:(g + 1) * 256], start=True, stop=True)
                    last.then_inc(sem("y_carried_ready"), 1)
                if t == 2:
                    pe.wait_ge(sem("h0t_kept"), NB)
                    pe.wait_ge(sem("cm_ready"), 1)
                    for g in range(2):
                        for b in range(NB):
                            r = 32 * (b % 4)
                            last = mm(PS[r:r + 32, 7, g * 256:(g + 1) * 256], CM[:, g, b, :],
                                      H0T[:, b, g * 256:(g + 1) * 256], start=b < 4, stop=b >= 4,
                                      tile_position=(0, r))
                    last.then_inc(sem("y_carried_ready"), 1)
                pe.wait_ge(sem("decay_ready"), t + 1)
                for h in range(SH):
                    last = mm(PS[0:n, 6, h * DH:(h + 1) * DH], SEG[0:n, h, 0:n], XD[0:n, t, h * DH:(h + 1) * DH],
                              start=True, stop=True)
                last.then_inc(sem("y_within_ready"), 1)
                if t < 2:
                    pe.wait_ge(sem("xde_ready"), 1)
                    pe.wait_ge(sem("state_ready"), t)
                    for g in range(2):
                        last = mm(PS[:, 0, g * 256:(g + 1) * 256], XB[:, t, 512 + g * P:512 + (g + 1) * P],
                                  XDE[:, t, g * 256:(g + 1) * 256], start=True, stop=True)
                    last.then_inc(sem("chunk_state_ready"), 1)
            pe.wait_ge(sem("state_ready"), 2)
            pe.wait_ge(sem("h0t_kept"), NB)
            for p in range(4):
                last = nc.tensor.transpose(PS[:, 2, p * P:(p + 1) * P], HT0[:, p * P:(p + 1) * P], ident)
            last.then_inc(sem("state_rows_ready"), 1)
            pe.wait_ge(sem("bnm_ready"), 1)
            pe.wait_ge(sem("seg_kept"), 3)
            for n in range(8):
                p, half = n // 2, n % 2
                if n >= 2:
                    pe.wait_ge(sem("h_updated"), n - 1)
                last = mm(PS[:, 4 + n % 2, :], XDE[0:NTS, 2, p * P:(p + 1) * P],
                          BNM[0:NTS, p // 2, 4 * half:4 * half + 4, :].rearrange("p b n -> p (b n)"),
                          start=True, stop=True)
                last.then_inc(sem("h_added"), 1)

            for t in range(3):
                n = ROWS[t]
                pe.wait_ge(sem("y_normed"), t + 1)
                if t == 0:
                    pe.wait_ge(sem("ssd_exps_ready"), 1)
                if t == 2:
                    pe.wait_ge(sem("state_rows_kept"), 1)
                for k in range(4):
                    last = nc.tensor.transpose(PS[:, t, k * n:(k + 1) * n], Y[0:n, t, k * P:(k + 1) * P],
                                               ident[0:n, 0:n])
                last.then_inc(sem("y_turned"), 1)

            for g in range(2):
                for bb in range(2):
                    for b in range(2):
                        name = f"K{4 * g + 2 * bb + b}"
                        loaded(name)
                        K = slot(name, 5, 512)
                        for j in range(5):
                            n = 20 * g + 10 * bb + 5 * b + j
                            pe.wait_ge(sem("kt_kept"), max(n - 2, 0))
                            if n == 0:
                                pe.wait_ge(sem("h_updated"), 8)
                                pe.wait_ge(sem("st_kept"), 3)
                            for p in range(4):
                                last = nc.tensor.transpose(PS[:, 3 + n % 3, p * P:(p + 1) * P],
                                                           K[:, j, p * P:(p + 1) * P], ident)
                            last.then_inc(sem("kt_turned"), 1)
                    pe.wait_ge(sem("kt_kept"), 20 * g + 10 * (bb + 1))
                    if g == 0 and bb == 0:
                        pe.wait_ge(sem("y_kept"), 3)
                    if bb == 0:
                        pe.wait_ge(sem("scores_s_kept"), g)
                    for part in range(3):
                        for p in range(4):
                            for b in range(2):
                                r = 64 * bb + 32 * b
                                batch = 4 * g + 2 * bb + b
                                lhs = QB[:, p, batch, :]
                                if part == 0:
                                    dst, rhs = PS[r:r + 32, 6, :], KTB[:, b, p, 0:512]
                                elif part == 1:
                                    dst, rhs = PS[r:r + 32, 7, 0:P], KTB[:, b, p, 512:640]
                                else:
                                    dst, rhs = PS[r:r + 32, 7, P:P + NTS], kTs[:, p, :]
                                last = mm(dst, lhs, rhs, start=p == 0, stop=p == 3, tile_position=(0, r),
                                          skip_group_check=True)
                    last.then_inc(sem("scores_s_ready"), 1)
                pe.wait_ge(sem("exp_ready"), 3 + g)
                for j in range(6):
                    w = P if j < 5 else NTS
                    last = nc.tensor.transpose(PS[0:w, 3 + j // 4, j % 4 * P:(j % 4 + 1) * P],
                                               SS[:, j * P:j * P + w], ident)
                last.then_inc(sem("probs_turned"), 1)
                pe.wait_ge(sem("probs_s_kept"), 2 * (g + 1))
                if g == 0:
                    pe.wait_ge(sem("y_turned_kept"), 3)
                for b in range(4):
                    loaded(f"V{4 * g + b}")
                for j in range(6):
                    for b in range(4):
                        rows = slice(0, P if j < 5 else NTS)
                        rhs = slot(f"V{4 * g + b}", 5, 512)[:, j, :] if j < 5 else V[0:NTS, 2, :]
                        last = mm(PS[32 * b:32 * b + 32, 1, :], PTS[rows, j, 32 * b:32 * b + 32], rhs,
                                  start=j == 0, stop=j == 5, tile_position=(0, 32 * b))
                last.then_inc(sem("att_rows_ready"), 1)
                pe.wait_ge(sem("att_rows_kept"), g + 1)
                for p in range(4):
                    last = mm(PS[:, 2, p * NTS + 16 * g:p * NTS + 16 * g + 16], SS[:, p * P:(p + 1) * P],
                              cst("token16"), start=True, stop=True)
                last.then_inc(sem("att_s_ready"), 1)

            def project_rows(lhs, nk, w_of, sem_out, sample_ready):
                for t in range(2):
                    if t:
                        pe.wait_ge(sem(sample_ready[0]), sample_ready[1])
                    for half in range(2):
                        w = w_of(half)
                        for k in range(nk):
                            last = mm(PS[:, 2 * t + half, :], lhs[:, k, t * P:(t + 1) * P], w(k),
                                      start=k == 0, stop=k == nk - 1)
                        last.then_inc(sem(sem_out), 1)
                for k in range(nk):
                    for c in range(4):
                        last = mm(PS[32 * c:32 * c + 32, 4, 0:256], lhs[:, k, SEQ:NTOK],
                                  w_of(c // 2)(k)[:, c % 2 * 256:(c % 2 + 1) * 256],
                                  start=k == 0, stop=k == nk - 1, tile_position=(0, 32 * c))
                last.then_inc(sem(sem_out), 1)

            def wout(half):
                loaded(f"wout{half}")
                w = slot(f"wout{half}", KT, 512)
                return lambda k: w[:, k, :]

            pe.wait_ge(sem("y_turned_kept"), 3)
            pe.wait_ge(sem("att_kept"), 2)
            project_rows(mixT, 8, wout, "mixed_ready", ("mix_ready", 1))

            for t in range(2):
                pe.wait_ge(sem("rows_normed"), 3 + t + 1)
                if t == 0:
                    pe.wait_ge(sem("probs_s_kept"), 4)
                    pe.wait_ge(sem("scores_s_kept"), 2)
                else:
                    pe.wait_ge(sem("residual_ready"), 1)
                for k in range(KT):
                    last = nc.tensor.transpose(PS[:, (5, 6, 7, 0)[2 * t + k // 4], k % 4 * P:(k % 4 + 1) * P],
                                               XN[:, t, k * P:(k + 1) * P], ident)
                last.then_inc(sem("hm_turned"), 1)
            for n in range(4):
                kv, t = n // 2, n % 2
                name = ("wmk", "wmv")[kv]
                loaded(name)
                w = slot(name, KT, 512)
                if n < 2:
                    pe.wait_ge(sem("hm_kept"), n + 1)
                elif n == 3:
                    pe.wait_ge(sem("mkv_kept"), 1)
                for k in range(KT):
                    last = mm(PS[:, MKV_BANKS[n], :], HMT[:, k, t * P:(t + 1) * P],
                              w[:, k, :], start=k == 0, stop=k == KT - 1)
                last.then_inc(sem("mkv_ready"), 1)

            pe.wait_ge(sem("residual_ready"), 3)
            transpose_rows(XN, (0, 1, 2), 5)
            pe.wait_ge(sem("cols_ready"), 6)
            loaded("wmq")
            w = slot("wmq", KT, 512)
            for t in range(2):
                for k in range(KT):
                    last = mm(PS[:, t, :], hT[:, k, COL0[t]:COL0[t] + ROWS[t]], w[:, k, :],
                              start=k == 0, stop=k == KT - 1)
                last.then_inc(sem("mq_ready"), 1)
            for k in range(KT):
                for h in range(MH):
                    last = mm(PS[32 * h:32 * h + 32, 2, 0:MD], hT[:, k, SEQ:NTOK], w[:, k, h * MD:(h + 1) * MD],
                              start=k == 0, stop=k == KT - 1, tile_position=(0, 32 * h))
            last.then_inc(sem("mq_ready"), 1)
            pe.wait_ge(sem("mk_normed"), 1)
            pe.wait_ge(sem("mkv_kept"), 4)
            for t in range(2):
                for h in range(MH):
                    last = nc.tensor.transpose(PS[:, 6 + t, h * P:(h + 1) * P], MK[:, t, h, :], ident)
                last.then_inc(sem("mk_turned"), 1)
            for t in range(3):
                n = ROWS[t]
                pe.wait_ge(sem("mq_normed"), t + 1)
                for h in range(MH):
                    last = nc.tensor.transpose(PS[:, 3 + t, h * n:(h + 1) * n], MQ[0:n, t, h, :], ident[0:n, 0:n])
                last.then_inc(sem("mq_turned"), 1)
            pe.wait_ge(sem("mk_turned_kept"), 2)
            pe.wait_ge(sem("mq_turned_kept"), 4)
            for i in range(2):
                for h in range(MH):
                    last = mm(PS[:, (6, 0)[i] + h // 2, h % 2 * 256:(h % 2 + 1) * 256], QMT[:, h, i * P:(i + 1) * P],
                              MKT[:, h, :], start=True, stop=True)
                last.then_inc(sem("mscores_ready"), 1)
            for i in range(2):
                pe.wait_ge(sem("probs_ready"), 3 + i)
                for j in range(2):
                    for h in range(MH):
                        last = nc.tensor.transpose(PS[:, 2 + 2 * i + j, h * P:(h + 1) * P],
                                                   SMM[i][:, h, j * P:(j + 1) * P], ident)
                last.then_inc(sem("probs_turned"), 1)
                pe.wait_ge(sem("mprobs_kept"), 2 * (i + 1))
                if i == 1:
                    pe.wait_ge(sem("mo_kept"), 1)
                for h in range(MH):
                    for j in range(2):
                        last = mm(PS[:, 2 + 2 * i, h * P:(h + 1) * P], MV[:, j, h * P:(h + 1) * P],
                                  PTM[:, j, h, :], start=j == 0, stop=j == 1)
                last.then_inc(sem("mo_ready"), 1)
            for g in range(2):
                for u in range(2):
                    name = f"mem{2 * g + u}"
                    loaded(name)
                    M = slot(name, 2, 2, 2, MH * MD)
                    for b in range(2):
                        for j in range(2):
                            n = 8 * g + 4 * u + 2 * b + j
                            pe.wait_ge(sem("ktm_kept"), max(n - 1, 0))
                            for h in range(MH):
                                last = nc.tensor.transpose(PS[:, (3, 5)[n % 2], h * P:(h + 1) * P],
                                                           M[:, 0, b, j, h * P:(h + 1) * P], ident)
                            last.then_inc(sem("ktm_turned"), 1)
                    pe.wait_ge(sem("ktm_kept"), 8 * g + 4 * (u + 1))
                    if u == 0:
                        pe.wait_ge(sem("exp_ready"), 6 + g)
                    for h in range(MH):
                        for b in range(2):
                            r = 64 * u + 32 * b
                            last = mm(PS[r:r + 32, 6, 0:NM], QMB[:, h, 4 * g + 2 * u + b, :], KTM[:, b, h, :],
                                      start=h == 0, stop=h == MH - 1, tile_position=(0, r))
                    last.then_inc(sem("mscores_s_ready"), 1)
                pe.wait_ge(sem("exp_ready"), 7 + g)
                for j in range(2):
                    last = nc.tensor.transpose(PS[:, 7, j * P:(j + 1) * P], SS2[:, j * P:(j + 1) * P], ident)
                last.then_inc(sem("probs_turned"), 1)
                pe.wait_ge(sem("mprobs_kept"), 4 + g + 1)
                if g == 0:
                    pe.wait_ge(sem("mo_kept"), 2)
                for j in range(2):
                    for b in range(4):
                        M = slot(f"mem{2 * g + b // 2}", 2, 2, 2, MH * MD)
                        last = mm(PS[32 * b:32 * b + 32, 2, :], PTM[:, 0, j, 32 * b:32 * b + 32],
                                  M[:, 1, b % 2, j, :], start=j == 0, stop=j == 1, tile_position=(0, 32 * b))
                last.then_inc(sem("att_rows_ready"), 1)
                pe.wait_ge(sem("att_rows_kept"), 3 + g)
                for h in range(MH):
                    last = mm(PS[:, 4, h * NTS + 16 * g:h * NTS + 16 * g + 16], MOM[:, h * P:(h + 1) * P],
                              cst("token16"), start=True, stop=True)
                last.then_inc(sem("mo_ready"), 1)

            def wmo(half):
                w = slot("wmo", MH, D)
                return lambda k: w[:, k, half * 512:(half + 1) * 512]

            pe.wait_ge(sem("mo_kept"), 2)
            loaded("wmo")
            project_rows(OT, MH, wmo, "mixed_ready", ("mo_kept", 3))

            pe.wait_ge(sem("residual_ready"), 6)
            transpose_rows(XN, (0, 1, 2), 8)
            pe.wait_ge(sem("cols_ready"), 9)
            pe.wait_ge(sem("router_loaded"), 16)
            for k in range(KT):
                g = k % 4
                last = mm(PS[32 * g:32 * g + 32, 5, 0:NTOK], WR[:, k, :], hT[:, k, :],
                          start=k < 4, stop=k >= 4, tile_position=(0, 32 * g))
            last.then_inc(sem("logits_ready"), 1)
            pe.wait_ge(sem("logit_parts_kept"), 1)
            for t in range(3):
                last = mm(PS[0:ROWS[t], 5, t * NE:(t + 1) * NE], LP[:, COL0[t]:COL0[t] + ROWS[t]], cst("expert")[:, 0:NE],
                          start=True, stop=True)
            last.then_inc(sem("logits_ready"), 1)
            halves = [(nb, half) for nb in range(2) for half in range(2)]

            def gate_up_biases(n, nb):
                pe.wait_ge(sem("erow_ready"), n + 1)
                for half in range(2):
                    c = half * 1024 + nb * 512
                    mm(PS[64 * half:64 * half + 64, nb, :], EROW[0:NE, :], BGU[0:NE, c:c + 512],
                       start=True, stop=False, tile_position=(0, 64 * half))

            pe.wait_ge(sem("expert_biases_loaded"), 32)
            gate_up_biases(0, 0)
            gate_up_biases(0, 1)
            pe.wait_ge(sem("routed"), 1)
            for t in range(3):
                n = ROWS[t]
                for s in range(t + 1):
                    m = ROWS[s]
                    lhs = (cst("strict") if s == t else cst("ones"))[0:m, 0:n]
                    mm(PS[0:n, 6, t * NE:(t + 1) * NE], lhs, MSK[0:m, s, :], start=s == 0, stop=s == t)
            for s in range(3):
                m = ROWS[s]
                last = mm(PS[:, 6, 96:128], cst("ones")[0:m, :], MSK[0:m, s, :], start=s == 0, stop=s == 2)
            last.then_inc(sem("ranks_ready"), 1)
            front = len(UNITS)

            def gather(n):
                pe.wait_ge(sem("sel_ready"), n + 1)
                for t in range(3):
                    m = ROWS[t]
                    for half in range(2):
                        last = mm(PS[64 * half:64 * half + 64, 2, :], SEL[0:m, t, :],
                                  XN[0:m, t, half * 512:(half + 1) * 512], start=t == 0, stop=t == 2,
                                  tile_position=(0, 64 * half))
                last.then_inc(sem("gathered"), 1)

            def turn_gathered(n):
                pe.wait_ge(sem("xg_kept"), n + 1)
                for c in range(4):
                    last = nc.tensor.transpose(PS[:, 2, c * P:(c + 1) * P], XG[:, c * P:(c + 1) * P], ident)
                last.then_inc(sem("xg_turned"), 1)

            def scatter(n, t, banks=(6, 7)):
                if banks == (6, 7):
                    pe.wait_ge(sem("scatter_added"), n + 1)
                for half in range(2):
                    r = slice(64 * half, 64 * half + 64)
                    last = mm(PS[:, banks[half], :], SW[r, t * P:(t + 1) * P], YB[r, :],
                              start=True, stop=True)
                last.then_inc(sem("scattered"), 1)

            def expert(it, q, pair, odd):
                pe.wait_ge(sem("xt_ready"), q + 1)
                for k in range(KT):
                    j = k // 2
                    if k == 0 and odd:
                        pe.wait_ge(sem("spare_loaded"), 16 + pair * 16)
                    elif k == 0:
                        pe.wait_ge(sem("slot0_loaded"), 16 * slot_loads(front, 0) + 16 + pair * 16)
                    elif k % 2 == 0:
                        pe.wait_ge(sem(f"slot{j}_loaded"), 16 * slot_loads(front, j) + 16 + it * 16)
                    w = SPARE if j == 0 and odd else slot(j, 2, 2 * FF)
                    for nb, half in halves:
                        c = half * 1024 + nb * 512
                        last = mm(PS[64 * half:64 * half + 64, nb, :], XT[:, k, :], w[:, k % 2, c:c + 512],
                                  start=False, stop=k == KT - 1, tile_position=(0, 64 * half))
                    if k % 2 == 1 and k < KT - 1:
                        last.then_inc(sem("expert_units_used"), 1)
                    if k == 1:
                        pe.wait_ge(sem("y_rows_ready"), it + 1)
                        pe.wait_ge(sem("sw_ready"), it + 1)
                        for half in range(2):
                            mm(PS[64 * half:64 * half + 64, 5, :], EROW[0:NE, :],
                               BD[0:NE, half * 512:(half + 1) * 512],
                               start=True, stop=False, tile_position=(0, 64 * half))
                        scatter(3 * q, 0)
                    elif k == 3:
                        scatter(3 * q + 1, 1)
                    elif k == 5:
                        scatter(3 * q + 2, 2)
                last.then_inc(sem("gate_up_ready"), 1)
                gather(q + 1)
                pe.wait_ge(sem("expert_steps"), 3 * it + 1)
                gate_up_biases(it + 1, 0)
                pe.wait_ge(sem("act_ready"), it + 2)
                for c in range(4):
                    last = nc.tensor.transpose(PS[:, 4, c * P:(c + 1) * P], AC[:, c * P:(c + 1) * P], ident)
                last.then_inc(sem("act_turned"), 1)
                gate_up_biases(it + 1, 1)
                pe.wait_ge(sem("at_ready"), it + 1)
                for k in range(KT):
                    j = 4 + k // 4
                    if k % 4 == 0:
                        pe.wait_ge(sem(f"slot{j}_loaded"), 16 * slot_loads(front, j) + 16 + it * 16)
                    w = slot(j, 4, D)
                    for half in range(2):
                        last = mm(PS[64 * half:64 * half + 64, 5, :], AT[:, k % 4, 64 * (k // 4):64 * (k // 4) + 64],
                                  w[:, k % 4, half * 512:(half + 1) * 512],
                                  start=False, stop=k == KT - 1, tile_position=(0, 64 * half))
                    if k == 3:
                        last.then_inc(sem("expert_units_used"), 1)
                        pe.wait_ge(sem("selw_ready"), it + 1)
                        for t in range(3):
                            n = ROWS[t]
                            turned = nc.tensor.transpose(PS[:, 3, COL0[t]:COL0[t] + n],
                                                         SELW[0:n, t].rearrange("p a s -> p (a s)"), ident[0:n, 0:n])
                        turned.then_inc(sem("sw_turned"), 1)
                        turn_gathered(q + 1)
                last.then_inc(sem("down_ready"), 1)

            pe.wait_ge(sem("act_ready"), 1)
            pe.wait_ge(sem("npass_ready"), 1)
            npass = pe.value_load(npass_i[0:1, 0:1], min_val=1, max_val=NPASS_MAX)
            with pe.Fori(0, npass) as r:
                pe.wait_ge(sem("sw_cleared"), r + 1)
                gather(r * (NE + 1))
                turn_gathered(r * (NE + 1))
                with pe.Fori(0, NE // 2) as h:
                    for odd in range(2):
                        expert(r * NE + h * 2 + odd, r * (NE + 1) + h * 2 + odd, r * (NE // 2) + h, odd)
                pe.wait_ge(sem("xt_ready"), (r + 1) * (NE + 1))
                pe.wait_ge(sem("sw_ready"), r * NE + NE + 1)
                pe.wait_ge(sem("y_rows_ready"), r * NE + NE + 1)
                for t in range(3):
                    scatter(3 * (r * (NE + 1) + NE) + t, t, LAST_BANKS[t])

        @block.vector
        def _(dve):
            v = nc.vector
            own, roots = [0], [0]

            def step(ins):
                own[0] += 1
                ins.then_inc(sem("dve_steps"), 1)

            def settle():
                dve.wait_ge(sem("dve_steps"), own[0])

            def bc(ap, axis, n):
                ap = ap.unsqueeze(axis)
                shape = list(ap.shape)
                shape[axis] = n
                return ap.to_broadcast(shape)

            def inverse_root(dst):
                roots[0] += 1
                dve.wait_ge(sem("roots_ready"), roots[0])
                step(v.reciprocal(dst, dst))
                settle()

            def norm_rows(src, t, gain=None):
                n = ROWS[t]
                inverse_root(RS[0:n, t:t + 1])
                if gain is None:
                    ins = v.tensor_scalar(XN[0:n, t, :], src[0:n, t, :], RS[0:n, t:t + 1], None, ALU.mult)
                else:
                    ins = v.scalar_tensor_tensor(XN[0:n, t, :], src[0:n, t, :], RS[0:n, t:t + 1], gain[0:n],
                                                 ALU.mult, ALU.mult)
                ins.then_inc(sem("rows_normed"), 1)

            def keep_columns(n0, gain=None):
                for t in range(3):
                    n = ROWS[t]
                    dve.wait_ge(sem("rows_turned"), n0 + t + 1)
                    for b in range(2):
                        src = (PS[:, 2 * t + b, :] if t < 2 else PS[:, 4, 4 * b * n:4 * (b + 1) * n])
                        src = src.rearrange("p (k n) -> p k n", k=4)
                        dst = hT[:, 4 * b:4 * b + 4, COL0[t]:COL0[t] + n]
                        if gain is None:
                            ins = v.tensor_copy(dst, src)
                        else:
                            ins = v.tensor_tensor(dst, src, bc(colp(gain)[:, 4 * b:4 * b + 4], 2, n), ALU.mult)
                        if b:
                            ins.then_inc(sem("cols_ready"), 1)

            def head_norm(x, n, heads, width, gain, scratch):
                sq = scratch[0:n, 0:heads, :]
                step(v.tensor_tensor(sq, x, x, ALU.mult))
                settle()
                ss = SSH[0:n, 0:heads]
                v.tensor_reduce(ss, sq, AX.X, ALU.add).then_inc(sem("head_squares_ready"), 1)
                inverse_root(ss)
                step(v.tensor_tensor(x, x, bc(ss, 2, width), ALU.mult))
                settle()

            def rope(x, n, heads, cos, sin, scratch):
                r = ROPE_HALF
                x1, x2 = x[:, :, 0:r], x[:, :, r:2 * r]
                c, s = bc(cos, 1, heads), bc(sin, 1, heads)
                t = [scratch[0:n, 0:heads, i * r:(i + 1) * r] for i in range(4)]
                step(v.tensor_tensor(t[0], x1, c, ALU.mult))
                step(v.tensor_tensor(t[1], x2, s, ALU.mult))
                step(v.tensor_tensor(t[2], x2, c, ALU.mult))
                step(v.tensor_tensor(t[3], x1, s, ALU.mult))
                settle()
                step(v.tensor_tensor(x1, t[0], t[1], ALU.subtract))
                return v.tensor_tensor(x2, t[2], t[3], ALU.add)

            step(v.memset(SSQ, 1.0))
            dve.wait_ge(sem("dve_steps"), 1)
            v.memset(small[:, 8:512], 0.0).then_inc(sem("small_cleared"), 1)
            dve.wait_ge(sem("consts_loaded"), 32)
            for t in range(3):
                norm_rows(X, t)
            keep_columns(0, "norm_mix")
            dve.wait_ge(sem("params_loaded"), 32)

            dve.wait_ge(sem("small_cleared"), 1)
            for t in range(2):
                dve.wait_ge(sem("proj_kept"), 3 + t)
                x = QK[:, t].rearrange("p j h d -> p (j h) d")
                head_norm(x, P, 2 * AH, DH, None, QSC)
                g = RP[:, 0:2 * DH].rearrange("p (j d) -> p j d", j=2)
                step(v.tensor_tensor(QK[:, t], QK[:, t], bc(g, 2, AH), ALU.mult))
                settle()
                rope(x, P, 2 * AH, cst("cos")[:, 8 * t:8 * t + 8], cst("sin")[:, 8 * t:8 * t + 8],
                     QSC).then_inc(sem("qk_normed"), 1)
                dve.wait_ge(sem("qk_normed"), t + 1)
            dve.wait_ge(sem("dt_raw_ready"), 1)
            step(v.tensor_tensor(DTR[:, 0:2, :], PS[:, 1, 0:16].rearrange("p (t h) -> p t h", t=2),
                                 bc(rowp("dt_bias"), 1, 2), ALU.add))
            v.tensor_tensor(DTR[0:NTS, 2, :], PS[0:NTS, 1, 16:24], rowp("dt_bias", NTS),
                            ALU.add).then_inc(sem("dt_raw_kept"), 1)
            dve.wait_ge(sem("proj_kept"), 9)
            x = QKS[0:64]
            head_norm(x, 64, AH, DH, None, QSC)
            step(v.tensor_tensor(x, x, bc(colp("qk_gain_s")[0:64], 1, AH), ALU.mult))
            settle()
            rope(x, 64, AH, cst("cos_s"), cst("sin_s"), QSC).then_inc(sem("qk_normed"), 1)
            dve.wait_ge(sem("dt_raw_kept"), 1)
            settle()
            v.scalar_tensor_tensor(DT1, DTR, -1.0, DTR, ALU.mult, ALU.max).then_inc(sem("dt_abs_ready"), 1)

            w = colp("conv_w")
            for m in range(8):
                dve.wait_ge(sem("xbc_kept"), 2 * m + 2)
                if m == 0:
                    dve.wait_ge(sem("pool_cleared"), 1)
                    dve.wait_ge(sem("conv_state_turned"), 1)
                for i in range(4):
                    if i == 0:
                        step(v.tensor_scalar(UT[:, m, 0:SEQ], XP[:, m, 0:SEQ], w[:, m:m + 1], None, ALU.mult))
                    else:
                        ins = v.scalar_tensor_tensor(UT[:, m, 0:SEQ], XP[:, m, i:i + SEQ], w[:, 8 * i + m:8 * i + m + 1],
                                                     UT[:, m, 0:SEQ], ALU.mult, ALU.add)
                        if i == 3:
                            ins.then_inc(sem("conv_ready"), 1)
                        else:
                            step(ins)
                    settle()
            us = UT[:, :, SEQ:NTOK].rearrange("p m (b t) -> p m b t", b=NB)
            cv = CVS.rearrange("p m (b t) -> p m b t", b=NB)
            dve.wait_ge(sem("conv_state_kept"), 1)
            for i in range(4):
                wi = bc(bc(w[:, 8 * i:8 * i + 8], 2, NB), 3, NS)
                step(v.tensor_tensor(cv if i else us, XS[:, :, :, i:i + NS], wi, ALU.mult))
                settle()
                if i:
                    ins = v.tensor_tensor(us, us, cv, ALU.add)
                    if i < 3:
                        step(ins)
                        settle()
            ins.then_inc(sem("conv_ready"), 1)

            dve.wait_ge(sem("dt_log_ready"), 1)
            step(v.tensor_scalar(DTR[:, :, :], DTR[:, :, :], 0.0, None, ALU.max))
            settle()
            step(v.tensor_tensor(DTV[:, :, :], DTR[:, :, :], DT1[:, :, :], ALU.add))
            settle()
            v.scalar_tensor_tensor(DTA[:, :, :], DTV[:, :, :], -1.0, bc(AEX, 1, 3), ALU.mult,
                                   ALU.mult).then_inc(sem("dta_ready"), 1)

            dve.wait_ge(sem("window_stored"), 64)
            dve.wait_ge(sem("qk_turned"), 5)
            for i in range(2):
                nk = (i + 1) * P
                dve.wait_ge(sem("scores_ready"), i + 1)
                src = PS[:, 4 * (1 - i):4 * (1 - i) + 4, :].rearrange("p b (c k) -> p b c k", c=2)[:, :, :, 0:nk]
                dst = SCO[i].rearrange("p (b c) k -> p b c k", c=2)
                v.tensor_tensor(dst, src, bc(bc(cst(f"bias{i}"), 1, 2), 1, 4), ALU.add).then_inc(sem("scores_kept"), 1)
                dve.wait_ge(sem("scores_kept"), i + 1)
                step(v.tensor_reduce(MX[:, i, :], SCO[i], AX.X, ALU.max))
                settle()
                v.tensor_scalar(NMX[:, i, :], MX[:, i, :], -DH ** -0.5, None, ALU.mult).then_inc(sem("max_ready"), 1)
            for i in range(2):
                dve.wait_ge(sem("exp_ready"), i + 1)
                step(v.reciprocal(RDEN[:, i, :], DEN[:, i, :]))
                settle()
                v.tensor_tensor(SCO[i], SCO[i], bc(RDEN[:, i, :], 2, (i + 1) * P),
                                ALU.mult).then_inc(sem("probs_ready"), 1)
                if i == 0:
                    dve.wait_ge(sem("tails_ready"), 1)
                    for t in range(3):
                        n = ROWS[t]
                        b = (4, 6, 0)[t]
                        dve.wait_ge(sem("xb_turned"), t + 1)
                        v.tensor_copy(XB[0:n, t, 0:512], PS[0:n, b, :])
                        v.tensor_copy(XB[0:n, t, 512:768], PS[0:n, b + 1, 0:256]).then_inc(sem("xb_kept"), 1)
                    for t in range(3):
                        n = ROWS[t]
                        step(v.tensor_copy(ACU[0:n, t, :], PS[0:n, 1, CUM + 8 * t:CUM + 8 * t + 8]))
                    settle()
                    for t in range(3):
                        n = ROWS[t]
                        ins = v.tensor_tensor(DT1[0:n, t, :], PS[0:n, 1, CUM + 32 + 8 * t:CUM + 40 + 8 * t],
                                              ACU[0:n, t, :], ALU.subtract)
                    ins.then_inc(sem("acum_ready"), 1)

            dve.wait_ge(sem("dta_ready"), 1)
            for t in range(3):
                n = ROWS[t]
                dve.wait_ge(sem("xb_kept"), t + 1)
                if t == 0:
                    dve.wait_ge(sem("scores_ready"), 2)
                step(v.tensor_tensor(XD[0:n, t, :].rearrange("p (h d) -> p h d", h=SH),
                                     XB[0:n, t, 0:512].rearrange("p (h d) -> p h d", h=SH),
                                     bc(DTV[0:n, t, :], 2, DH), ALU.mult))
            dve.wait_ge(sem("ssd_exps_ready"), 1)
            dve.wait_ge(sem("probs_turned"), 2)
            settle()
            for t in range(3):
                n = ROWS[t]
                ins = v.tensor_tensor(XDE[0:n, t, :].rearrange("p (h d) -> p h d", h=SH),
                                      XD[0:n, t, :].rearrange("p (h d) -> p h d", h=SH),
                                      bc(TOE[0:n, t, :], 2, DH), ALU.mult)
            ins.then_inc(sem("xde_ready"), 1)
            for t in range(3):
                n = ROWS[t]
                tri = cst("tri") if t < 2 else cst("tri_s")
                dve.wait_ge(sem("st_ready"), t + 1)
                v.tensor_tensor(STM[0:n, :, 0:n], PS[0:n, 3, 0:256].rearrange("p (g q) -> p g q", g=2)[:, :, 0:n],
                                bc(tri, 1, 2), ALU.mult).then_inc(sem("st_kept"), 1)
                dve.wait_ge(sem("arow_ready"), t + 1)
                dve.wait_ge(sem("y_within_ready"), t)
                seg = SEG[0:n, :, 0:n].rearrange("p (a h) q -> p a h q", a=2)
                src = PS[0:n, 4:6, 0:4 * n].rearrange("p a (h q) -> p a h q", h=4)
                acu = bc(ACU[0:n, t, :].rearrange("p (a h) -> p a h", a=2), 3, n)
                v.tensor_tensor(seg, src, acu, ALU.subtract).then_inc(sem("seg_kept"), 1)
                dve.wait_ge(sem("seg_kept"), t + 1)
                v.tensor_scalar(SEG[0:n, :, 0:n], SEG[0:n, :, 0:n], 0.0, None, ALU.min).then_inc(sem("seg_ready"), 1)
                dve.wait_ge(sem("seg_exp_ready"), t + 1)
                dve.wait_ge(sem("st_kept"), t + 1)
                seg = SEG[0:n, :, 0:n].rearrange("p (g h) q -> p g h q", g=2)
                v.tensor_tensor(seg, seg, bc(STM[0:n, :, 0:n], 2, 4), ALU.mult).then_inc(sem("decay_ready"), 1)
                y = Y[0:n, t, :]
                yh = y.rearrange("p (h d) -> p h d", h=SH)
                if t == 0:
                    dve.wait_ge(sem("att_ready"), 2)
                step(v.tensor_tensor(yh, XB[0:n, t, 0:512].rearrange("p (h d) -> p h d", h=SH),
                                     bc(rowp("d_skip", n), 2, DH), ALU.mult))
                if t:
                    dve.wait_ge(sem("y_carried_ready"), t)
                    src = PS[0:n, 7, :]
                    if t == 2:
                        step(v.tensor_copy(YSQ[0:n], src))
                        for c in range(1, 4):
                            settle()
                            step(v.tensor_tensor(YSQ[0:n], PS[32 * c:32 * c + 32, 7, :], YSQ[0:n], ALU.add))
                        settle()
                        src = YSQ[0:n]
                    step(v.tensor_tensor(YSQ[0:n].rearrange("p (h d) -> p h d", h=SH),
                                         src.rearrange("p (h d) -> p h d", h=SH),
                                         bc(EAC[0:n, t, :], 2, DH), ALU.mult))
                    settle()
                    step(v.tensor_tensor(y, y, YSQ[0:n], ALU.add))
                settle()
                dve.wait_ge(sem("y_within_ready"), t + 1)
                v.tensor_tensor(y, y, PS[0:n, 6, :], ALU.add).then_inc(sem("y_kept"), 1)
                dve.wait_ge(sem("y_kept"), t + 1)
                dve.wait_ge(sem("z_silu_ready"), t + 1)
                v.tensor_tensor(y, y, Z[0:n, t, :], ALU.mult).then_inc(sem("y_gated"), 1)
                if t < 2:
                    dve.wait_ge(sem("chunk_state_ready"), t + 1)
                    if t == 1:
                        h3 = HT0.rearrange("p (h d) -> p h d", h=SH)
                        step(v.tensor_tensor(h3, h3, bc(DEC1, 2, DH), ALU.mult))
                        settle()
                        v.tensor_tensor(HT0, HT0, PS[:, 0, :], ALU.add).then_inc(sem("state_ready"), 1)
                    else:
                        v.tensor_copy(HT0, PS[:, 0, :]).then_inc(sem("state_ready"), 1)
                        dve.wait_ge(sem("state_ready"), 1)
            dve.wait_ge(sem("h0_scaled"), 4)
            H0 = slot("h0", NB, 4, NST)
            for n in range(8):
                p, half = n // 2, n % 2
                dve.wait_ge(sem("h_added"), n + 1)
                dst = H0[:, 4 * half:4 * half + 4, p, :]
                v.tensor_tensor(dst, dst, PS[:, 4 + n % 2, :].rearrange("p (b n) -> p b n", b=4),
                                ALU.add).then_inc(sem("h_updated"), 1)
            dve.wait_ge(sem("y_gated"), 3)
            inverse_root(RS)
            for t in range(3):
                n = ROWS[t]
                v.tensor_scalar(Y[0:n, t, :], Y[0:n, t, :], RS[0:n, t:t + 1], None,
                                ALU.mult).then_inc(sem("y_normed"), 1)
            for t in range(3):
                n = ROWS[t]
                dve.wait_ge(sem("y_turned"), t + 1)
                v.tensor_tensor(mixT[:, 4:8, COL0[t]:COL0[t] + n],
                                PS[:, t, 0:4 * n].rearrange("p (k n) -> p k n", k=4),
                                bc(colp("ssm_out_gain"), 2, n), ALU.mult).then_inc(sem("y_turned_kept"), 1)

            for g in range(2):
                dve.wait_ge(sem("scores_s_ready"), 2 * g + 2)
                if g:
                    dve.wait_ge(sem("att_s_ready"), 1)
                step(v.tensor_tensor(SS[:, 0:512], PS[:, 6, :], cst("bias_past")[:, 0:512], ALU.add))
                step(v.tensor_tensor(SS[:, 512:640], PS[:, 7, 0:P], cst("bias_past")[:, 512:640], ALU.add))
                v.tensor_tensor(SS[:, 640:672], PS[:, 7, P:P + NTS], cst(f"bias_new{g}"),
                                ALU.add).then_inc(sem("scores_s_kept"), 1)
                settle()
                dve.wait_ge(sem("scores_s_kept"), g + 1)
                step(v.tensor_reduce(MX[:, 2, g:g + 1], SS, AX.X, ALU.max))
                settle()
                v.tensor_scalar(NMX[:, 2, g:g + 1], MX[:, 2, g:g + 1], -DH ** -0.5, None,
                                ALU.mult).then_inc(sem("max_ready"), 1)
                dve.wait_ge(sem("exp_ready"), 3 + g)
                step(v.reciprocal(RDEN[:, 2, g:g + 1], DEN[:, 2, g:g + 1]))
                settle()
                step(v.tensor_scalar(HD, cst("head8"), RDEN[:, 2, g:g + 1], None, ALU.mult))
                settle()
                dve.wait_ge(sem("att_rows_ready"), g + 1)
                v.tensor_tensor(SS[:, 0:512].rearrange("p (h d) -> p h d", h=AH),
                                PS[:, 1, :].rearrange("p (h d) -> p h d", h=AH), bc(HD, 2, DH),
                                ALU.mult).then_inc(sem("att_rows_kept"), 1)

            def add_rows(n0, t):
                if t < 2:
                    for half in range(2):
                        dve.wait_ge(sem("mixed_ready"), n0 + 2 * t + half + 1)
                        x = X[:, t, half * 512:(half + 1) * 512]
                        ins = v.tensor_tensor(x, x, PS[:, 2 * t + half, :], ALU.add)
                        if not half:
                            step(ins)
                else:
                    dve.wait_ge(sem("mixed_ready"), n0 + 5)
                    for c in range(4):
                        x = X[0:NTS, 2, c * 256:(c + 1) * 256]
                        ins = v.tensor_tensor(x, PS[32 * c:32 * c + 32, 4, 0:256], x, ALU.add)
                        if c < 3:
                            step(ins)
                ins.then_inc(sem("residual_ready"), 1)
                settle()

            dve.wait_ge(sem("att_s_ready"), 2)
            dve.wait_ge(sem("mem_loaded"), 16)
            for t in range(2):
                norm_rows(MP, t)
            for t in range(3):
                add_rows(0, t)

            for t in range(2):
                dve.wait_ge(sem("hm_turned"), t + 1)
                for b in range(2):
                    ins = v.tensor_tensor(HMT[:, 4 * b:4 * b + 4, t * P:(t + 1) * P],
                                          PS[:, (5, 6, 7, 0)[2 * t + b], :].rearrange("p (k n) -> p k n", k=4),
                                          bc(colp("mem_in_gain")[:, 4 * b:4 * b + 4], 2, P), ALU.mult)
                ins.then_inc(sem("hm_kept"), 1)
            for t in range(3):
                norm_rows(X, t)
            dve.wait_ge(sem("mkv_kept"), 2)
            x = MK.rearrange("p t h d -> p (t h) d")
            head_norm(x, P, 8, MD, None, SMM[0].rearrange("p h (a d) -> p (h a) d", a=2))
            v.tensor_tensor(x, x, bc(rowp("mem_k_gain"), 1, 8), ALU.mult).then_inc(sem("mk_normed"), 1)

            keep_columns(3, "norm_mem")
            for t in range(3):
                n = ROWS[t]
                dve.wait_ge(sem("mq_kept"), t + 1)
                head_norm(MQ[0:n, t], n, MH, MD, None, SMM[0][:, :, 0:MD])
                v.tensor_tensor(MQ[0:n, t], MQ[0:n, t], bc(rowp("mem_q_gain", n), 1, MH),
                                ALU.mult).then_inc(sem("mq_normed"), 1)

            def memory_max(src, r, cols):
                step(v.tensor_reduce(MX[:, r, cols], src, AX.X, ALU.max))
                settle()
                v.tensor_scalar(NMX[:, r, cols], MX[:, r, cols], -MD ** -0.5, None,
                                ALU.mult).then_inc(sem("max_ready"), 1)

            for i in range(2):
                dve.wait_ge(sem("mscores_ready"), i + 1)
                b0 = (6, 0)[i]
                memory_max(PS[:, b0:b0 + 2, :].rearrange("p b (c k) -> p (b c) k", c=2), i, slice(0, 4))
            for i in range(2):
                dve.wait_ge(sem("exp_ready"), 5 + i)
                step(v.reciprocal(RDEN[:, i, 0:4], DEN[:, i, 0:4]))
                settle()
                v.tensor_tensor(SMM[i], SMM[i], bc(RDEN[:, i, 0:4], 2, NM), ALU.mult).then_inc(sem("probs_ready"), 1)
            for g in range(2):
                dve.wait_ge(sem("mscores_s_ready"), 2 * g + 2)
                c = slice(4 + g, 5 + g)
                memory_max(PS[:, 6, 0:NM], 0, c)
                dve.wait_ge(sem("exp_ready"), 7 + g)
                step(v.reciprocal(RDEN[:, 0, c], DEN[:, 0, c]))
                settle()
                step(v.tensor_scalar(HD[:, 0:MH], cst("head4"), RDEN[:, 0, c], None, ALU.mult))
                settle()
                dve.wait_ge(sem("att_rows_ready"), 3 + g)
                if g:
                    dve.wait_ge(sem("mo_ready"), 3)
                v.tensor_tensor(MOM.rearrange("p (h d) -> p h d", h=MH),
                                PS[:, 2, :].rearrange("p (h d) -> p h d", h=MH), bc(HD[:, 0:MH], 2, MD),
                                ALU.mult).then_inc(sem("att_rows_kept"), 1)
            for t in range(3):
                add_rows(5, t)
                if t:
                    norm_rows(X, t - 1, rowp("norm_ffn"))
            norm_rows(X, 2, rowp("norm_ffn"))

            def select(n, e):
                if n is not None:
                    dve.wait_ge(sem("gathered"), n)
                v.tensor_tensor(SEL, bc(cst("iota64"), 1, 3), bc(POSM[:, bass.ds(e, 1), :].rearrange("p a t -> p (a t)"), 2, SLOTS),
                                ALU.is_equal).then_inc(sem("sel_ready"), 1)

            def expert_row(e):
                v.tensor_scalar(EROW[0:NE, :], cst("ones")[0:NE, 0:SLOTS], cst("expert")[0:NE, bass.ds(e, 1)], None,
                                ALU.mult).then_inc(sem("erow_ready"), 1)

            keep_columns(6)
            v.memset(YB, 0.0).then_inc(sem("y_rows_ready"), 1)
            v.memset(SW[:, 0:P], 0.0).then_inc(sem("sw_ready"), 1)
            v.memset(SW[:, P:3 * P], 0.0).then_inc(sem("sw_cleared"), 1)
            v.memset(AC, 0.0).then_inc(sem("act_ready"), 1)
            step(v.memset(LG, 0.0))
            step(v.memset(POSM, -1.0))
            step(v.memset(GW, 0.0))
            expert_row(0)
            dve.wait_ge(sem("logits_ready"), 2)
            settle()
            br = rowp("b_router")
            step(v.tensor_tensor(LG[:, 0:2, :], PS[:, 5, 0:64].rearrange("p (t e) -> p t e", t=2), bc(br, 1, 2),
                                 ALU.add))
            step(v.tensor_tensor(LG[0:NTS, 2, :], PS[0:NTS, 5, 64:96], br[0:NTS], ALU.add))
            settle()
            for t in range(3):
                step(v.max(TOPV[:, t, :], LG[:, t, :]))
            settle()
            for t in range(3):
                step(v.max_index(top_i[:, t, :], TOPV[:, t, :], LG[:, t, :]))
            step(v.tensor_tensor(TOPW, TOPV[:, :, 0:TOPK], bc(TOPV[:, :, 0], 2, TOPK), ALU.subtract))
            settle()
            v.tensor_copy(TOPF[:, :, :], top_i[:, :, :]).then_inc(sem("top_ready"), 1)
            dve.wait_ge(sem("top_exp_ready"), 1)
            dve.wait_ge(sem("top_ready"), 1)
            step(v.tensor_reduce(TS[:, 0:3], TOPW, AX.X, ALU.add))
            settle()
            step(v.reciprocal(TS[:, 3:6], TS[:, 0:3]))
            settle()
            step(v.tensor_tensor(TOPW, TOPW, bc(TS[:, 3:6], 2, TOPK), ALU.mult))
            iota = bc(bc(cst("iota32"), 1, TOPK), 1, 3)
            step(v.tensor_tensor(OH4, iota, bc(TOPF[:, :, 0:TOPK], 3, NE), ALU.is_equal))
            settle()
            v.tensor_reduce(MSK, OH4.rearrange("p t j e -> p t e j"), AX.X, ALU.add).then_inc(sem("routed"), 1)
            dve.wait_ge(sem("routed"), 1)
            step(v.tensor_tensor(OH4, OH4, bc(TOPW, 3, NE), ALU.mult))
            settle()
            v.tensor_reduce(GW[:, 0:NE, :].rearrange("p e t -> p t e"), OH4.rearrange("p t j e -> p t e j"), AX.X,
                            ALU.add).then_inc(sem("gw_ready"), 1)
            dve.wait_ge(sem("ranks_ready"), 1)
            pos = POSM[:, 0:NE, :].rearrange("p e t -> p t e")
            step(v.scalar_tensor_tensor(pos[:, 0:2], MSK[:, 0:2], -1024.0,
                                        PS[:, 6, 0:64].rearrange("p (t e) -> p t e", t=2), ALU.mult, ALU.add))
            step(v.scalar_tensor_tensor(pos[0:NTS, 2], MSK[0:NTS, 2], -1024.0, PS[0:NTS, 6, 64:96], ALU.mult, ALU.add))
            v.tensor_reduce(CNT[:, 0:1], PS[:, 6, 96:128], AX.X, ALU.max).then_inc(sem("scatter_added"), 1)
            dve.wait_ge(sem("scatter_added"), 1)
            settle()
            step(v.tensor_scalar(POSM[:, 0:NE, :], POSM[:, 0:NE, :], 1024.0, None, ALU.add))
            settle()
            select(None, 0)
            step(v.tensor_scalar(TS[:, 0:NPASS_MAX - 1], cst("thr"), CNT[:, 0:1], None, ALU.is_lt))
            settle()
            step(v.tensor_reduce(NPF, TS[:, 0:NPASS_MAX - 1], AX.X, ALU.add))
            settle()
            v.tensor_scalar(npass_i[:, 0:1], NPF, 1.0, None, ALU.add).then_inc(sem("npass_ready"), 1)
            def add_scattered(t, b):
                n = ROWS[t]
                x = X[0:n, t, :].rearrange("p (b c) -> p b c", b=2)
                v.tensor_tensor(x, x, PS[0:n, b:b + 2, :], ALU.add).then_inc(sem("scatter_added"), 1)

            dve.wait_ge(sem("npass_ready"), 1)
            npass = dve.value_load(npass_i[0:1, 0:1], min_val=1, max_val=NPASS_MAX)
            with dve.Fori(0, npass) as r:
                with dve.Fori(0, NE) as e:
                    it = r * NE + e
                    q = r * (NE + 1) + e
                    select(q + 1, e + 1)
                    def add_rows(t):
                        dve.wait_ge(sem("scattered"), 3 * q + t + 1)
                        add_scattered(t, 6)

                    add_rows(0)
                    expert_row(e + 1)
                    add_rows(1)
                    add_rows(2)
                    dve.wait_ge(sem("gate_up_ready"), it + 1)
                    gu = PS[:, 0:2, :].rearrange("p b (c two) -> p b c two", two=2)
                    v.tensor_scalar(G1, gu[:, :, :, 0], 7.0, None, ALU.min).then_inc(sem("gate_ready"), 1)
                    v.tensor_scalar(U1, gu[:, :, :, 1], 7.0, -7.0, ALU.min, ALU.max).then_inc(sem("expert_steps"), 1)
                    dve.wait_ge(sem("sigmoid_ready"), it + 1)
                    v.tensor_tensor(SG, SG, G1, ALU.mult).then_inc(sem("expert_steps"), 1)
                    dve.wait_ge(sem("expert_steps"), 3 * it + 2)
                    v.scalar_tensor_tensor(AC, U1.rearrange("p b c -> p (b c)"), 1.0, SG.rearrange("p b c -> p (b c)"),
                                           ALU.add, ALU.mult).then_inc(sem("act_ready"), 1)
                    posb = bc(bc(POSM[:, bass.ds(e, 1), :].rearrange("p a t -> p (a t)"), 2, 2), 3, SLOTS)
                    gwb = bc(bc(GW[:, bass.ds(e, 1), :].rearrange("p a t -> p (a t)"), 2, 2), 3, SLOTS)
                    v.tensor_tensor(SELW, bc(bc(cst("iota64"), 1, 2), 1, 3), posb,
                                    ALU.is_equal).then_inc(sem("expert_steps"), 1)
                    dve.wait_ge(sem("expert_steps"), 3 * it + 3)
                    v.tensor_tensor(SELW, SELW, gwb, ALU.mult).then_inc(sem("selw_ready"), 1)
                last = 3 * (r * (NE + 1) + NE)
                for t in range(3):
                    dve.wait_ge(sem("scattered"), last + t + 1)
                    add_scattered(t, LAST_BANKS[t][0])
                dve.wait_ge(sem("gathered"), (r + 1) * (NE + 1))
                v.tensor_scalar(POSM, POSM, float(SLOTS), None, ALU.subtract).then_inc(sem("slots_moved"), 1)
                dve.wait_ge(sem("slots_moved"), r + 1)
                dve.wait_ge(sem("scatter_added"), last + 4)
                v.memset(SW, 0.0).then_inc(sem("sw_cleared"), 1)
                select(None, 0)

        @block.scalar
        def _(act):
            s = nc.scalar

            heads_rooted = [0]

            def root(dst, sums, width):
                s.activation(dst, sums, ACT.Sqrt, scale=1.0 / width, bias=cst("eps")[0:dst.shape[0], :]
                             ).then_inc(sem("roots_ready"), 1)

            def root_heads(rows, heads, width):
                heads_rooted[0] += 1
                act.wait_ge(sem("head_squares_ready"), heads_rooted[0])
                root(SSH[0:rows, 0:heads], SSH[0:rows, 0:heads], width)

            rows_squared = [0]

            def square_rows(src, t):
                n = ROWS[t]
                rows_squared[0] += 1
                s.activation(XN[0:n, t, :], src[0:n, t, :], ACT.Square,
                             accum_out=SSQ[0:n, t:t + 1]).then_inc(sem("rows_squared"), 1)
                act.wait_ge(sem("rows_squared"), rows_squared[0])
                root(RS[0:n, t:t + 1], SSQ[0:n, t:t + 1], D)

            def square_y(t):
                n = ROWS[t]
                s.activation(Z[0:n, t, :], Y[0:n, t, :], ACT.Square,
                             accum_out=SSQ[0:n, t:t + 1]).then_inc(sem("y_squared"), 1)

            act.wait_ge(sem("dve_steps"), 1)
            act.wait_ge(sem("x_first_loaded"), 16)
            act.wait_ge(sem("consts_loaded"), 32)
            for t in range(3):
                if t == 1:
                    act.wait_ge(sem("x_loaded"), 32)
                square_rows(X, t)
            act.wait_ge(sem("conv_state_turned"), 1)
            s.copy(XS[:, :, :, 0:3], PS[:, 5, 0:192].rearrange("p (m b i) -> p m b i", m=8,
                                                               b=NB)).then_inc(sem("conv_state_kept"), 1)
            act.wait_ge(sem("params_loaded"), 32)
            act.wait_ge(sem("small_cleared"), 1)
            s.activation(AEX, rowp("a_log"), ACT.Exp)
            for i in range(8):
                g, t = i // 2, i % 2
                act.wait_ge(sem("proj_ready"), i + 1)
                dst = (QK[:, t, 0].rearrange("p h d -> p (h d)"), QK[:, t, 1].rearrange("p h d -> p (h d)"),
                       V[:, t, :], Z[:, t, :])[g]
                s.copy(dst, PS[:, i, :]).then_inc(sem("proj_kept"), 1)
                if i in (5, 7):
                    root_heads(P, 2 * AH, DH)
            act.wait_ge(sem("proj_ready"), 9)
            s.copy(QKS[0:64].rearrange("p h d -> p (h d)"), PS[0:64, 0, :]).then_inc(sem("proj_kept"), 1)
            s.copy(V[0:NTS, 2, :], PS[64:96, 0, :]).then_inc(sem("proj_kept"), 1)
            s.copy(Z[0:NTS, 2, :], PS[96:128, 0, :]).then_inc(sem("proj_kept"), 1)

            def silu_conv(m, tokens, convolved):
                act.wait_ge(sem("conv_ready"), convolved)
                s.activation(UT[:, m, tokens], UT[:, m, tokens], ACT.Silu,
                             bias=colp("conv_b")[:, m:m + 1]).then_inc(sem("conv_silu_ready"), 1)

            for m in range(8):
                bank = (2 + m) % 8
                act.wait_ge(sem("xbc_ready"), m + 1)
                s.copy(XP[:, m, 3:3 + SEQ], PS[:, bank, 0:SEQ]).then_inc(sem("xbc_kept"), 1)
                s.copy(XS[:, m, :, 3:3 + NS], PS[:, bank, SEQ:NTOK].rearrange("p (b t) -> p b t", b=NB)
                       ).then_inc(sem("xbc_kept"), 1)
                if m == 1:
                    root_heads(64, AH, DH)
                elif m == 2:
                    act.wait_ge(sem("dt_abs_ready"), 1)
                    s.activation(DT1[:, :, :], DT1[:, :, :], ACT.Exp, scale=-1.0).then_inc(sem("dt_exp_ready"), 1)
                elif m == 3:
                    act.wait_ge(sem("dt_exp_ready"), 1)
                    s.activation(DT1[:, :, :], DT1[:, :, :], ACT.Ln,
                                 bias=cst("ones")[:, 0:1]).then_inc(sem("dt_log_ready"), 1)
                elif m == 4:
                    act.wait_ge(sem("proj_kept"), 11)
                    for t in range(3):
                        n = ROWS[t]
                        s.activation(Z[0:n, t, :], Z[0:n, t, :], ACT.Silu).then_inc(sem("z_silu_ready"), 1)
                elif m >= 5:
                    for c in ((0, 1, 2), (3, 4), (5,))[m - 5]:
                        silu_conv(c, slice(0, SEQ), c + 1)
            for n in range(4):
                t, j = n // 2, n % 2
                act.wait_ge(sem("qk_turned"), n + 1)
                s.copy((qT, kT)[j][:, :, t * P:(t + 1) * P],
                       PS[:, n, :].rearrange("p (c n) -> p c n", c=4)).then_inc(sem("qk_kept"), 1)
            act.wait_ge(sem("qk_turned"), 5)
            act.wait_ge(sem("pool_cleared"), 2)
            s.copy(kTs, PS[:, 5, 0:P].rearrange("p (c n) -> p c n", c=4)).then_inc(sem("qk_kept"), 1)
            for e in range(2):
                r = slice(64 * e, 64 * e + 64)
                dst = arena[r, 4 * e:4 * e + 1056].rearrange("p (c x) -> p c x", c=4)[:, :, 0:256]
                dst = dst.rearrange("p c (b u) -> p c b u", b=NB)[:, :, :, 0:NS]
                s.copy(dst, PS[r, 4, 0:P].rearrange("p (c b t) -> p c b t", c=4, b=NB)).then_inc(sem("qk_kept"), 1)
            act.wait_ge(sem("tail_rows_ready"), 1)
            for j in range(2):
                s.copy(CONVO[0:27, 512 * j:512 * j + 512], PS[0:27, 6 + j, :]).then_inc(sem("tail_rows_kept"), 1)
            for m in (6, 7):
                silu_conv(m, slice(0, SEQ), m + 1)
            for m in range(8):
                silu_conv(m, slice(SEQ, NTOK), 9)
            for i in range(2):
                nk = (i + 1) * P
                act.wait_ge(sem("max_ready"), i + 1)
                for h in range(8):
                    ins = s.activation(SCO[i][:, h, :], SCO[i][:, h, :], ACT.Exp, bias=NMX[:, i, h:h + 1],
                                       scale=DH ** -0.5, accum_out=DEN[:, i, h:h + 1])
                ins.then_inc(sem("exp_ready"), 1)
            act.wait_ge(sem("conv_stored"), 32)
            for i in range(2):
                act.wait_ge(sem("probs_turned"), i + 1)
                banks = (2, 3, 5, 6)
                for j in range(i + 1):
                    for c in range(2):
                        ins = s.copy(PT[:, j, 4 * c:4 * c + 4, :],
                                     PS[:, banks[2 * j + c], :].rearrange("p (h q) -> p h q", h=4))
                ins.then_inc(sem("probs_kept"), 1)
                if i == 0:
                    act.wait_ge(sem("acum_ready"), 1)
                    s.activation(TOE, DT1, ACT.Exp)
                    s.activation(EAC, ACU, ACT.Exp)
                    s.activation(DEC1, PS[:, 1, CUM + 40:CUM + 48], ACT.Exp)
                    s.activation(DECS, PS[:, 1, CUM + 64:CUM + 96].rearrange("p (c b) -> p c b", c=4),
                                 ACT.Exp).then_inc(sem("ssd_exps_ready"), 1)
                act.wait_ge(sem("att_ready"), i + 1)
                s.copy(mixT[:, 0:4, i * P:(i + 1) * P],
                       PS[:, (4, 7)[i], :].rearrange("p (c q) -> p c q", c=4)).then_inc(sem("att_kept"), 1)
            H0T = slot("scratch", NB, 512)
            act.wait_ge(sem("proj_ready"), 9)
            for t in range(3):
                n = ROWS[t]
                if t < 2:
                    for b in range(4 * t, 4 * t + 4):
                        act.wait_ge(sem("h0_turned"), b + 1)
                        s.copy(H0T[:, b, :], PS[:, 1 + b % 2, :]).then_inc(sem("h0t_kept"), 1)
                act.wait_ge(sem("seg_ready"), t + 1)
                s.activation(SEG[0:n, :, 0:n], SEG[0:n, :, 0:n], ACT.Exp).then_inc(sem("seg_exp_ready"), 1)
                if t:
                    act.wait_ge(sem("y_gated"), t)
                    square_y(t - 1)
            act.wait_ge(sem("y_gated"), 3)
            square_y(2)
            act.wait_ge(sem("y_squared"), 3)
            root(RS, SSQ, 512)
            act.wait_ge(sem("state_rows_ready"), 1)
            s.copy(HOUT, PS[:, 2, :].rearrange("p (c n) -> p c n", c=4)).then_inc(sem("state_rows_kept"), 1)
            act.wait_ge(sem("h_added"), 8)
            for g in range(2):
                for n in range(20 * g, 20 * g + 20):
                    b, j = n // 5 % 2, n % 5
                    act.wait_ge(sem("kt_turned"), n + 1)
                    s.copy(KTB[:, b, :, j * P:(j + 1) * P],
                           PS[:, 3 + n % 3, :].rearrange("p (c k) -> p c k", c=4)).then_inc(sem("kt_kept"), 1)
                act.wait_ge(sem("max_ready"), 3 + g)
                s.activation(SS, SS, ACT.Exp, bias=NMX[:, 2, g:g + 1], scale=DH ** -0.5,
                             accum_out=DEN[:, 2, g:g + 1]).then_inc(sem("exp_ready"), 1)
                act.wait_ge(sem("probs_turned"), 3 + g)
                s.copy(PTS[:, 0:4, :], PS[:, 3, :].rearrange("p (j r) -> p j r", j=4))
                s.copy(PTS[:, 4, :], PS[:, 4, 0:P]).then_inc(sem("probs_s_kept"), 1)
                s.copy(PTS[0:NTS, 5, :], PS[0:NTS, 4, P:2 * P]).then_inc(sem("probs_s_kept"), 1)
            act.wait_ge(sem("att_s_ready"), 2)
            s.copy(mixT[:, 0:4, SEQ:NTOK],
                   PS[:, 2, 0:P].rearrange("p (c n) -> p c n", c=4)).then_inc(sem("mix_ready"), 1)
            act.wait_ge(sem("mem_loaded"), 16)
            for t in range(2):
                square_rows(MP, t)
            act.wait_ge(sem("hm_turned"), 2)
            for t in range(3):
                act.wait_ge(sem("residual_ready"), t + 1)
                square_rows(X, t)
            for n in range(4):
                act.wait_ge(sem("mkv_ready"), n + 1)
                dst = MK[:, n % 2].rearrange("p h d -> p (h d)") if n < 2 else MV[:, n % 2, :]
                s.copy(dst, PS[:, MKV_BANKS[n], :]).then_inc(sem("mkv_kept"), 1)
                if n == 1:
                    root_heads(P, 8, MD)
            for t in range(3):
                n = ROWS[t]
                act.wait_ge(sem("mq_ready"), t + 1)
                if t < 2:
                    s.copy(MQ[0:n, t].rearrange("p h d -> p (h d)"), PS[0:n, t, :]).then_inc(sem("mq_kept"), 1)
                else:
                    for h in range(MH):
                        ins = s.copy(MQ[0:n, t, h, :], PS[32 * h:32 * h + 32, 2, 0:MD])
                    ins.then_inc(sem("mq_kept"), 1)
                    for j in range(2):
                        act.wait_ge(sem("mk_turned"), j + 1)
                        s.copy(MKT[:, :, j * P:(j + 1) * P],
                               PS[:, 6 + j, :].rearrange("p (h n) -> p h n", h=MH)).then_inc(sem("mk_turned_kept"), 1)
                root_heads(n, MH, MD)
            for t in range(2):
                act.wait_ge(sem("mq_turned"), t + 1)
                s.copy(QMT[:, :, t * P:(t + 1) * P],
                       PS[:, 3 + t, :].rearrange("p (h n) -> p h n", h=MH)).then_inc(sem("mq_turned_kept"), 1)
            act.wait_ge(sem("mq_turned"), 3)
            act.wait_ge(sem("pool_cleared"), 4)
            for h in range(MH):
                s.copy(QMB[:, h, :, 4 * h:4 * h + 4],
                       PS[:, 5, h * NTS:(h + 1) * NTS].rearrange("p (b t) -> p b t", b=NB)
                       ).then_inc(sem("mq_turned_kept"), 1)
            for i in range(2):
                act.wait_ge(sem("max_ready"), 5 + i)
                if i:
                    act.wait_ge(sem("mq_turned"), 3)
                for h in range(MH):
                    ins = s.activation(SMM[i][:, h, :], PS[:, (6, 0)[i] + h // 2, h % 2 * 256:(h % 2 + 1) * 256],
                                       ACT.Exp, bias=NMX[:, i, h:h + 1], scale=MD ** -0.5,
                                       accum_out=DEN[:, i, h:h + 1])
                ins.then_inc(sem("exp_ready"), 1)
            for i in range(2):
                act.wait_ge(sem("probs_turned"), 5 + i)
                for j in range(2):
                    s.copy(PTM[:, j], PS[:, 2 + 2 * i + j, :].rearrange("p (h q) -> p h q", h=MH)
                           ).then_inc(sem("mprobs_kept"), 1)
                act.wait_ge(sem("mo_ready"), i + 1)
                s.copy(OT[:, :, i * P:(i + 1) * P],
                       PS[:, 2 + 2 * i, :].rearrange("p (h q) -> p h q", h=MH)).then_inc(sem("mo_kept"), 1)
            for g in range(2):
                for n in range(8 * g, 8 * g + 8):
                    b, j = n // 2 % 2, n % 2
                    act.wait_ge(sem("ktm_turned"), n + 1)
                    s.copy(KTM[:, b, :, j * P:(j + 1) * P],
                           PS[:, (3, 5)[n % 2], :].rearrange("p (h k) -> p h k", h=MH)).then_inc(sem("ktm_kept"), 1)
                act.wait_ge(sem("max_ready"), 7 + g)
                s.activation(SS2, PS[:, 6, 0:NM], ACT.Exp, bias=NMX[:, 0, 4 + g:5 + g], scale=MD ** -0.5,
                             accum_out=DEN[:, 0, 4 + g:5 + g]).then_inc(sem("exp_ready"), 1)
                act.wait_ge(sem("probs_turned"), 7 + g)
                s.copy(PTM[:, 0, 0:2, :], PS[:, 7, 0:256].rearrange("p (j r) -> p j r", j=2)
                       ).then_inc(sem("mprobs_kept"), 1)
            act.wait_ge(sem("mo_ready"), 4)
            s.copy(OT[:, :, SEQ:NTOK], PS[:, 4, 0:P].rearrange("p (h n) -> p h n", h=MH)).then_inc(sem("mo_kept"), 1)
            act.wait_ge(sem("rows_turned"), 6)
            for t in range(3):
                act.wait_ge(sem("residual_ready"), 4 + t)
                square_rows(X, t)
            act.wait_ge(sem("logits_ready"), 1)
            s.copy(LP, PS[:, 5, 0:NTOK]).then_inc(sem("logit_parts_kept"), 1)
            act.wait_ge(sem("top_ready"), 1)
            s.activation(TOPW, TOPW, ACT.Exp).then_inc(sem("top_exp_ready"), 1)

            def keep_gathered(n):
                act.wait_ge(sem("gathered"), n + 1)
                s.copy(XG, PS[:, 2, :]).then_inc(sem("xg_kept"), 1)

            def keep_columns(n):
                act.wait_ge(sem("xg_turned"), n + 1)
                s.copy(XT.rearrange("p (h c) s -> p c h s", h=2),
                       PS[:, 2, :].rearrange("p (c h s) -> p c h s", c=4, h=2)).then_inc(sem("xt_ready"), 1)

            act.wait_ge(sem("npass_ready"), 1)
            npass = act.value_load(npass_i[0:1, 0:1], min_val=1, max_val=NPASS_MAX)
            with act.Fori(0, npass) as r:
                keep_gathered(r * (NE + 1))
                keep_columns(r * (NE + 1))
                with act.Fori(0, NE) as e:
                    it = r * NE + e
                    q = r * (NE + 1) + e
                    act.wait_ge(sem("gate_ready"), it + 1)
                    s.activation(SG, G1, ACT.Sigmoid, scale=1.702).then_inc(sem("sigmoid_ready"), 1)
                    keep_gathered(q + 1)
                    act.wait_ge(sem("act_turned"), it + 1)
                    s.copy(AT, PS[:, 4, :].rearrange("p (c n) -> p c n", c=4)).then_inc(sem("at_ready"), 1)
                    act.wait_ge(sem("sw_turned"), it + 1)
                    s.copy(SW[:, 0:NTOK], PS[:, 3, 0:NTOK]).then_inc(sem("sw_ready"), 1)
                    keep_columns(q + 1)
                    act.wait_ge(sem("down_ready"), it + 1)
                    s.copy(YB, PS[:, 5, :]).then_inc(sem("y_rows_ready"), 1)

        @block.gpsimd
        def _(pool):
            g_ = nc.gpsimd

            def bc(ap, axis, n):
                ap = ap.unsqueeze(axis)
                shape = list(ap.shape)
                shape[axis] = n
                return ap.to_broadcast(shape)

            g_.memset(XP[:, :, 0:3], 0.0).then_inc(sem("pool_cleared"), 1)
            pool.wait_ge(sem("proj_kept"), 11)
            pool.wait_ge(sem("qk_normed"), 3)
            pool.dma_start(o["win_k_prompt"][0, 0].rearrange("(t p) h d -> p t (h d)", p=P),
                           QK[:, :, 1].rearrange("p t h d -> p t (h d)")).then_inc(sem("window_stored"), 16)
            pool.dma_start(o["win_v_prompt"][0, 0].rearrange("(t p) h d -> p t (h d)", p=P),
                           V[:, 0:2, :]).then_inc(sem("window_stored"), 16)
            pool.dma_start(o["win_k_sample"].rearrange("l b t h d -> (l b t) (h d)"),
                           QKS[32:64].rearrange("p h d -> p (h d)")).then_inc(sem("window_stored"), 16)
            pool.dma_start(o["win_v_sample"].rearrange("l b t h d -> (l b t) (h d)"),
                           V[0:NTS, 2, :]).then_inc(sem("window_stored"), 16)
            for m in range(8):
                pool.wait_ge(sem("xbc_kept"), 2 * m + 2)
                g_.tensor_copy(TAIL[:, m, 0:24].rearrange("p (b i) -> p b i", b=NB), XS[:, m, :, NS:NS + 3])
            g_.tensor_copy(TAIL[:, :, 24:27], XP[:, :, SEQ:SEQ + 3]).then_inc(sem("tails_ready"), 1)
            pool.wait_ge(sem("xbc_ready"), 8)
            g_.memset(arena[:, 0:1024], 0.0).then_inc(sem("pool_cleared"), 1)
            pool.wait_ge(sem("tail_rows_kept"), 2)
            pool.dma_start(o["conv_sample"].rearrange("l b i c -> (l b i) c"), CONVO[0:24]
                           ).then_inc(sem("conv_stored"), 16)
            pool.dma_start(o["conv_prompt"].rearrange("l b i c -> (l b i) c"), CONVO[24:27]
                           ).then_inc(sem("conv_stored"), 16)
            pool.wait_ge(sem("window_stored"), 64)
            pool.wait_ge(sem("qk_turned"), 5)
            pool.wait_ge(sem("dta_ready"), 1)
            g_.tensor_copy(DREP[0:NTS], bc(DTA[0:NTS, 2, :], 2, DH)).then_inc(sem("drep_ready"), 1)
            pool.wait_ge(sem("cumulated"), 1)
            for t in range(3):
                n = ROWS[t]
                pool.wait_ge(sem("arow_ready"), t)
                tri = cst("tri") if t < 2 else cst("tri_s")
                g_.tensor_tensor(DTRI[0:n, :, 0:n], bc(DTA[0:n, t, :], 2, n), bc(tri, 1, SH),
                                 ALU.mult).then_inc(sem("dtri_ready"), 1)
                if t == 0:
                    pool.wait_ge(sem("probs_turned"), 2)
                    g_.memset(arena[:, 4736:5248], 0.0).then_inc(sem("pool_cleared"), 1)
                    pool.wait_ge(sem("pool_cleared"), 3)
                    pool.wait_ge(sem("conv_silu_ready"), 16)
                    for g in range(2):
                        dst = arena[:, 4736 + 256 * g:4736 + 256 * g + 288].rearrange("p (b x) -> p b x", x=36)[:, :, 0:NS]
                        ins = g_.tensor_copy(dst, UT[:, 6 + g, SEQ:NTOK].rearrange("p (b t) -> p b t", b=NB))
                    ins.then_inc(sem("cm_ready"), 1)
                if t == 1:
                    pool.wait_ge(sem("h0_turned"), NB)
                    pool.wait_ge(sem("ssd_exps_ready"), 1)
                    H0 = slot("h0", NB, 4, NST)
                    for p in range(4):
                        g_.tensor_tensor(H0[:, :, p, :], H0[:, :, p, :], bc(DECS[:, p, :], 2, NST),
                                         ALU.mult).then_inc(sem("h0_scaled"), 1)
            pool.wait_ge(sem("st_ready"), 3)
            pool.wait_ge(sem("y_carried_ready"), 1)
            pool.wait_ge(sem("xb_kept"), 3)
            for g in range(2):
                ins = g_.tensor_tensor(BNM[0:NTS, g], bc(XB[0:NTS, 2, 512 + g * P:512 + (g + 1) * P], 1, NB),
                                       bc(cst("bsel"), 2, P), ALU.mult)
            ins.then_inc(sem("bnm_ready"), 1)
            pool.wait_ge(sem("state_rows_kept"), 1)
            pool.dma_start(o["ssm_prompt"][0, 0].rearrange("(c h) d n -> (h d) c n", h=2), HOUT
                           ).then_inc(sem("prompt_state_stored"), 16)
            pool.wait_ge(sem("h_updated"), 8)
            H0 = slot("h0", NB * 4, NST)
            pool.dma_start(o["ssm_sample"][0].rearrange("b (c h) d n -> (h d) (b c) n", h=2), H0
                           ).then_inc(sem("states_stored"), 16)
            pool.dma_start(MP, a["mem_prompt"][0].rearrange("(t p) d -> p t d", p=P)).then_inc(sem("mem_loaded"), 16)
            pool.wait_ge(sem("att_s_ready"), 2)
            g_.memset(QMB, 0.0).then_inc(sem("pool_cleared"), 1)
            pool.wait_ge(sem("mkv_kept"), 4)
            pool.dma_start(o["mem_v_prompt"][0, 0].rearrange("(t p) h d -> p t (h d)", p=P), MV
                           ).then_inc(sem("mem_stored"), 16)
            pool.wait_ge(sem("mk_normed"), 1)
            pool.dma_start(o["mem_k_prompt"][0, 0].rearrange("(t p) h d -> p t (h d)", p=P),
                           MK.rearrange("p t h d -> p t (h d)")).then_inc(sem("mem_stored"), 16)
            pool.wait_ge(sem("mk_turned"), 2)
            pool.wait_ge(sem("mem_stored"), 32)
            pool.dma_start(BGU[0:NE], a["b_gate_up"].rearrange("l e f -> (l e) f")
                           ).then_inc(sem("expert_biases_loaded"), 16)
            pool.dma_start(BD[0:NE], a["b_down"].rearrange("l e f -> (l e) f")
                           ).then_inc(sem("expert_biases_loaded"), 16)
            pool.wait_ge(sem("prompt_state_stored"), 16)

        @block.sync
        def _(sp):
            sp.dma_start(X[:, 0, :], a["x_prompt"][0, 0:P]).then_inc(sem("x_first_loaded"), 16)
            sp.dma_start(CN[:, 0:P + 1], a["consts"][:, 0:P + 1]).then_inc(sem("consts_loaded"), 16)
            sp.dma_start(CP[:, :], a["col_params"]).then_inc(sem("consts_loaded"), 16)
            sp.dma_start(X[:, 1, :], a["x_prompt"][0, P:SEQ]).then_inc(sem("x_loaded"), 16)
            sp.dma_start(X[0:NTS, 2, :], a["x_sample"].rearrange("b t d -> (b t) d")).then_inc(sem("x_loaded"), 16)
            sp.dma_start(SC[0:24], a["state_conv"].rearrange("l b i c -> (l b i) c")).then_inc(sem("state_conv_loaded"), 16)
            w_in = a["w_in"][0].rearrange("(k p) n -> p k n", p=P)
            in_col = dict(q=0, k=512, v=1024, z=1536, xbc0=2056, xbc1=2568)

            def load(name):
                u = U[name]
                if name in in_col:
                    dst, src = slot(name, KT, 512), w_in[:, :, in_col[name]:in_col[name] + 512]
                elif name == "h0":
                    dst, src = slot(name, NB * 4, NST), a["state_ssm"][0].rearrange("b (c h) d n -> (h d) (b c) n", h=2)
                elif name[0] in "KV":
                    cache = a["cache_win_k" if name[0] == "K" else "cache_win_v"]
                    c = cache[0, int(name[1:])].rearrange("s h d -> s (h d)")
                    old = c[0:512].rearrange("(i r) d -> i r d", r=16)
                    s_old = slot(name, 5, 512)[:, 0, :]
                    sp.dma_start(s_old, old[:, 0:4, :]).then_inc(sem(f"slot{u % RING}_loaded"), 16)
                    dst = slot(name, 5 * 512)[:, 512:2560]
                    src = c[PAST - 512:PAST].rearrange("(p j) d -> p (j d)", j=4)
                    sp.dma_start(dst, src).then_inc(sem(f"slot{u % RING}_loaded"), 16)
                    return
                elif name.startswith("wout"):
                    half = int(name[4])
                    dst = slot(name, KT, 512)
                    src = a["w_out"][0].rearrange("(k p) n -> p k n", p=P)[:, :, half * 512:(half + 1) * 512]
                elif name in ("wmk", "wmv", "wmq"):
                    dst = slot(name, KT, 512)
                    src = a["w_mem_" + name[2]][0].rearrange("(k p) n -> p k n", p=P)
                elif name == "wmo":
                    dst, src = slot(name, MH, D), a["w_mem_o"][0].rearrange("(k p) n -> p k n", p=P)
                sp.dma_start(dst, src).then_inc(sem(f"slot{u % RING}_loaded"), 16)

            freed = dict(q=("proj_ready", 9), k=("proj_ready", 9), v=("proj_ready", 9), z=("proj_ready", 9),
                         xbc0=("xbc_ready", 4), xbc1=("xbc_ready", 8), h0=("states_stored", 16),
                         scratch=("y_carried_ready", 2), wout0=("mixed_ready", 5), wout1=("mixed_ready", 5),
                         wmk=("mkv_ready", 2), wmv=("mkv_ready", 4), wmq=("mq_ready", 3), mem0=("att_rows_ready", 3),
                         mem1=("att_rows_ready", 3), mem2=("att_rows_ready", 4), mem3=("att_rows_ready", 4), wmo=("mixed_ready", 10))
            for b in range(NB):
                freed[f"K{b}"] = ("kt_turned", 5 * b + 5)
                freed[f"V{b}"] = ("att_rows_ready", b // 4 + 1)

            def wait_freed(u):
                name = UNITS[u - RING]
                sp.wait_ge(sem(freed[name][0]), freed[name][1])

            for u, name in enumerate(UNITS):
                if name in ("scratch", "pad"):
                    continue
                if u >= RING:
                    wait_freed(u)
                if name.startswith("mem"):
                    i = int(name[3:])
                    M = slot(name, 2, 4, MH * MD)
                    for j, kv in enumerate("kv"):
                        src = a["cache_mem_" + kv][0, 2 * i:2 * i + 2].rearrange("b (t p) h d -> p (b t) (h d)", p=P)
                        sp.dma_start(M[:, j], src
                                     ).then_inc(sem(f"slot{u % RING}_loaded"), 16)
                else:
                    load(name)
                if u == 0:
                    sp.dma_start(CN[:, P + 1:], a["consts"][:, P + 1:]).then_inc(sem("params_loaded"), 16)
                    sp.dma_start(RP[:, :], a["row_params"].to_broadcast([P, NR])).then_inc(sem("params_loaded"), 16)
                if u == 3:
                    sp.dma_start(WDT[:, :, :], w_in[:, :, 2048:2056]).then_inc(sem("dt_weights_loaded"), 16)
                if u == 12:
                    sp.dma_start(WR[:, :, :], a["w_router"][0].rearrange("(k p) n -> p k n", p=P)
                                 ).then_inc(sem("router_loaded"), 16)
            gu = a["w_gate_up"][0].rearrange("e (j t p) n -> e j p t n", p=P, t=2)
            dn = a["w_down"][0].rearrange("e (j t p) n -> e j p t n", p=P, t=4)

            def load_expert(j, e, odd):
                src = gu[e, j] if j < 4 else dn[e, j - 4]
                dst = slot(j, 2, 2 * FF) if j < 4 else slot(j, 4, D)
                loaded = f"slot{j}_loaded"
                if j == 0 and odd:
                    dst, loaded = SPARE, "spare_loaded"
                if not isinstance(e, int):
                    src = (gu[bass.ds(e, 1), j] if j < 4 else dn[bass.ds(e, 1), j - 4]).rearrange("a p t n -> (a p) t n")
                sp.dma_start(dst, src).then_inc(sem(loaded), 16)

            base = len(UNITS) - RING
            for j in (0, 1, 2, 4, 5, 3):
                name = UNITS[base + j]
                if name == "pad":
                    name = UNITS[base + j - RING]
                if j == 3:
                    sp.wait_ge(sem("mo_ready"), 4)
                    load_expert(0, 1, 1)
                sp.wait_ge(sem(freed[name][0]), freed[name][1])
                load_expert(j, 0, 0)

            def unit_used(j, n):
                if j == 3:
                    sp.wait_ge(sem("gate_up_ready"), n)
                elif j == 5:
                    sp.wait_ge(sem("down_ready"), n)
                else:
                    sp.wait_ge(sem("expert_units_used"), (n - 1) * 4 + (j + 1 if j < 3 else 4))

            def next_expert(n, e, odd):
                unit_used(0, n - 1)
                load_expert(0, e, odd)
                for j in range(1, RING):
                    unit_used(j, n)
                    load_expert(j, e, odd)

            for j in range(1, RING):
                unit_used(j, 1)
                load_expert(j, 1, 1)
            with sp.Fori(1, NE // 2) as h:
                for odd in range(2):
                    next_expert(h * 2 + odd, h * 2 + odd, odd)
            sp.wait_ge(sem("npass_ready"), 1)
            npass = sp.value_load(npass_i[0:1, 0:1], min_val=1, max_val=NPASS_MAX)
            with sp.If(npass > 1):
                with sp.Fori(1, npass) as r:
                    with sp.Fori(0, NE // 2) as h:
                        for odd in range(2):
                            next_expert(r * NE + h * 2 + odd, h * 2 + odd, odd)
            for t in range(3):
                n = ROWS[t]
                dst = o["y_prompt"][0, t * P:(t + 1) * P] if t < 2 else o["y_sample"].rearrange("b t d -> (b t) d")
                sp.wait_ge(sem("scatter_added"), npass * (3 * (NE + 1)) + max(t - 1, 0))
                sp.dma_start(dst, X[0:n, t, :]).then_inc(sem("rows_stored"), 16)
            sp.wait_ge(sem("rows_stored"), 48)
            sp.wait_ge(sem("prompt_state_stored"), 16)
            sp.wait_ge(sem("window_stored"), 64)
            sp.wait_ge(sem("conv_stored"), 32)
            sp.wait_ge(sem("states_stored"), 16)
            sp.wait_ge(sem("mem_stored"), 32)


OUTS = [("y_prompt", (1, SEQ, D)), ("y_sample", (NB, NS, D)),
        ("win_k_prompt", (1, 1, SEQ, AH, DH)), ("win_v_prompt", (1, 1, SEQ, AH, DH)),
        ("win_k_sample", (1, NB, NS, AH, DH)), ("win_v_sample", (1, NB, NS, AH, DH)),
        ("conv_prompt", (1, 1, 3, D)), ("conv_sample", (1, NB, 3, D)),
        ("ssm_prompt", (1, 1, SH, DH, NST)), ("ssm_sample", (1, NB, SH, DH, NST)),
        ("mem_k_prompt", (1, 1, NM, MH, MD)), ("mem_v_prompt", (1, 1, NM, MH, MD))]
WHOLE = ["x_prompt", "x_sample", "cache_win_k", "cache_win_v", "state_conv", "state_ssm", "cache_mem_k",
         "cache_mem_v", "mem_prompt", "w_in", "w_out", "w_mem_q", "w_mem_k", "w_mem_v", "w_mem_o", "w_router",
         "w_gate_up", "b_gate_up", "w_down", "b_down"]


def lay_out(inputs):
    arrays = {n: np.ascontiguousarray(inputs[n]) for n in WHOLE}
    arrays["consts"] = packed_constants()[1]
    row = [np.asarray(inputs[n]).reshape(1, -1) for n, _ in ROWP]
    arrays["row_params"] = np.ascontiguousarray(np.concatenate(row, 1))

    def columns(x):
        return np.asarray(x).reshape(-1, P).T

    gains = np.concatenate([np.tile(np.asarray(inputs["q_gain"]).reshape(1, -1), (32, 1)),
                            np.tile(np.asarray(inputs["k_gain"]).reshape(1, -1), (96, 1))], 0)
    col = [columns(inputs[n]) for n in ("norm_mix", "norm_mem", "mem_in_gain", "ssm_out_gain", "conv_b")]
    arrays["col_params"] = np.ascontiguousarray(np.concatenate(col + [columns(inputs["conv_w"]), gains], 1))
    return arrays


def kernel(**inputs):
    import concourse.bacc as bacc
    from concourse.bass_utils import run_bass_kernel_spmd

    nc = bacc.Bacc("TRN2", target_bir_lowering=False, num_devices=1)
    arrays, a, o = {}, {}, {}
    for n, x in lay_out(inputs).items():
        arrays[f"in_{n}"] = x
        a[n] = nc.dram_tensor(f"in_{n}", x.shape, mybir.dt.from_np(x.dtype), kind="ExternalInput").ap()
    for n, shape in OUTS:
        o[n] = nc.dram_tensor(f"out_{n}", shape, F32, kind="ExternalOutput").ap()
    build(nc, a, o)
    r = run_bass_kernel_spmd(nc, [arrays], core_ids=[0])
    return tuple(r.results[0][f"out_{n}"] for n, _ in OUTS)
```
